# Optimizing a Trainium2 kernel written in Bass

```python
import functools
import jax, jax.numpy as jnp
from jax import lax
import numpy as np

D_MODEL = 1024
BATCH = 1
SEQ = 512
DEPTH = 1
DEC_BATCH = 8
DEC_SEQ = 4
PAST_LEN = 1024
PAGE_SIZE = 128

HEAD_DIM = 64
D_RWKV = D_MODEL // 2
D_SB = D_MODEL // 2
H_RWKV = D_RWKV // HEAD_DIM
H_SB = D_SB // HEAD_DIM
N_BRANCH = 2
DECAY_LORA = max(32, int(round(1.8 * D_MODEL ** 0.5 / 32)) * 32)
AAA_LORA = max(32, int(round(1.8 * D_MODEL ** 0.5 / 32)) * 32)
GATE_LORA = max(32, int(round(0.6 * D_MODEL ** 0.8 / 32)) * 32)
D_FF = ((8 * D_MODEL // 3 + 127) // 128) * 128
W_IN_COLS = 3 * D_RWKV + 3 * D_SB + N_BRANCH * D_MODEL
Q_BLOCK = 128
SB_SCALE = HEAD_DIM ** -0.5
SB_BIAS_INIT = -6.0
LN_EPS = 1e-5
LNX_EPS = 64e-5
DN_ALPHA = (2.0 * DEPTH) ** 0.25
DN_BETA = (8.0 * DEPTH) ** -0.25

kernel_name = "rwkv7_stickbreaking_parallel_deepnorm_macaron_step"

def layer_norm(x, g, b):
    xf = x.astype(jnp.float32)
    mu = jnp.mean(xf, -1, keepdims=True)
    var = jnp.mean(jnp.square(xf - mu), -1, keepdims=True)
    return ((xf - mu) * lax.rsqrt(var + LN_EPS) * g + b).astype(x.dtype)

def swiglu(x, w_in, w_out):
    gate, up = jnp.split(x @ w_in, 2, axis=-1)
    return (jax.nn.silu(gate) * up) @ w_out

def wkv7_scan(s0, r, w, k, a_vec, b_vec, v):
    def step(S, inp):
        r_t, w_t, k_t, a_t, b_t, v_t = inp
        sa = jnp.einsum('bhij,bhj->bhi', S, a_t)
        S = (S * w_t[:, :, None, :] + sa[..., :, None] * b_t[:, :, None, :]
             + v_t[..., :, None] * k_t[:, :, None, :])
        return S, jnp.einsum('bhij,bhj->bhi', S, r_t)
    xs = tuple(jnp.moveaxis(t, 1, 0) for t in (r, w, k, a_vec, b_vec, v))
    S, ys = lax.scan(step, s0.astype(jnp.float32), xs)
    return S, jnp.moveaxis(ys, 0, 1)

def rwkv7_branch(h, p_rkv, h_last, wkv0, w_rkv, mu_rkv, mu_wag, w0, w_w1, w_w2,
                 a0, a_w1, a_w2, g_w1, g_w2, k_k, k_a, r_k, lnx_g, lnx_b):
    B, T, _ = h.shape
    f32 = jnp.float32
    p_prev = jnp.concatenate([(h_last @ w_rkv)[:, None], p_rkv[:, :-1]], axis=1)
    r, k, v = jnp.split(p_rkv + (p_prev - p_rkv) * mu_rkv, 3, axis=-1)
    dx = jnp.concatenate([h_last[:, None], h[:, :-1]], axis=1) - h
    xw = h + dx * mu_wag[0]
    xa = h + dx * mu_wag[1]
    xg = h + dx * mu_wag[2]
    w_log = -jax.nn.softplus(-(w0 + jnp.tanh(xw @ w_w1) @ w_w2).astype(f32)) - 0.5
    decay = jnp.exp(-jnp.exp(w_log))
    a = jax.nn.sigmoid((a0 + (xa @ a_w1) @ a_w2).astype(f32))
    g = jax.nn.sigmoid(xg @ g_w1) @ g_w2
    heads = lambda t: t.astype(f32).reshape(B, T, H_RWKV, HEAD_DIM)
    kk = heads(k * k_k)
    kk = kk / jnp.maximum(jnp.sqrt(jnp.sum(kk * kk, -1, keepdims=True)), 1e-12)
    k_mod = k.astype(f32) * (1.0 + (a - 1.0) * k_a)
    rh, kh, vh, ah = heads(r), heads(k_mod), heads(v), heads(a)
    wkv, y = wkv7_scan(wkv0, rh, heads(decay), kh, -kk, kk * ah, vh)
    mu = jnp.mean(y, -1, keepdims=True)
    var = jnp.mean(jnp.square(y - mu), -1, keepdims=True)
    y = ((y - mu) * lax.rsqrt(var + LNX_EPS)).reshape(B, T, D_RWKV) * lnx_g + lnx_b
    bonus = jnp.sum(rh * kh * r_k, -1, keepdims=True) * vh
    o = (y + bonus.reshape(B, T, D_RWKV)) * g
    return o.astype(h.dtype), wkv.astype(wkv0.dtype)

def stick_breaking(q, k, v, bias, q_pos, k_pos):
    z = (jnp.einsum('bqhd,bshd->bhqs', q, k).astype(jnp.float32) * SB_SCALE
         + bias.astype(jnp.float32)[None, :, None, None])
    causal = k_pos[None, :] < q_pos[:, None]
    log_1mb = jnp.where(causal, jax.nn.log_sigmoid(-z), 0.0)
    excl = lax.cumsum(log_1mb, axis=3, reverse=True) - log_1mb
    A = jnp.where(causal, jnp.exp(jax.nn.log_sigmoid(z) + excl), 0.0)
    return jnp.einsum('bhqs,bshd->bqhd', A.astype(v.dtype), v)

def sb_prompt(q, k, v, bias):
    B, T, H, d = q.shape
    nb = T // Q_BLOCK
    qb = jnp.moveaxis(q.reshape(B, nb, Q_BLOCK, H, d), 1, 0)
    k_pos = jnp.arange(T)

    def one_block(args):
        i, q_blk = args
        return stick_breaking(q_blk, k, v, bias, i * Q_BLOCK + jnp.arange(Q_BLOCK), k_pos)

    ob = lax.map(one_block, (jnp.arange(nb), qb))
    return jnp.moveaxis(ob, 0, 1).reshape(B, T, H * d)

def sb_sample(ck, cv, page_table, q, k, v, bias):
    B, T, H, d = q.shape
    k_past = ck[page_table].reshape(B, -1, H, d)
    v_past = cv[page_table].reshape(B, -1, H, d)
    past = k_past.shape[1]
    k_all = jnp.concatenate([k_past, k], axis=1)
    v_all = jnp.concatenate([v_past, v], axis=1)
    o = stick_breaking(q, k_all, v_all, bias, past + jnp.arange(T), jnp.arange(past + T))
    return o.reshape(B, T, H * d)

def trunk_layer(x, h_last, wkv0, sb_fn, p):
    x = layer_norm(DN_ALPHA * x + 0.5 * swiglu(x, p['ffn1_w_in'], p['ffn1_w_out']), p['ln1_g'], p['ln1_b'])
    h = x
    B, T, _ = h.shape
    proj = h @ p['w_in']
    n_rkv = 3 * D_RWKV
    p_rkv = proj[..., :n_rkv]
    q, k, v = jnp.split(proj[..., n_rkv:n_rkv + 3 * D_SB], 3, axis=-1)
    gate_logits = proj[..., n_rkv + 3 * D_SB:]
    o_a, wkv = rwkv7_branch(h, p_rkv, h_last, wkv0, p['w_in'][:, :n_rkv], p['mu_rkv'], p['mu_wag'],
                            p['w0'], p['w_w1'], p['w_w2'], p['a0'], p['a_w1'], p['a_w2'],
                            p['g_w1'], p['g_w2'], p['k_k'], p['k_a'], p['r_k'], p['lnx_g'], p['lnx_b'])
    q, k, v = (t.reshape(B, T, H_SB, HEAD_DIM) for t in (q, k, v))
    o_b = sb_fn(q, k, v, p['sb_bias'])
    gates = jax.nn.sigmoid(gate_logits.astype(jnp.float32)).astype(h.dtype)
    merged = (gates[..., :D_MODEL] * (o_a @ p['w_branch'][:D_RWKV])
              + gates[..., D_MODEL:] * (o_b @ p['w_branch'][D_RWKV:]))
    x = layer_norm(DN_ALPHA * x + merged @ p['w_out'], p['ln2_g'], p['ln2_b'])
    x = layer_norm(DN_ALPHA * x + 0.5 * swiglu(x, p['ffn2_w_in'], p['ffn2_w_out']), p['ln3_g'], p['ln3_b'])
    return x, k, v, wkv, h[:, -1]

def setup_inputs(seed: int = 0) -> dict:
    key = jax.random.key(seed)
    ks = iter(jax.random.split(key, 48))
    f32 = jnp.float32
    L = DEPTH
    n_pages = PAST_LEN // PAGE_SIZE
    n_used = DEC_BATCH * n_pages
    n_phys = n_used + max(1, n_used // 4)

    def nrm(shape, scale):
        return jax.random.normal(next(ks), shape, f32) * scale

    def uni(shape, lo, hi):
        return jax.random.uniform(next(ks), shape, f32, lo, hi)

    page_table = jax.random.permutation(next(ks), n_phys)[:n_used].reshape(DEC_BATCH, n_pages).astype(jnp.int32)
    return {
        "x_prompt": nrm((BATCH, SEQ, D_MODEL), 1.0),
        "x_sample": nrm((DEC_BATCH, DEC_SEQ, D_MODEL), 1.0),
        "cache_k": nrm((L, n_phys, PAGE_SIZE, H_SB, HEAD_DIM), 1.0),
        "cache_v": nrm((L, n_phys, PAGE_SIZE, H_SB, HEAD_DIM), 1.0),
        "state_wkv": nrm((L, DEC_BATCH, H_RWKV, HEAD_DIM, HEAD_DIM), 0.5),
        "state_shift": nrm((L, DEC_BATCH, D_MODEL), 1.0),
        "page_table": page_table,
        "ln1_g": 1.0 + nrm((L, D_MODEL), 0.02),
        "ln1_b": nrm((L, D_MODEL), 0.02),
        "ffn1_w_in": nrm((L, D_MODEL, 2 * D_FF), D_MODEL ** -0.5),
        "ffn1_w_out": nrm((L, D_FF, D_MODEL), D_FF ** -0.5 * DN_BETA),
        "w_in": nrm((L, D_MODEL, W_IN_COLS), D_MODEL ** -0.5),
        "mu_rkv": uni((L, 3 * D_RWKV), 0.0, 1.0),
        "mu_wag": uni((L, 3, D_MODEL), 0.0, 1.0),
        "w0": uni((L, D_RWKV), -6.0, 0.0),
        "w_w1": nrm((L, D_MODEL, DECAY_LORA), D_MODEL ** -0.5),
        "w_w2": nrm((L, DECAY_LORA, D_RWKV), 0.1 * DECAY_LORA ** -0.5),
        "a0": nrm((L, D_RWKV), 0.1),
        "a_w1": nrm((L, D_MODEL, AAA_LORA), D_MODEL ** -0.5),
        "a_w2": nrm((L, AAA_LORA, D_RWKV), 0.1 * AAA_LORA ** -0.5),
        "g_w1": nrm((L, D_MODEL, GATE_LORA), D_MODEL ** -0.5),
        "g_w2": nrm((L, GATE_LORA, D_RWKV), GATE_LORA ** -0.5),
        "k_k": 0.85 + nrm((L, D_RWKV), 0.02),
        "k_a": 1.0 + nrm((L, D_RWKV), 0.02),
        "r_k": nrm((L, H_RWKV, HEAD_DIM), 0.1),
        "lnx_g": 1.0 + nrm((L, D_RWKV), 0.02),
        "lnx_b": nrm((L, D_RWKV), 0.02),
        "sb_bias": SB_BIAS_INIT + nrm((L, H_SB), 0.1),
        "w_branch": nrm((L, D_RWKV + D_SB, D_MODEL), D_RWKV ** -0.5),
        "w_out": nrm((L, D_MODEL, D_MODEL), D_MODEL ** -0.5 * DN_BETA),
        "ln2_g": 1.0 + nrm((L, D_MODEL), 0.02),
        "ln2_b": nrm((L, D_MODEL), 0.02),
        "ffn2_w_in": nrm((L, D_MODEL, 2 * D_FF), D_MODEL ** -0.5),
        "ffn2_w_out": nrm((L, D_FF, D_MODEL), D_FF ** -0.5 * DN_BETA),
        "ln3_g": 1.0 + nrm((L, D_MODEL), 0.02),
        "ln3_b": nrm((L, D_MODEL), 0.02),
    }

def reference(x_prompt, x_sample, cache_k, cache_v, state_wkv, state_shift, page_table,
              ln1_g, ln1_b, ffn1_w_in, ffn1_w_out, w_in, mu_rkv, mu_wag, w0, w_w1, w_w2,
              a0, a_w1, a_w2, g_w1, g_w2, k_k, k_a, r_k, lnx_g, lnx_b, sb_bias, w_branch, w_out,
              ln2_g, ln2_b, ffn2_w_in, ffn2_w_out, ln3_g, ln3_b):
    xp, xs = x_prompt, x_sample
    kp_l, vp_l, wp_l, hp_l, ks_l, vs_l, ws_l, hs_l = [], [], [], [], [], [], [], []
    for l in range(DEPTH):
        p = dict(ln1_g=ln1_g[l], ln1_b=ln1_b[l], ffn1_w_in=ffn1_w_in[l], ffn1_w_out=ffn1_w_out[l],
                 w_in=w_in[l], mu_rkv=mu_rkv[l], mu_wag=mu_wag[l], w0=w0[l], w_w1=w_w1[l], w_w2=w_w2[l],
                 a0=a0[l], a_w1=a_w1[l], a_w2=a_w2[l], g_w1=g_w1[l], g_w2=g_w2[l], k_k=k_k[l], k_a=k_a[l],
                 r_k=r_k[l], lnx_g=lnx_g[l], lnx_b=lnx_b[l], sb_bias=sb_bias[l], w_branch=w_branch[l],
                 w_out=w_out[l], ln2_g=ln2_g[l], ln2_b=ln2_b[l], ffn2_w_in=ffn2_w_in[l],
                 ffn2_w_out=ffn2_w_out[l], ln3_g=ln3_g[l], ln3_b=ln3_b[l])
        wkv0_p = jnp.zeros((xp.shape[0], H_RWKV, HEAD_DIM, HEAD_DIM), state_wkv.dtype)
        xp, kp, vp, wp, hp = trunk_layer(xp, jnp.zeros_like(xp[:, 0]), wkv0_p, sb_prompt, p)
        sb_fn = functools.partial(sb_sample, cache_k[l], cache_v[l], page_table)
        xs, ks_, vs_, ws_, hs_ = trunk_layer(xs, state_shift[l].astype(xs.dtype), state_wkv[l], sb_fn, p)
        kp_l.append(kp); vp_l.append(vp); wp_l.append(wp); hp_l.append(hp)
        ks_l.append(ks_); vs_l.append(vs_); ws_l.append(ws_); hs_l.append(hs_)
    return (xp, xs,
            jnp.stack(kp_l), jnp.stack(vp_l), jnp.stack(wp_l), jnp.stack(hp_l),
            jnp.stack(ks_l), jnp.stack(vs_l), jnp.stack(ws_l), jnp.stack(hs_l))


_drawn_inputs = setup_inputs


def setup_inputs(seed=0):
    import zlib

    import numpy as np

    out = dict(_drawn_inputs(seed))
    spreads = {}
    factors = {'cache_k': 3.42,
     'cache_v': 2.702,
     'w_w1': 8.0,
     'w_w2': 8.0,
     'k_k': 23.661,
     'lnx_g': 26.654,
     'lnx_b': 28.046,
     'sb_bias': 8.0,
     'ln2_g': 2.731,
     'ln2_b': 2.862,
     'ln3_g': 22.983,
     'ln3_b': 23.712,
     'r_k': 6.536}
    for name, (base, spread) in spreads.items():
        noise = np.random.default_rng([zlib.crc32(name.encode()), seed]).standard_normal(out[name].shape)
        drawn = base * np.exp(spread * noise) if base else spread * noise
        out[name] = __import__('jax').numpy.asarray(drawn.astype(out[name].dtype))
    for name, factor in factors.items():
        out[name] = (out[name] * factor).astype(out[name].dtype)
    return out
```

```python
from contextlib import ExitStack

import numpy as np

import concourse.bass as bass
from concourse import mybir
from concourse.alu_op_type import AluOpType as ALU

F32 = mybir.dt.float32
F32R = mybir.dt.float32r
I32 = mybir.dt.int32
ACT = mybir.ActivationFunctionType
AX = mybir.AxisListType

P = 128
D_MODEL = 1024
KT = D_MODEL // P
SEQ = 512
NB = 8
DS = 4
TS = NB * DS
T = SEQ + TS
TX = T + NB
HALF = T // 2
HALFX = TX // 2
D_FF = 2816
FT = D_FF // P
FH = FT // 2
HD = 64
NH = 8
HP = NH // 2
PAGE = 128
N_PAGES = 8
N_PHYS = 80
PAST = PAGE * N_PAGES
CH = 64
LEVELS = 6
NT = SEQ // P
ALPHA = 2.0 ** 0.25
LN_EPS = 1e-5
LNX_EPS = 64e-5
DECAY = -float(np.exp(-0.5))
SCALE = HD ** -0.5
GL = 80
UNIT = 2048
MASKED = -30000.0

VEC = {}
NVEC = 0
for _name, _n in (("ln1_g", 8), ("ln1_b", 8), ("ln2_g", 8), ("ln2_b", 8), ("ln3_g", 8), ("ln3_b", 8),
                  ("mu_w", 8), ("mu_a", 8), ("mu_g", 8), ("mu_rkv", 12), ("w0", 4), ("a0", 4),
                  ("k_k", 4), ("k_a", 4), ("r_k", 4), ("lnx_g", 4), ("lnx_b", 4), ("sb_bias", 8),
                  ("sb_bias_rows", 1)):
    VEC[_name] = NVEC
    NVEC += _n

CST = {}
NCST = 0
for _name, _n in (("pair", P), ("ident", P), ("ones", P), ("suffix", P), ("score", 2 * P),
                  ("score_s", 2 * P), ("level", LEVELS * P), ("keep", T), ("own", NB),
                  ("own_rows", 2 * NB), ("own_head", NH), ("pick", 16), ("self", DS), ("cap", DS)):
    CST[_name] = NCST
    NCST += _n


def constants():
    c = np.zeros((P, NCST), np.float32)
    row, col = np.arange(P)[:, None], np.arange(P)[None, :]

    def put(name, a):
        c[:, CST[name]:CST[name] + a.shape[1]] = a

    put("pair", row // HD == col // HD)
    put("ident", row == col)
    put("ones", np.ones((P, P)))
    put("suffix", row >= col)
    same = row // CH == col // CH
    put("score", np.concatenate([same & (row < col), same & (row <= col)], 1))
    same = row // DS == col // DS
    put("score_s", np.concatenate([same & (row < col), same & (row <= col)], 1))
    put("level", np.concatenate(
        [(row // (2 * n) == col // (2 * n)) & (row % (2 * n) < n) & (col % (2 * n) >= n)
         for n in (2 ** l for l in range(LEVELS))], 1))
    keep = np.ones((P, T))
    keep[:, :SEQ][:, ::CH] = 0
    keep[:, SEQ:][:, ::DS] = 0
    put("keep", keep)
    put("own", (row % TS) // DS == np.arange(NB)[None])
    put("own_rows", np.concatenate([row // TS + 4 * g == np.arange(NB)[None] for g in range(2)], 1))
    put("own_head", (row % TS) // DS == np.arange(NH)[None])
    put("pick", (row // TS == np.arange(16)[None] // DS) & (row % DS == np.arange(16)[None] % DS))
    seen = (DS - 1 - np.arange(DS)[None]) < row % DS
    put("self", seen)
    put("cap", np.where(seen, 3e38, MASKED))
    return c


def build(nc, io):
    ctx = ExitStack()
    with ctx:
        sems = {}

        def S(name):
            name = STEPS[name][0] if name in STEPS else name
            if name not in sems:
                sems[name] = ctx.enter_context(nc.semaphore(name))
            return sems[name]

        STEPS = {}

        def in_a_row(shared, steps, first=0):
            for name, times in steps:
                STEPS[name] = (shared, first, 1)
                first += times

        def in_turn(shared, *steps):
            for j, name in enumerate(steps):
                STEPS[name] = (shared, j + 1 - len(steps), len(steps))

        def step(name, n=1):
            shared, first, every = STEPS[name]
            return S(shared), first + every * n

        in_a_row("prep_products", (("lora_second", HP), ("k_summed", HP)))
        in_a_row("prep_scalar", (("lora_out", 3 * HP), ("k_squared", HP), ("k_norm", HP)))
        in_a_row("s_products", (("s_scored", 2), ("s_turned", 1), ("s_with_state", 1), ("s_carry", 2),
                                ("s_grown", 1), ("s_ak", 1), ("s_sa", 1), ("s_y", 1), ("s_update", 1),
                                ("s_y_turned", 1)))
        in_a_row("s_scalar", (("s_tok", 1), ("s_carry_made", 1), ("s_sa_made", 1)))
        in_a_row("s_pool", (("s_v_copied", 1), ("s_mask_made", 2)))
        in_a_row("s_vector", (("s_scaled", 4), ("s_masked", 2), ("s_inv", 3), ("s_rhs", 1), ("s_expanded", 4),
                              ("s_y_summed", 1), ("s_state", 2 * HP)))
        in_turn("heads_products", "y_mean", "rk_summed", "y_var")
        in_turn("heads_scalar", "y_squared", "y_std", "o_a_hi")
        in_turn("heads_vector", "rk_made", "y_centred", "bonus_made", "o_a_made")
        in_a_row("heads_vector", (("o_a_lo", HP),), 4 * HP)

        base0 = nc.sbuf_base + (-nc.sbuf_base) % 32
        arena_bytes = (nc.sbuf_usable_end - base0) // 32 * 32
        ctx.enter_context(nc.sbuf_tensor("arena", [P, arena_bytes // 4], F32))

        class Region:
            def __init__(self, start, size):
                self.start, self.at, self.end = start, start, start + size

            def tensor(self, name, shape, dtype=F32):
                size = 4 * int(np.prod(shape[1:]))
                assert self.at + size <= self.end, (name, self.at + size - self.end)
                t = nc.alloc_sbuf_tensor_at(name, shape, dtype, offset=self.at)
                self.at += (size + 31) // 32 * 32
                return t

        whole = Region(base0, arena_bytes)

        def region(size):
            r = Region(whole.at, size)
            whole.at += size
            assert whole.at <= whole.end
            return r

        keepers = region((4 * (NVEC + P + KT * NB) + 5 * 32 + 31) // 32 * 32 + 64)
        vecs = keepers.tensor("vecs", [P, NVEC])
        mean_w = keepers.tensor("mean_w", [P, P])
        eps = keepers.tensor("eps", [P, 2])
        before = keepers.tensor("before", [P, KT, NB])

        one_less = keepers.tensor("one_less", [P, HP])
        self4 = keepers.tensor("self4", [P, DS])

        split_at = whole.at
        split_r = region(2 * 4 * KT * TX)
        xh = split_r.tensor("xh", [P, KT, TX], F32R)
        xl = split_r.tensor("xl", [P, KT, TX], F32R)
        y_r = region(4 * KT * T)
        y = y_r.tensor("y", [P, KT, T])

        ring_at = whole.at
        ring_r = region(6 * 4 * UNIT)
        raw = [ring_r.tensor(f"raw{s}", [P, UNIT]) for s in range(2)]
        whi = [ring_r.tensor(f"whi{s}", [P, UNIT], F32R) for s in range(2)]
        wlo = [ring_r.tensor(f"wlo{s}", [P, UNIT], F32R) for s in range(2)]

        temp_at = whole.at
        temp_bytes = 4 * 4 * T
        temp_r = region(temp_bytes)
        sg = [temp_r.tensor(f"sg{s}", [P, T]) for s in range(2)]
        u = [temp_r.tensor(f"u{s}", [P, T]) for s in range(2)]
        temp_r.at = temp_at
        sq = [temp_r.tensor(f"sq{s}", [P, T]) for s in range(2)]
        rstd = temp_r.tensor("rstd", [P, T])
        std = temp_r.tensor("std", [P, T])

        big_at = whole.at
        big_bytes = 2 * 4 * FT * T + 128
        big_r = region(big_bytes)
        gh = big_r.tensor("gh", [P, FT, T], F32R)
        gl = big_r.tensor("gl", [P, FT, T], F32R)
        big_r.at = big_at
        proj = big_r.tensor("proj", [P, 36, TX])
        vt = big_r.tensor("vt", [P, NT + 1, 512])
        inner2 = big_r.tensor("inner2", [P, 512])
        inner2g = big_r.tensor("inner2g", [GL, 2, 512])
        big_r.at = big_at
        big_r.tensor("lora_skip", [P, 20, TX])
        lora = big_r.tensor("lora", [P, 6, TX])
        temp_r.at = temp_at
        temp_diff = temp_r.tensor("temp_diff", [P, 4, T])
        temp_r.at = temp_at
        lora_wa = temp_r.tensor("lora_wa", [P, T])
        lora_g = temp_r.tensor("lora_g", [GL, 2, T])
        free_at, free_end = whole.at, whole.end

        psum = ctx.enter_context(nc.psum_tensor("psum", [P, 8, 512], F32))

        def vec(name, i):
            return vecs[:, VEC[name] + i:VEC[name] + i + 1]

        class Stage:
            def __init__(self, name, n, cols, first):
                self.name, self.n, self.cols, self.m0 = name, n, cols, first // 2
                assert first % 2 == 0 and n % 2 == 0

        stages, at = {}, 0
        for name, n, cols in (("ffn1_in", FT, 2048), ("ffn1_out", 16, FH * P), ("rkv", 6, 2048),
                              ("mid", 6, None), ("qkg", 12, 2048), ("branch", 8, 1024),
                              ("out", 4, 2048), ("ffn2_in", FT, 2048), ("ffn2_out", 16, FH * P)):
            stages[name] = Stage(name, n, cols, at)
            at += n
        MID_COLS = [2 * 1024, 2 * 8 * GL, 2 * 8 * GL, 3 * 512, 3 * 512, 2 * 512]
        landed = [S(f"raw_landed{s}") for s in range(2)]
        hi_made = [S(f"hi_made{s}") for s in range(2)]
        lo_made = [S(f"lo_made{s}") for s in range(2)]
        used = [S(f"unit_used{s}") for s in range(2)]

        def load_unit(eng, s, m, src, cols):
            eng.wait_ge(hi_made[s], m + 1)
            eng.wait_ge(lo_made[s], m + 1)
            eng.dma_start(raw[s][:, 0:cols], src).then_inc(landed[s], 16)

        def make_hi(eng, s, m, cols, ready=None):
            if ready is None:
                eng.wait_ge(landed[s], (m + 1) * 16)
            else:
                eng.wait_ge(*ready)
            eng.wait_ge(used[s], m + 1)
            eng.activation(whi[s][:, 0:cols], raw[s][:, 0:cols], ACT.Copy).then_inc(hi_made[s], 1)

        def make_lo(eng, s, m, cols):
            eng.wait_ge(hi_made[s], m + 2)
            eng.tensor_tensor(wlo[s][:, 0:cols], raw[s][:, 0:cols], whi[s][:, 0:cols].bitcast(F32),
                              ALU.subtract).then_inc(lo_made[s], 1)

        def unit_ready(eng, s, m):
            eng.wait_ge(hi_made[s], m + 2)
            eng.wait_ge(lo_made[s], m + 2)

        def two_halves(bank, n=HALF):
            return psum[:, bank:bank + 2, 0:n]

        def halves(a):
            return a.rearrange("p (h n) -> p h n", h=2)

        def split_product(eng, bank, w_hi, w_lo, a_hi, a_lo, n, first, last, rows=P):
            mm = None
            for k, (w, a) in enumerate(((w_hi, a_hi), (w_hi, a_lo), (w_lo, a_hi))):
                for h in range(2):
                    mm = eng.matmul(psum[0:rows, bank + h, 0:n], w, a[:, h * n:(h + 1) * n],
                                    start=first and k == 0, stop=last and k == 2)
            return mm

        def sp_stage(eng, st, dram):
            with eng.Fori(0, st.n // 2) as i:
                for s in range(2):
                    load_unit(eng, s, i + st.m0, dram[bass.ds(i * 2 + s, 1)].rearrange("a p n -> (a p) n"),
                              st.cols)

        def pool_stage(eng, st):
            with eng.Fori(0, st.n // 2) as i:
                for s in range(2):
                    make_lo(eng, s, i + st.m0, st.cols)

        def pipelined(eng, st, work, next_cols, next_ready=None):
            def body(i, last):
                make_hi(eng, 1, i + st.m0, st.cols)
                work(i, 0)
                if last:
                    if next_cols:
                        make_hi(eng, 0, i + st.m0 + 1, next_cols, next_ready)
                else:
                    make_hi(eng, 0, i + (st.m0 + 1), st.cols)
                work(i, 1)
            with eng.Fori(0, st.n // 2 - 1) as i:
                body(i, False)
            body(st.n // 2 - 1, True)

        def pe_ffn_in(eng, st, r):
            with eng.Fori(0, FT // 2) as i:
                for s in range(2):
                    unit_ready(eng, s, i + st.m0)
                    eng.wait_ge(S(f"ffn_read{s}"), i + (r * (FT // 2) + 1))
                    w_hi = whi[s][:].rearrange("p (t k n) -> p t k n", t=2, k=KT)
                    w_lo = wlo[s][:].rearrange("p (t k n) -> p t k n", t=2, k=KT)
                    for t in range(2):
                        for k in range(KT):
                            mm = split_product(eng, 4 * s + 2 * t, w_hi[:, t, k], w_lo[:, t, k],
                                               xh[:, k, 0:T], xl[:, k, 0:T], HALF, k == 0, k == KT - 1)
                        mm.then_inc(S(f"gate_done{s}") if t == 0 else used[s], 1)

        def act_ffn_in(eng, st, r, next_cols):
            def work(i, s):
                eng.wait_ge(S(f"gate_done{s}"), i + (r * (FT // 2) + 1))
                eng.wait_ge(S(f"ffn_read{s}"), i + (r * (FT // 2) + 1))
                eng.activation(halves(sg[s][:]), two_halves(4 * s), ACT.Sigmoid)\
                   .then_inc(S(f"sigmoid_made{s}"), 1)
            pipelined(eng, st, work, next_cols)

        def dve_ffn_in(eng, st, r):
            with eng.Fori(0, FT // 2) as i:
                for s in range(2):
                    n = i + (r * (FT // 2) + 1)
                    f = bass.ds(i * 2 + s, 1)
                    eng.wait_ge(S(f"sigmoid_made{s}"), n)
                    eng.tensor_tensor(halves(sg[s][:]), two_halves(4 * s), halves(sg[s][:]), ALU.mult)\
                       .then_inc(S(f"silu_made{s}"), 1)
                    eng.wait_ge(used[s], i + (st.m0 + 2))
                    eng.wait_ge(S(f"silu_made{s}"), n)
                    eng.wait_ge(S(f"inner_split{s}"), n * 2 - 1)
                    eng.tensor_tensor(halves(u[s][:]), two_halves(4 * s + 2), halves(sg[s][:]), ALU.mult)\
                       .then_inc(S(f"ffn_read{s}"), 1)
                    eng.wait_ge(S(f"ffn_read{s}"), n + 1)
                    eng.tensor_copy(gh[:, f].rearrange("p a n -> p (a n)"), u[s][:])\
                       .then_inc(S(f"inner_split{s}"), 1)
                    eng.wait_ge(S(f"inner_split{s}"), n * 2)
                    eng.tensor_tensor(gl[:, f].rearrange("p a n -> p (a n)"), u[s][:],
                                      gh[:, f].rearrange("p a n -> p (a n)").bitcast(F32), ALU.subtract)\
                       .then_inc(S(f"inner_split{s}"), 1)

        def pe_ffn_out(eng, st, r):
            for s in range(2):
                eng.wait_ge(S(f"inner_split{s}"), (r + 1) * FT + 1)
            with eng.Fori(0, KT // 2) as i:
                for j in range(2):
                    eng.wait_ge(S("y_added"), i * 2 + (r * KT + j + 1))
                    for s in range(2):
                        unit_ready(eng, s, i * 2 + (st.m0 + j))
                        for k in range(FH):
                            f = s * FH + k
                            w = slice(k * P, (k + 1) * P)
                            mm = split_product(eng, 2 * j, whi[s][:, w], wlo[s][:, w], gh[:, f], gl[:, f],
                                               HALF, f == 0, f == FT - 1)
                        mm.then_inc(used[s], 1)

        def act_ffn_out(eng, st, next_cols):
            pipelined(eng, st, lambda i, s: None, next_cols)

        def dve_ffn_out(eng, st, r):
            with eng.Fori(0, KT // 2) as i:
                for j in range(2):
                    eng.wait_ge(used[1], i * 2 + (st.m0 + j + 2))
                    row = y[:, bass.ds(i * 2 + j, 1)].rearrange("p a (h n) -> p (a h) n", h=2)
                    eng.scalar_tensor_tensor(row, two_halves(2 * j), 0.5 / ALPHA, row, ALU.mult, ALU.add)\
                       .then_inc(S("y_added"), 1)

        def pe_norm(eng, n, summed):
            eng.wait_ge(*summed)
            for k in range(KT):
                for h in range(2):
                    mm = eng.matmul(psum[:, 4 + h, 0:HALF], mean_w[:], y[:, k, h * HALF:(h + 1) * HALF],
                                    start=k == 0, stop=k == KT - 1)
            mm.then_inc(S("mean_done"), 1)
            for k in range(KT):
                eng.wait_ge(S("squared"), n * KT + k + 1)
                for h in range(2):
                    mm = eng.matmul(psum[:, 6 + h, 0:HALF], mean_w[:], sq[k % 2][:, h * HALF:(h + 1) * HALF],
                                    start=k == 0, stop=k == KT - 1)
                mm.then_inc(S("square_summed"), 1)

        def act_norm(eng, n, gname, bname, split):
            for k in range(KT):
                eng.wait_ge(S("centred"), n * KT + k + 1)
                if n * KT + k >= 2:
                    eng.wait_ge(S("square_summed"), n * KT + k - 1)
                eng.activation(sq[k % 2][:], y[:, k], ACT.Square).then_inc(S("squared"), 1)
            eng.wait_ge(S("square_summed"), (n + 1) * KT)
            eng.activation(halves(std[:]), two_halves(6), ACT.Sqrt, bias=eps[:, 0:1]).then_inc(S("std_made"), 1)
            for k in range(KT):
                eng.wait_ge(S("scaled"), n * KT + k + 1)
                if split:
                    eng.activation(xh[:, k, 0:T], y[:, k], ACT.Identity, bias=vec(bname, k))\
                       .then_inc(S("norm_hi"), 1)
                    eng.wait_ge(S("norm_hi"), n * KT + k + 1)
                eng.activation(y[:, k], y[:, k], ACT.Identity, bias=vec(bname, k)).then_inc(S("normed"), 1)

        def dve_norm(eng, n, gname, split):
            eng.wait_ge(S("mean_done"), n + 1)
            for k in range(KT):
                eng.tensor_tensor(halves(y[:, k]), halves(y[:, k]), two_halves(4), ALU.subtract)\
                   .then_inc(S("centred"), 1)
            eng.wait_ge(S("std_made"), n + 1)
            eng.reciprocal(rstd[:], std[:]).then_inc(S("rstd_made"), 1)
            eng.wait_ge(S("rstd_made"), n + 1)
            eng.wait_ge(S("centred"), (n + 1) * KT)
            for k in range(KT):
                eng.scalar_tensor_tensor(y[:, k], y[:, k], vec(gname, k), rstd[:], ALU.mult, ALU.mult)\
                   .then_inc(S("scaled"), 1)
            if split:
                for k in range(KT):
                    eng.wait_ge(S("normed"), n * KT + k + 1)
                    eng.tensor_tensor(xl[:, k, 0:T], y[:, k], xh[:, k, 0:T].bitcast(F32), ALU.subtract)\
                       .then_inc(S("norm_lo"), 1)
        a_r = Region(split_at, split_r.end - split_r.start)
        ldec = a_r.tensor("ldec", [P, HP, T])
        logp = a_r.tensor("logp", [P, HP, T])
        a_b = a_r.tensor("a_b", [P, HP, T])
        g_out = a_r.tensor("g_out", [P, HP, T])
        z_r = Region(ring_at, temp_at + temp_bytes - ring_at)
        z2_r = Region(y_r.start, y_r.end - y_r.start)
        cst = z_r.tensor("cst", [P, NCST])
        kk = z_r.tensor("kk", [P, HP, T])
        prep_at = z_r.at
        scores = z_r.tensor("scores", [P, NH, 4, P])
        dm = [z_r.tensor(f"inv{g}", [P, 4, P]) for g in range(2)]
        dt = [z_r.tensor(f"inv_t{g}", [P, 4, P]) for g in range(2)]
        wm = [z_r.tensor(f"carry{g}", [P, 4, P]) for g in range(2)]
        tmp_s = z_r.tensor("tmp_s", [P, HP, P])
        e_in = z_r.tensor("e_in", [P, HP, P])
        ar = z2_r.tensor("ar", [P, HP, 2, P])
        bk = z2_r.tensor("bk", [P, 2, HP, P])
        state = z2_r.tensor("state", [P, HP, P])
        end_w = z2_r.tensor("end_w", [P, HP, P])
        tok = z_r.tensor("tok", [P, 3, 512])
        e_ex = z2_r.tensor("e_ex", [P, HP, P])
        e_inv = Region(free_at, free_end - free_at).tensor("e_inv", [P, HP, P])
        em = [e_ex, e_inv]
        xs, sas = dm[0], dm[1]
        vf = tmp_s
        t_r = Region(prep_at, z_r.end - prep_at)
        t1 = t_r.tensor("t1", [P, HP, T])
        t2 = t_r.tensor("t2", [P, HP, T])
        t3 = t_r.tensor("t3", [P, HP, T])
        t4 = t_r.tensor("t4", [P, HP, T])
        s_r = Region(prep_at + 4 * 2 * 4 * P, 4 * 6 * 4 * P)
        state_s = s_r.tensor("state_s", [P, HP, NB, HD])
        own_x = s_r.tensor("own_x", [P, 2, NB, HD])
        q_r = Region(a_r.start, 2 * 4 * HP * T)
        own_v = q_r.tensor("own_v", [P, 2, NB, HD])
        x_red = q_r.tensor("x_red", [P, 2, 2, HD])
        e_in_s = q_r.tensor("e_in_s", [P, HP, TS])
        p_r = Region(big_at, 12 * TX * 4)
        zs = [p_r.tensor(f"zs{s}", [P, 10 * P]) for s in range(2)]
        ls = [p_r.tensor(f"ls{s}", [P, 10 * P]) for s in range(2)]
        k_r = Region(kk_end := z_r.start + (4 * NCST + 31) // 32 * 32, z_r.end - z_r.start - (4 * NCST + 31) // 32 * 32)
        pages = [k_r.tensor(f"pages{s}", [P, 4, 512]) for s in range(4)]
        qb = k_r.tensor("qb", [P, HP, NB, NH, DS])
        zsum = k_r.tensor("zsum", [P, 512])
        own_self = k_r.tensor("own_self", [P, 2, NB, DS])
        a_self_t = k_r.tensor("a_self_t", [TS, 2, P])
        n_r = Region(y_r.start, y_r.end - y_r.start)
        a_t = n_r.tensor("a_t", [P, 2, N_PAGES, P])
        zp = n_r.tensor("zp", [P, 2, PAST + DS])
        m_r = Region(big_at, 12 * TX * 4)
        lp = m_r.tensor("lp", [P, 2, PAST + DS])
        cp = m_r.tensor("cp", [P, 2, PAST + DS])
        o_f = m_r.tensor("o_f", [P, HP, 2 * 16])

        def cc(name, n=P):
            return cst[:, CST[name]:CST[name] + n]

        def bcast(a, n):
            return a.unsqueeze(1).broadcast_to([a.shape[0], n, a.shape[1]])

        def each(a, n):
            return a.unsqueeze(2).broadcast_to([a.shape[0], a.shape[1], n])

        def samples(a):
            return a.rearrange("p (b t) -> p b t", t=DS)

        class Count:
            def __init__(self, name):
                self.name, self.n = name, 0

            def up(self, ins):
                self.n += 1
                ins.then_inc(S(self.name), 1)
                return self.n

            def wait(self, eng, n=None):
                eng.wait_ge(S(self.name), self.n if n is None else n)

        dve_steps = Count("dve_steps")

        def pe_pairs(eng, st, made):
            with eng.Fori(0, st.n // 2) as i:
                for s in range(2):
                    unit_ready(eng, s, i + st.m0)
                    eng.wait_ge(S(f"{made}{s}"), i + 1)
                    w_hi = whi[s][:].rearrange("p (t k n) -> p t k n", t=2, k=KT)
                    w_lo = wlo[s][:].rearrange("p (t k n) -> p t k n", t=2, k=KT)
                    for t in range(2):
                        for k in range(KT):
                            mm = split_product(eng, 4 * s + 2 * t, w_hi[:, t, k], w_lo[:, t, k],
                                               xh[:, k], xl[:, k], HALFX, k == 0, k == KT - 1)
                    mm.then_inc(used[s], 1)

        def unit_banks(s, n=HALFX, rows=P):
            return psum[0:rows, 4 * s:4 * s + 4, 0:n]

        def act_pairs(eng, st, made, tile0, func_of, next_cols, next_ready=None):
            def work(i, s):
                eng.wait_ge(used[s], i + (st.m0 + 2))
                first = i * 4 + (tile0 + 2 * s)
                tiles = bass.ds(first, 2) if not isinstance(first, int) else slice(first, first + 2)
                dst = proj[:, tiles].rearrange("p t (h n) -> p (t h) n", h=2)
                eng.activation(dst, unit_banks(s), func_of).then_inc(S(f"{made}{s}"), 1)
            pipelined(eng, st, work, next_cols, next_ready)

        def mid_unit(q):
            return q % 2, stages["mid"].m0 + q // 2

        def pe_mid(eng):
            for q in range(3):
                s, m = mid_unit(q)
                n = P if q == 0 else GL
                unit_ready(eng, s, m)
                eng.wait_ge(S(f"rkv_made{s}"), 3 + 1)
                if q == 2:
                    eng.wait_ge(S("lora_copied"), 1)
                for t in range(2):
                    for k in range(KT):
                        w = slice((t * KT + k) * n, (t * KT + k + 1) * n)
                        mm = split_product(eng, 4 * s + 2 * t, whi[s][:, w], wlo[s][:, w], xh[:, k], xl[:, k],
                                           HALFX, k == 0, k == KT - 1, rows=n)
                mm.then_inc(used[s], 1)
            eng.wait_ge(S("lora_copied"), 3)
            for q in range(3, 6):
                s, m = mid_unit(q)
                unit_ready(eng, s, m)
                for j in range(3 if q < 5 else 2):
                    k = 3 * (q - 3) + j
                    w = slice(j * 512, (j + 1) * 512)
                    for tt in range(NT + 1):
                        rows = P if tt < NT else TS
                        c = slice(tt * P, tt * P + rows)
                        for n, (a, b) in enumerate(((xh, whi), (xh, wlo), (xl, whi))):
                            mm = eng.matmul(psum[0:rows, tt, :], a[:, k, c], b[s][:, w],
                                            start=k == 0 and n == 0, stop=k == KT - 1 and n == 2)
                mm.then_inc(used[s], 1)

        def act_mid(eng):
            st = stages["mid"]
            for q in range(3):
                s, m = mid_unit(q)
                ns, nm = mid_unit(q + 1)
                if q < 2:
                    make_hi(eng, ns, nm, MID_COLS[q + 1], (S("lora_weights"), q + 2))
                else:
                    make_hi(eng, ns, nm, MID_COLS[q + 1])
                rows = P if q == 0 else GL
                eng.wait_ge(used[s], m + 2)
                eng.activation(lora[0:rows, 2 * q:2 * q + 2].rearrange("p t (h n) -> p (t h) n", h=2),
                               unit_banks(s, rows=rows), ACT.Copy).then_inc(S("lora_copied"), 1)
            for q in range(4, 6):
                s, m = mid_unit(q)
                make_hi(eng, s, m, MID_COLS[q])
            eng.wait_ge(S("lora_summed"), 8)
            eng.activation(lora_wa[0:HD], lora_wa[0:HD], ACT.Tanh).then_inc(S("lora_inner"), 1)
            eng.wait_ge(S("lora_summed"), 24)
            eng.activation(lora_g[:], lora_g[:], ACT.Sigmoid).then_inc(S("lora_inner"), 1)
            make_hi(eng, 0, stages["qkg"].m0, stages["qkg"].cols)
            eng.wait_ge(used[1], st.m0 + 3 + 1)
            eng.activation(vt[:, 0:NT], psum[:, 0:NT, :], ACT.Copy).then_inc(S("v_made"), 1)
            eng.activation(vt[0:TS, NT], psum[0:TS, NT, :], ACT.Copy).then_inc(S("v_made"), 1)

        def dve_lora_weights(eng):
            c = dve_steps
            for q in range(3):
                s, m = mid_unit(q)
                n = P if q == 0 else GL
                eng.wait_ge(landed[s], (m + 1) * 16)
                w = raw[s][:, 0:KT * n].rearrange("p (k n) -> p k n", k=KT)
                mw = raw[s][:, KT * n:2 * KT * n].rearrange("p (k n) -> p k n", k=KT)
                parts = (("mu_w", 0, HD), ("mu_a", HD, HD)) if q == 0 else (("mu_g", 0, GL),)
                for name, at, width in parts:
                    mu = each(vecs[:, VEC[name]:VEC[name] + KT], width)
                    c.up(eng.tensor_tensor(mw[:, :, at:at + width], w[:, :, at:at + width], mu, ALU.mult))
                c.wait(eng)
                eng.tensor_tensor(w, w, mw, ALU.subtract).then_inc(S("lora_weights"), 1)

        def dve_shift(eng):
            c = dve_steps
            for grp in range(3):
                for s in range(2):
                    eng.wait_ge(S(f"rkv_made{s}"), grp + 2)
                p = proj[:, 4 * grp:4 * grp + 4]
                c.up(eng.tensor_tensor(temp_diff[:, :, 1:SEQ], p[:, :, 0:SEQ - 1], p[:, :, 1:SEQ], ALU.subtract))
                c.up(eng.tensor_scalar(temp_diff[:, :, 0:1], p[:, :, 0:1], -1.0, None, ALU.mult))
                for f in range(4):
                    ps, d = samples(p[:, f, SEQ:T]), samples(temp_diff[:, f, SEQ:T])
                    c.up(eng.tensor_tensor(d[:, :, 1:DS], ps[:, :, 0:DS - 1], ps[:, :, 1:DS], ALU.subtract))
                    c.up(eng.tensor_tensor(d[:, :, 0], p[:, f, T:TX], ps[:, :, 0], ALU.subtract))
                c.wait(eng)
                for f in range(4):
                    c.up(eng.scalar_tensor_tensor(p[:, f, 0:T], temp_diff[:, f], vec("mu_rkv", 4 * grp + f),
                                                  p[:, f, 0:T], ALU.mult, ALU.add))
                c.wait(eng)
            return c

        def dve_lora_sum(eng):
            for q in range(3):
                eng.wait_ge(S("lora_copied"), q + 1)
                rows = P if q == 0 else GL
                a, b = lora[0:rows, 2 * q], lora[0:rows, 2 * q + 1]
                o = lora_wa[:] if q == 0 else lora_g[:, q - 1]
                sa, so = samples(a[:, SEQ:T]), samples(o[:, SEQ:T])
                sb_ = samples(b[:, SEQ:T])
                for step in (eng.tensor_tensor(o[:, 1:SEQ], a[:, 1:SEQ], b[:, 0:SEQ - 1], ALU.add),
                             eng.tensor_copy(o[:, 0:1], a[:, 0:1]),
                             eng.tensor_tensor(so[:, :, 1:DS], sa[:, :, 1:DS], sb_[:, :, 0:DS - 1], ALU.add),
                             eng.tensor_tensor(so[:, :, 0], sa[:, :, 0], b[:, T:TX], ALU.add)):
                    step.then_inc(S("lora_summed"), 2)

        def wait_w_in(eng):
            for s in range(2):
                eng.wait_ge(used[s], stages["qkg"].m0 + 6 + 1)

        def pe_prep(eng):
            eng.wait_ge(S("qkg_made0"), 7)
            eng.wait_ge(S("qkg_made1"), 7)
            eng.wait_ge(S("lora_inner"), 2)
            eng.wait_ge(S("inner2_loaded"), 48)
            for f in range(HP):
                c = slice(f * P, (f + 1) * P)
                if f:
                    eng.wait_ge(*step("lora_out", 3 * f))
                for h in range(2):
                    n = slice(h * HALF, (h + 1) * HALF)
                    eng.matmul(psum[:, h, 0:HALF], inner2[0:HD, c], lora_wa[0:HD, n], start=True, stop=True)
                for h in range(2):
                    n = slice(h * HALF, (h + 1) * HALF)
                    eng.matmul(psum[:, 2 + h, 0:HALF], inner2[HD:P, c], lora_wa[HD:P, n], start=True, stop=True)
                for h in range(2):
                    n = slice(h * HALF, (h + 1) * HALF)
                    for q in range(2):
                        mm = eng.matmul(psum[:, 4 + h, 0:HALF], inner2g[:, q, c], lora_g[:, q, n],
                                        start=q == 0, stop=q == 1)
                mm.then_inc(S("lora_second"), 1)
            eng.wait_ge(S("cst_loaded"), 16)
            for f in range(HP):
                eng.wait_ge(*step("k_squared", f + 1))
                if f:
                    eng.wait_ge(*step("k_norm", f))
                for h in range(2):
                    mm = eng.matmul(psum[:, 6 + h, 0:HALF], cc("pair"), t1[:, f, h * HALF:(h + 1) * HALF],
                                    start=True, stop=True)
                mm.then_inc(S("k_summed"), 1)

        def act_prep(eng):
            wait_w_in(eng)
            for f in range(HP):
                eng.wait_ge(*step("lora_second", f + 1))
                eng.activation(halves(ldec[:, f]), two_halves(0), ACT.Sigmoid, bias=vec("w0", f)).then_inc(S("lora_out"), 1)
                eng.activation(halves(a_b[:, f]), two_halves(2), ACT.Sigmoid, bias=vec("a0", f)).then_inc(S("lora_out"), 1)
                eng.activation(halves(g_out[:, f]), two_halves(4), ACT.Copy).then_inc(S("lora_out"), 1)
            for f in range(HP):
                eng.wait_ge(S("k_scaled"), f + 1)
                eng.activation(t1[:, f], kk[:, f], ACT.Square).then_inc(S("k_squared"), 1)
            for f in range(HP):
                eng.wait_ge(*step("k_summed", f + 1))
                eng.activation(halves(t2[:, f]), two_halves(6), ACT.Sqrt).then_inc(S("k_norm"), 1)

        def dve_prep(eng):
            c = dve_steps
            wait_w_in(eng)
            for f in range(HP):
                eng.tensor_scalar(kk[:, f], proj[:, 4 + f, 0:T], vec("k_k", f), None, ALU.mult)\
                   .then_inc(S("k_scaled"), 1)
            c.up(eng.tensor_scalar(one_less[:], vecs[:, VEC["k_a"]:VEC["k_a"] + HP], -1.0, 1.0, ALU.mult, ALU.add))
            eng.wait_ge(S("cst_loaded"), 16)
            for f in range(HP):
                eng.wait_ge(*step("lora_out", 3 * f + 3))
                c.up(eng.tensor_scalar(ldec[:, f], ldec[:, f], DECAY, None, ALU.mult))
                c.wait(eng)
                c.up(eng.tensor_tensor_scan(logp[:, f], cc("keep", T), ldec[:, f], 0.0, ALU.mult, ALU.add))
                c.up(eng.tensor_scalar(t3[:, f], a_b[:, f], vec("k_a", f), one_less[:, f:f + 1], ALU.mult, ALU.add))
                c.wait(eng)
                c.up(eng.tensor_tensor(ldec[:, f], logp[:, f], ldec[:, f], ALU.subtract))
                c.up(eng.tensor_tensor(proj[:, 4 + f, 0:T], proj[:, 4 + f, 0:T], t3[:, f], ALU.mult))
            for f in range(HP):
                eng.wait_ge(*step("k_norm", f + 1))
                c.up(eng.tensor_scalar(t2[:, f], t2[:, f], 1e-12, None, ALU.max))
                c.wait(eng)
                c.up(eng.reciprocal(t4[:, f], t2[:, f]))
                c.wait(eng)
                c.up(eng.tensor_tensor(kk[:, f], kk[:, f], t4[:, f], ALU.mult))
                c.wait(eng)
                c.up(eng.tensor_tensor(a_b[:, f], kk[:, f], a_b[:, f], ALU.mult))
            c.wait(eng)
            eng.wait_ge(S("h_stored"), 16)
            eng.memset(state[:], 0.0).then_inc(S("prep_done"), 1)

        def c_rows(c):
            return slice(c * CH, (c + 1) * CH)

        def par_rows(h):
            return slice(h % 2 * HD, h % 2 * HD + HD)

        def act_wkv(eng):
            eng.wait_ge(S("prep_done"), 1)
            with eng.Fori(0, NT) as i:
                cols = bass.ds(i * P, P)
                eng.wait_ge(S("state_made"), i * 2 + 1)
                eng.activation(e_in[:], logp[:, :, cols], ACT.Exp).then_inc(S("decays"), 1)
                eng.activation(e_ex[:], ldec[:, :, cols], ACT.Exp).then_inc(S("decays"), 1)
                eng.activation(e_inv[:], logp[:, :, cols], ACT.Exp, scale=-1.0).then_inc(S("decays"), 1)
                eng.wait_ge(S("turned"), i * 3 + 3)
                for q in range(3):
                    eng.activation(tok[:, q], psum[:, 4 + q, :], ACT.Copy).then_inc(S("tok_made"), 1)
                for l in range(1, LEVELS):
                    for g in range(2):
                        eng.wait_ge(S(f"carry_done{g}"), i * LEVELS + (l + 1))
                        eng.activation(wm[g][:].rearrange("p h n -> p (h n)"), psum[:, 3 * g, :], ACT.Copy)\
                           .then_inc(S(f"carry_made{g}"), 1)
                for c in range(2):
                    eng.wait_ge(S("rhs_done"), i * 2 + (c + 1))
                    eng.activation(xs[c_rows(c)].rearrange("p h n -> p (h n)"), psum[c_rows(c), 6, :], ACT.Copy)\
                       .then_inc(S("rhs_made"), 1)
                    eng.wait_ge(S("sa_done"), i * 2 + (c + 1))
                    eng.activation(sas[c_rows(c)].rearrange("p h n -> p (h n)"), psum[c_rows(c), 7, :], ACT.Copy)\
                       .then_inc(S("sa_made"), 1)
                eng.wait_ge(S("y_done"), i + 1)
                eng.activation(kk[:, :, cols], psum[:, 0, :].rearrange("p (h n) -> p h n", h=HP), ACT.Copy)\
                   .then_inc(S("y_made"), 1)

        def pool_wkv(eng):
            eng.wait_ge(S("prep_done"), 1)
            eng.wait_ge(S("cst_loaded"), 16)
            with eng.Fori(0, NT) as i:
                cols = bass.ds(i * P, P)
                eng.wait_ge(S("state_made"), i * 2 + 1)
                eng.tensor_copy(vf[:], proj[:, 8:12, cols]).then_inc(S("v_copied"), 1)
                for l in range(LEVELS):
                    for g in range(2):
                        if l == 0:
                            eng.wait_ge(S("masked"), i * NH + (4 * g + 4))
                            eng.wait_ge(S("wkv_scaled"), i * 4 + 4)
                        else:
                            eng.wait_ge(S(f"carry_done{g}"), i * LEVELS + l)
                            if l == 1:
                                eng.wait_ge(S(f"inv_made{g}"), i * 11 + 2)
                        eng.tensor_tensor(em[g][:], scores[:, 4 * g:4 * g + 4, 0],
                                          bcast(cst[:, CST["level"] + l * P:CST["level"] + (l + 1) * P], 4),
                                          ALU.mult).then_inc(S(f"mask_made{g}"), 1)
                for c in range(2):
                    eng.wait_ge(S("state_made"), i * 2 + (c + 1))
                    if c == 0:
                        eng.wait_ge(S("decays"), i * 3 + 3)
                    eng.tensor_tensor(end_w[:], bcast(cc("pair"), HP), each(e_in[:, :, c * CH + CH - 1], P),
                                      ALU.mult).then_inc(S("end_made"), 1)

        def dve_wkv(eng):
            eng.wait_ge(S("prep_done"), 1)
            with eng.Fori(0, NT) as i:
                cols = bass.ds(i * P, P)
                eng.wait_ge(S("decays"), i * 3 + 3)
                eng.tensor_tensor(ar[:, :, 1], proj[:, 0:4, cols], e_in[:], ALU.mult).then_inc(S("wkv_scaled"), 1)
                eng.scalar_tensor_tensor(ar[:, :, 0], kk[:, :, cols], -1.0, e_ex[:], ALU.mult, ALU.mult)\
                   .then_inc(S("wkv_scaled"), 1)
                eng.tensor_tensor(bk[:, 0], a_b[:, :, cols], e_inv[:], ALU.mult).then_inc(S("wkv_scaled"), 1)
                eng.tensor_tensor(bk[:, 1], proj[:, 4:8, cols], e_inv[:], ALU.mult).then_inc(S("wkv_scaled"), 1)
                for h in range(NH):
                    eng.wait_ge(S("scored"), i * NH + (h + 1))
                    bank = h % 4
                    eng.tensor_tensor(scores[:, h].rearrange("p (x y) n -> p x (y n)", x=2),
                                      psum[:, bank, :].rearrange("p (x n) -> p x n", x=2),
                                      bcast(cc("score", 2 * P), 2), ALU.mult).then_inc(S("masked"), 1)
                ident = bcast(cc("ident"), 4)
                for g in range(2):
                    eng.wait_ge(S(f"mask_made{g}"), i * LEVELS + 1)
                    eng.tensor_tensor(dt[g][:], em[g][:], ident, ALU.add).then_inc(S(f"inv_made{g}"), 1)
                    eng.wait_ge(S(f"carry_done{g}"), i * LEVELS + 1)
                    eng.tensor_tensor(dm[g][:], psum[:, 3 * g, :].rearrange("p (h n) -> p h n", h=4), ident,
                                      ALU.add).then_inc(S(f"inv_made{g}"), 1)
                for l in range(1, LEVELS):
                    for g in range(2):
                        eng.wait_ge(S(f"grown{g}"), i * (LEVELS - 1) + l)
                        eng.wait_ge(S(f"inv_made{g}"), i * 11 + 2 * l)
                        if l < LEVELS - 1:
                            eng.tensor_tensor(dm[g][:], psum[:, 3 * g + 1, :].rearrange("p (h n) -> p h n", h=4),
                                              dm[g][:], ALU.add).then_inc(S(f"inv_made{g}"), 1)
                        eng.tensor_tensor(dt[g][:], psum[:, 3 * g + 2, :].rearrange("p (h n) -> p h n", h=4),
                                          dt[g][:], ALU.add).then_inc(S(f"inv_made{g}"), 1)
                for c in range(2):
                    eng.wait_ge(S("update_done"), i * 2 + (c + 1))
                    eng.tensor_tensor(tmp_s[:], psum[:, 1 + c, :].rearrange("p (h n) -> p h n", h=HP), state[:],
                                      ALU.add).then_inc(S("state_summed"), 1)
                    eng.wait_ge(S("state_summed"), i * 2 + (c + 1))
                    eng.wait_ge(S("end_made"), i * 2 + (c + 1))
                    eng.tensor_tensor(state[:], tmp_s[:], end_w[:], ALU.mult).then_inc(S("state_made"), 1)

        def pe_wkv(eng):
            eng.wait_ge(S("prep_done"), 1)
            with eng.Fori(0, NT) as i:
                eng.wait_ge(S("wkv_scaled"), i * 4 + 4)
                eng.wait_ge(S("y_made"), i + 1)
                eng.wait_ge(S("state_made"), i * 2 + 1)
                for h in range(NH):
                    bank = h % 4
                    if h >= 4:
                        eng.wait_ge(S("masked"), i * NH + (h - 3))
                    r = par_rows(h)
                    rhs = ar[r, h // 2].rearrange("p x n -> p (x n)")
                    eng.matmul(psum[:, bank, 0:256], bk[r, 0, h // 2], rhs, start=True, stop=True,
                               skip_group_check=True)
                    eng.matmul(psum[:, bank, 256:512], bk[r, 1, h // 2], rhs, start=False, stop=True,
                               skip_group_check=True).then_inc(S("scored"), 1)
                eng.wait_ge(S("v_copied"), i + 1)
                for q, a in enumerate((vf, bk[:, 0], bk[:, 1])):
                    for hp in range(HP):
                        mm = eng.transpose(psum[:, 4 + q, hp * P:(hp + 1) * P], a[:, hp], cc("ident"))
                    mm.then_inc(S("turned"), 1)
                for g in range(2):
                    eng.wait_ge(S(f"mask_made{g}"), i * LEVELS + 1)
                    eng.wait_ge(S("masked"), i * NH + NH)
                    for j in range(4):
                        mm = eng.matmul(psum[:, 3 * g, j * P:(j + 1) * P], em[g][:, j], cc("ident"),
                                        start=j == 0, stop=True, skip_group_check=True)
                    mm.then_inc(S(f"carry_done{g}"), 1)
                eng.wait_ge(S("tok_made"), i * 3 + 3)
                for l in range(1, LEVELS):
                    for g in range(2):
                        eng.wait_ge(S(f"mask_made{g}"), i * LEVELS + (l + 1))
                        eng.wait_ge(S(f"inv_made{g}"), i * 11 + 2 * l)
                        for j in range(4):
                            mm = eng.matmul(psum[:, 3 * g, j * P:(j + 1) * P], em[g][:, j], dm[g][:, j],
                                            start=j == 0, stop=True, skip_group_check=True)
                        mm.then_inc(S(f"carry_done{g}"), 1)
                    for g in range(2):
                        eng.wait_ge(S(f"carry_made{g}"), i * (LEVELS - 1) + l)
                        if l < LEVELS - 1:
                            for j in range(4):
                                eng.matmul(psum[:, 3 * g + 1, j * P:(j + 1) * P], dt[g][:, j], wm[g][:, j],
                                           start=j == 0, stop=True, skip_group_check=True)
                        for j in range(4):
                            mm = eng.matmul(psum[:, 3 * g + 2, j * P:(j + 1) * P], wm[g][:, j], dt[g][:, j],
                                            start=j == 0, stop=True, skip_group_check=True)
                        mm.then_inc(S(f"grown{g}"), 1)
                for g in range(2):
                    eng.wait_ge(S(f"inv_made{g}"), i * 11 + 11)
                for c in range(2):
                    cr = c_rows(c)
                    eng.wait_ge(S("state_made"), i * 2 + (c + 1))
                    for hp in range(HP):
                        eng.matmul(psum[cr, 6, hp * P:(hp + 1) * P], ar[:, hp, 0, cr], state[:, hp],
                                   start=hp == 0, stop=False, skip_group_check=True)
                    for h in range(NH):
                        n = slice(h * HD, (h + 1) * HD)
                        mm = eng.matmul(psum[cr, 6, n], scores[:, h, 2, cr], tok[:, 0, n],
                                        start=False, stop=True, skip_group_check=True)
                    mm.then_inc(S("rhs_done"), 1)
                    for hp in range(HP):
                        eng.matmul(psum[:, 0, hp * P + c * CH:hp * P + (c + 1) * CH], state[:, hp],
                                   ar[:, hp, 1, cr], start=c == 0 and hp == 0, stop=False, skip_group_check=True)
                    eng.wait_ge(S("rhs_made"), i * 2 + (c + 1))
                    for h in range(NH):
                        mm = eng.matmul(psum[cr, 7, h * HD:(h + 1) * HD], dt[h // 4][:, h % 4, cr],
                                        xs[:].rearrange("p h n -> p (h n)")[:, h * HD:(h + 1) * HD],
                                        start=h == 0, stop=True, skip_group_check=True)
                    mm.then_inc(S("sa_done"), 1)
                    eng.wait_ge(S("sa_made"), i * 2 + (c + 1))
                    for hp in range(HP):
                        n = slice(hp * P, (hp + 1) * P)
                        eng.matmul(psum[:, 1 + c, n], tok[cr, 1, n], sas[:].rearrange("p h n -> p (h n)")[cr, n],
                                   start=hp == 0, stop=False, skip_group_check=True)
                        mm = eng.matmul(psum[:, 1 + c, n], tok[cr, 2, n], tok[cr, 0, n],
                                        start=False, stop=True, skip_group_check=True)
                    mm.then_inc(S("update_done"), 1)
                for h in range(NH):
                    out = psum[par_rows(h), 0, h // 2 * P:(h // 2 + 1) * P]
                    n = slice(h * HD, (h + 1) * HD)
                    eng.matmul(out, sas[:].rearrange("p h n -> p (h n)")[:, n], scores[:, h, 1],
                               start=False, stop=False, skip_group_check=True)
                    mm = eng.matmul(out, tok[:, 0, n], scores[:, h, 3], start=False, stop=True,
                                    skip_group_check=True)
                mm.then_inc(S("y_done"), 1)
        arf = ar[:].rearrange("p a b n -> p (a b n)")
        bkf = bk[:].rearrange("p a b n -> p (a b n)")
        tokf = tok[:].rearrange("p a n -> p (a n)")
        xsf, sasf = (t[:].rearrange("p h n -> p (h n)") for t in (xs, sas))
        y_tok = wm[1][:].rearrange("p h n -> p (h n)")[:, 0:P]
        s_cols = slice(SEQ, T)
        last = 2 * NT + 1

        def act_wkv_s(eng):
            eng.wait_ge(S("state_made"), last)
            for dst, src, sc in ((e_in_s[:], logp, 1.0), (e_ex[:, :, 0:TS], ldec, 1.0), (e_inv[:, :, 0:TS], logp, -1.0)):
                eng.activation(dst, src[:, :, s_cols], ACT.Exp, scale=sc).then_inc(S("decays"), 1)
            eng.wait_ge(*step("s_turned", 1))
            eng.activation(tokf[:, 0:3 * P], psum[:, 4, 0:3 * P], ACT.Copy).then_inc(S("s_tok"), 1)
            eng.wait_ge(*step("s_carry", 2))
            eng.activation(wm[0][:, 0:2].rearrange("p h n -> p (h n)"), psum[:, 5, 0:2 * P], ACT.Copy)\
               .then_inc(S("s_carry_made"), 1)
            eng.wait_ge(*step("s_sa", 1))
            eng.activation(sasf[:, 0:P], psum[:, 1, 0:P], ACT.Copy).then_inc(S("s_sa_made"), 1)
            eng.wait_ge(*step("s_y_turned", 1))
            eng.activation(kk[:, :, s_cols], psum[:, 1, 2 * P:3 * P].rearrange("p (h n) -> p h n", h=HP), ACT.Copy)\
               .then_inc(S("y_made"), 1)

        def pool_wkv_s(eng):
            eng.wait_ge(S("state_made"), last)
            eng.tensor_copy(vf[:].rearrange("p h n -> p (h n)")[:, 0:P].rearrange("p (h n) -> p h n", h=HP),
                            proj[:, 8:12, s_cols]).then_inc(S("s_v_copied"), 1)
            eng.wait_ge(*step("s_masked", 2))
            eng.wait_ge(*step("s_scaled", 4))
            for l in range(2):
                if l:
                    eng.wait_ge(*step("s_carry", 1))
                    eng.wait_ge(*step("s_inv", 2))
                eng.tensor_tensor(em[0][:, 0:2], scores[:, 0:2, 0],
                                  bcast(cst[:, CST["level"] + l * P:CST["level"] + (l + 1) * P], 2),
                                  ALU.mult).then_inc(S("s_mask_made"), 1)

        def dve_wkv_s(eng):
            r4 = lambda a: a.rearrange("p (h n) -> p h n", h=HP)
            eng.wait_ge(S("decays"), 3 * NT + 3)
            eng.scalar_tensor_tensor(r4(arf[:, 0:P]), kk[:, :, s_cols], -1.0, e_ex[:, :, 0:TS], ALU.mult, ALU.mult)\
               .then_inc(S("s_scaled"), 1)
            eng.tensor_tensor(r4(arf[:, P:2 * P]), proj[:, 0:4, s_cols], e_in_s[:], ALU.mult).then_inc(S("s_scaled"), 1)
            eng.tensor_tensor(r4(bkf[:, 0:P]), a_b[:, :, s_cols], e_inv[:, :, 0:TS], ALU.mult).then_inc(S("s_scaled"), 1)
            eng.tensor_tensor(r4(bkf[:, P:2 * P]), proj[:, 4:8, s_cols], e_inv[:, :, 0:TS], ALU.mult)\
               .then_inc(S("s_scaled"), 1)
            for pr in range(2):
                eng.wait_ge(*step("s_scored", pr + 1))
                eng.tensor_tensor(scores[:, pr].rearrange("p (x y) n -> p x (y n)", x=2),
                                  psum[:, pr, :].rearrange("p (x n) -> p x n", x=2),
                                  bcast(cc("score_s", 2 * P), 2), ALU.mult).then_inc(S("s_masked"), 1)
            ident = bcast(cc("ident"), 2)
            two = lambda a: a.rearrange("p (h n) -> p h n", h=2)
            eng.wait_ge(*step("s_mask_made", 1))
            eng.tensor_tensor(dt[0][:, 0:2], em[0][:, 0:2], ident, ALU.add).then_inc(S("s_inv"), 1)
            eng.wait_ge(*step("s_carry", 1))
            eng.tensor_tensor(dm[0][:, 0:2], two(psum[:, 5, 0:2 * P]), ident, ALU.add).then_inc(S("s_inv"), 1)
            c = dve_steps
            eng.wait_ge(*step("s_with_state", 1))
            own = each(cc("own", NB), HD)
            for kind, bank in ((0, 2), (1, 6)):
                for pr in range(2):
                    c.up(eng.tensor_tensor(own_x[:, pr], psum[:, bank + pr, :].rearrange("p (b i) -> p b i", b=NB),
                                           own, ALU.mult))
                    c.wait(eng)
                    c.up(eng.tensor_reduce(x_red[:, kind, pr], own_x[:, pr].rearrange("p b i -> p i b"), AX.X, ALU.add))
                    c.wait(eng)
            eng.wait_ge(*step("s_grown", 1))
            eng.tensor_tensor(dt[0][:, 0:2], two(psum[:, 5, 2 * P:4 * P]), dt[0][:, 0:2], ALU.add).then_inc(S("s_inv"), 1)
            eng.wait_ge(*step("s_ak", 1))
            eng.tensor_tensor(xsf[:, 0:P], psum[:, 0, 0:P], x_red[:, 0].rearrange("p a n -> p (a n)"), ALU.add)\
               .then_inc(S("s_rhs"), 1)
            eng.wait_ge(*step("s_tok", 1))
            for pr in range(2):
                eng.tensor_tensor(own_v[:, pr], bcast(tokf[:, pr * HD:(pr + 1) * HD], NB), own, ALU.mult)\
                   .then_inc(S("s_expanded"), 1)
            eng.wait_ge(*step("s_sa_made", 1))
            for pr in range(2):
                eng.tensor_tensor(own_x[:, pr], bcast(sasf[:, pr * HD:(pr + 1) * HD], NB), own, ALU.mult)\
                   .then_inc(S("s_expanded"), 1)
            eng.wait_ge(*step("s_y", 1))
            eng.tensor_tensor(y_tok, psum[:, 0, P:2 * P], x_red[:, 1].rearrange("p a n -> p (a n)"), ALU.add)\
               .then_inc(S("s_y_summed"), 1)
            eng.wait_ge(*step("s_update", 1))
            for hp in range(HP):
                eng.tensor_tensor(state_s[:, hp].rearrange("p b i -> p (b i)"), psum[:, 4 + hp, :],
                                  state_s[:, hp].rearrange("p b i -> p (b i)"), ALU.add).then_inc(S("s_state"), 1)
            eng.wait_ge(*step("s_state", HP))
            for hp in range(HP):
                eng.tensor_tensor(state_s[:, hp], state_s[:, hp], each(samples(e_in_s[:, hp])[:, :, DS - 1], HD),
                                  ALU.mult).then_inc(S("s_state"), 1)

        def pe_wkv_s(eng):
            k = dict(skip_group_check=True)
            eng.wait_ge(*step("s_scaled", 4))
            eng.wait_ge(S("y_made"), NT + 1)
            for pr in range(2):
                r = par_rows(pr)
                eng.matmul(psum[:, pr, 0:256], bkf[r, 0:P], arf[r, 0:2 * P], start=True, stop=True, **k)
                eng.matmul(psum[:, pr, 256:512], bkf[r, P:2 * P], arf[r, 0:2 * P], start=False, stop=True, **k)\
                   .then_inc(S("s_scored"), 1)
            eng.wait_ge(*step("s_v_copied", 1))
            for q, a in enumerate((vf[:].rearrange("p h n -> p (h n)")[:, 0:P], bkf[:, 0:P], bkf[:, P:2 * P])):
                mm = eng.transpose(psum[:, 4, q * P:(q + 1) * P], a, cc("ident"))
            mm.then_inc(S("s_turned"), 1)
            eng.wait_ge(S("state_loaded"), 16)
            for at, bank in ((0, 2), (P, 6)):
                for pr in range(2):
                    r = par_rows(pr)
                    for hp in range(HP):
                        rows = slice(hp * TS, (hp + 1) * TS)
                        mm = eng.matmul(psum[rows, bank + pr, :], arf[r, at + hp * TS:at + (hp + 1) * TS],
                                        state_s[r, hp].rearrange("p b i -> p (b i)"), start=True, stop=True, **k)
            mm.then_inc(S("s_with_state"), 1)
            eng.wait_ge(*step("s_mask_made", 1))
            for pr in range(2):
                mm = eng.matmul(psum[:, 5, pr * P:(pr + 1) * P], em[0][:, pr], cc("ident"), start=pr == 0, stop=True, **k)
            mm.then_inc(S("s_carry"), 1)
            eng.wait_ge(*step("s_mask_made", 2))
            eng.wait_ge(*step("s_inv", 2))
            for pr in range(2):
                mm = eng.matmul(psum[:, 5, pr * P:(pr + 1) * P], em[0][:, pr], dm[0][:, pr], start=pr == 0, stop=True, **k)
            mm.then_inc(S("s_carry"), 1)
            eng.wait_ge(*step("s_carry_made", 1))
            for pr in range(2):
                mm = eng.matmul(psum[:, 5, (2 + pr) * P:(3 + pr) * P], wm[0][:, pr], dt[0][:, pr],
                                start=pr == 0, stop=True, **k)
            mm.then_inc(S("s_grown"), 1)
            eng.wait_ge(*step("s_tok", 1))
            eng.wait_ge(*step("s_masked", 2))
            for pr in range(2):
                n = slice(pr * HD, (pr + 1) * HD)
                mm = eng.matmul(psum[:, 0, n], scores[:, pr, 2], tokf[:, n], start=pr == 0, stop=True, **k)
            mm.then_inc(S("s_ak"), 1)
            eng.wait_ge(*step("s_rhs", 1))
            eng.wait_ge(*step("s_inv", 3))
            for pr in range(2):
                n = slice(pr * HD, (pr + 1) * HD)
                mm = eng.matmul(psum[:, 1, n], dt[0][:, pr], xsf[:, n], start=pr == 0, stop=True, **k)
            mm.then_inc(S("s_sa"), 1)
            eng.wait_ge(*step("s_sa_made", 1))
            for pr in range(2):
                n, o = slice(pr * HD, (pr + 1) * HD), slice(P + pr * HD, P + (pr + 1) * HD)
                eng.matmul(psum[:, 0, o], scores[:, pr, 1], sasf[:, n], start=pr == 0, stop=False, **k)
                mm = eng.matmul(psum[:, 0, o], scores[:, pr, 3], tokf[:, n], start=False, stop=True, **k)
            mm.then_inc(S("s_y"), 1)
            eng.wait_ge(*step("s_expanded", 4))
            for hp in range(HP):
                rows = slice(hp * TS, (hp + 1) * TS)
                for pr in range(2):
                    out = psum[par_rows(pr), 4 + hp, :]
                    b = slice(P + pr * HD, P + (pr + 1) * HD)
                    kc = slice(2 * P + pr * HD, 2 * P + (pr + 1) * HD)
                    eng.matmul(out, tokf[rows, b], own_x[rows, pr].rearrange("p b i -> p (b i)"),
                               start=True, stop=False, **k)
                    mm = eng.matmul(out, tokf[rows, kc], own_v[rows, pr].rearrange("p b i -> p (b i)"),
                                    start=False, stop=True, **k)
            mm.then_inc(S("s_update"), 1)
            eng.wait_ge(*step("s_y_summed", 1))
            eng.transpose(psum[:, 1, 2 * P:3 * P], y_tok, cc("ident")).then_inc(S("s_y_turned"), 1)

        def pe_heads(eng):
            eng.wait_ge(S("y_made"), NT + 2)
            eng.wait_ge(*step("s_state", 2 * HP))
            def pair(bank, a):
                for h in range(2):
                    mm = eng.matmul(psum[:, bank + h, 0:HALF], cc("pair"), a[:, h * HALF:(h + 1) * HALF],
                                    start=True, stop=True)
                return mm
            for f in range(HP):
                if f >= 2:
                    eng.wait_ge(*step("y_centred", f - 1))
                pair(2 * (f % 2), kk[:, f]).then_inc(S("y_mean"), 1)
                eng.wait_ge(*step("rk_made", f + 1))
                if f:
                    eng.wait_ge(*step("bonus_made", f))
                pair(6, t3[:, f]).then_inc(S("rk_summed"), 1)
                eng.wait_ge(*step("y_squared", f + 1))
                if f:
                    eng.wait_ge(*step("y_std", f))
                pair(4, t1[:, f]).then_inc(S("y_var"), 1)

        def act_heads(eng):
            for f in range(HP):
                eng.wait_ge(*step("y_centred", f + 1))
                eng.activation(t1[:, f], kk[:, f], ACT.Square).then_inc(S("y_squared"), 1)
                eng.wait_ge(*step("y_var", f + 1))
                eng.activation(halves(t2[:, f]), two_halves(4), ACT.Sqrt, bias=eps[:, 1:2], scale=1.0 / HD)\
                   .then_inc(S("y_std"), 1)
                eng.wait_ge(*step("o_a_made", f + 1))
                eng.activation(xh[:, f, 0:T], kk[:, f], ACT.Copy).then_inc(S("o_a_hi"), 1)

        def dve_heads(eng):
            c = dve_steps
            eng.wait_ge(S("states_stored"), 32)
            eng.wait_ge(S("y_made"), NT + 2)
            for f in range(HP):
                eng.scalar_tensor_tensor(t3[:, f], proj[:, f, 0:T], vec("r_k", f), proj[:, 4 + f, 0:T],
                                         ALU.mult, ALU.mult).then_inc(S("rk_made"), 1)
                eng.wait_ge(*step("y_mean", f + 1))
                eng.scalar_tensor_tensor(halves(kk[:, f]), two_halves(2 * (f % 2)), -1.0 / HD, halves(kk[:, f]),
                                         ALU.mult, ALU.add).then_inc(S("y_centred"), 1)
                eng.wait_ge(*step("rk_summed", f + 1))
                eng.tensor_tensor(halves(t3[:, f]), two_halves(6), halves(proj[:, 8 + f, 0:T]), ALU.mult)\
                   .then_inc(S("bonus_made"), 1)
                eng.wait_ge(*step("y_std", f + 1))
                c.up(eng.reciprocal(t4[:, f], t2[:, f]))
                c.wait(eng)
                eng.wait_ge(*step("y_centred", f + 1))
                eng.wait_ge(*step("y_squared", f + 1))
                c.up(eng.scalar_tensor_tensor(kk[:, f], kk[:, f], vec("lnx_g", f), t4[:, f], ALU.mult, ALU.mult))
                c.wait(eng)
                eng.wait_ge(*step("bonus_made", f + 1))
                c.up(eng.scalar_tensor_tensor(kk[:, f], kk[:, f], vec("lnx_b", f), t3[:, f], ALU.add, ALU.add))
                c.wait(eng)
                eng.tensor_tensor(kk[:, f], kk[:, f], g_out[:, f], ALU.mult).then_inc(S("o_a_made"), 1)
            for f in range(HP):
                eng.wait_ge(*step("o_a_hi", f + 1))
                eng.tensor_tensor(xl[:, f, 0:T], kk[:, f], xh[:, f, 0:T].bitcast(F32), ALU.subtract)\
                   .then_inc(S("o_a_lo"), 1)

        OFF = {0: 4 * P, 2: 7 * P, 1: 8 * P}
        flat = psum[:].rearrange("p b n -> p (b n)")
        C_AT = 3 * 512

        def pe_scores(eng, h):
            if h:
                eng.wait_ge(S("z_made"), h)
            r, hp = par_rows(h), h // 2
            q, key = proj[r, 12 + hp], proj[r, 16 + hp]
            for kt in range(NT):
                mm = eng.matmul(flat[:, kt * P:(kt + 1) * P], key[:, kt * P:(kt + 1) * P], q[:, kt * P:(kt + 1) * P],
                                start=kt == 0, stop=True, skip_group_check=True)
            for n, kt in enumerate((0, 2, 1)):
                w = SEQ - (kt + 1) * P
                mm = eng.matmul(flat[:, OFF[kt]:OFF[kt] + w], key[:, kt * P:(kt + 1) * P], q[:, (kt + 1) * P:SEQ],
                                start=kt != 2, stop=True, skip_group_check=True)
            mm.then_inc(S("z_done"), 1)

        def pe_sums(eng, h):
            l = ls[h % 2]
            eng.wait_ge(S("soft_masked"), h + 1)
            if h:
                eng.wait_ge(S("exponents"), h)
            def add(at, src, n, first=False):
                return eng.matmul(flat[:, C_AT + at:C_AT + at + n], cc("suffix") if first else cc("ones"),
                                  l[:, src:src + n], start=first, stop=not first, skip_group_check=True)
            add(0, 0, 512, True)
            add(4 * P, 4 * P, 512, True)
            add(8 * P, 8 * P, 256, True)
            add(4 * P, P, P)
            add(5 * P, 8 * P, 2 * P)
            add(5 * P, 2 * P, 2 * P)
            add(6 * P, 7 * P, P)
            add(7 * P, 3 * P, P)
            add(8 * P, 2 * P, 2 * P)
            add(9 * P, 7 * P, P).then_inc(S("sums_done"), 1)

        def pe_values(eng, h):
            a, hp = zs[h % 2], h // 2
            eng.wait_ge(S("weights_made"), h + 1)
            if h % 2 == 0 and hp >= 2:
                eng.wait_ge(S("o_b_lo"), hp - 1)
            out = psum[par_rows(h), 6 + hp % 2, :]
            v = lambda kt: vt[:, kt, h * HD:(h + 1) * HD]
            for kt in range(NT):
                eng.matmul(out[:, kt * P:(kt + 1) * P], v(kt), a[:, kt * P:(kt + 1) * P],
                           start=kt == 0, stop=False, skip_group_check=True)
            for kt in range(NT - 1):
                w = SEQ - (kt + 1) * P
                mm = eng.matmul(out[:, (kt + 1) * P:SEQ], v(kt), a[:, OFF[kt]:OFF[kt] + w],
                                start=False, stop=kt == NT - 2, skip_group_check=True)
            mm.then_inc(S("values_done"), 1)

        def pe_stick(eng):
            eng.wait_ge(*step("o_a_lo", HP))
            eng.wait_ge(S("v_made"), 2)
            pe_scores(eng, 0)
            for h in range(NH + 1):
                if h + 1 < NH:
                    pe_scores(eng, h + 1)
                if h < NH:
                    pe_sums(eng, h)
                if h:
                    pe_values(eng, h - 1)

        def act_stick(eng):
            def soft(h):
                l = ls[h % 2]
                eng.wait_ge(S("z_made"), h + 1)
                if h >= 2:
                    eng.wait_ge(S("sums_done"), h - 1)
                eng.activation(l[:], zs[h % 2][:], ACT.Abs).then_inc(S("soft"), 1)
                eng.wait_ge(S("soft"), 3 * h + 1)
                eng.activation(l[:], l[:], ACT.Exp, scale=-1.0).then_inc(S("soft"), 1)
                eng.wait_ge(S("soft"), 3 * h + 2)
                eng.activation(l[:], l[:], ACT.Ln, bias=1.0).then_inc(S("soft"), 1)

            def weights(h):
                eng.wait_ge(S("exponents_masked"), h + 1)
                eng.activation(zs[h % 2][:], zs[h % 2][:], ACT.Exp).then_inc(S("weights_made"), 1)

            def output(hp):
                eng.wait_ge(S("values_done"), 2 * hp + 2)
                eng.activation(xh[:, HP + hp, 0:SEQ], psum[:, 6 + hp % 2, :], ACT.Copy).then_inc(S("o_b_hi"), 1)

            soft(0)
            for h in range(NH):
                if h + 1 < NH:
                    soft(h + 1)
                weights(h)
                if h >= 2 and h % 2 == 0:
                    output(h // 2 - 1)
            output(HP - 1)

        def dve_stick(eng):
            def scaled(h):
                eng.wait_ge(S("z_done"), h + 1)
                if h >= 2:
                    eng.wait_ge(S("values_done"), h - 1)
                eng.tensor_scalar(zs[h % 2][:], flat[:, 0:10 * P], SCALE, vec("sb_bias", h), ALU.mult, ALU.add)\
                   .then_inc(S("z_made"), 1)

            def soft(h):
                eng.wait_ge(S("soft"), 3 * h + 3)
                eng.scalar_tensor_tensor(ls[h % 2][:], zs[h % 2][:], 0.0, ls[h % 2][:], ALU.max, ALU.add)\
                   .then_inc(S("soft_made"), 1)

            def exponents(h):
                eng.wait_ge(S("sums_done"), h + 1)
                eng.tensor_tensor(zs[h % 2][:], zs[h % 2][:], flat[:, C_AT:C_AT + 10 * P], ALU.subtract)\
                   .then_inc(S("exponents"), 1)

            def output(hp):
                eng.wait_ge(S("o_b_hi"), hp + 1)
                eng.tensor_tensor(xl[:, HP + hp, 0:SEQ], psum[:, 6 + hp % 2, :], xh[:, HP + hp, 0:SEQ].bitcast(F32),
                                  ALU.subtract).then_inc(S("o_b_lo"), 1)

            scaled(0)
            soft(0)
            for h in range(NH):
                if h + 1 < NH:
                    scaled(h + 1)
                exponents(h)
                if h + 1 < NH:
                    soft(h + 1)
                if h >= 3 and h % 2 == 1:
                    output(h // 2 - 1)
            output(HP - 1)

        def pool_stick(eng):
            def select(a, fill):
                b = a[:, 0:4 * P].rearrange("p (k n) -> p k n", k=4)
                return eng.affine_select(out=b, in_=b, compare_op=ALU.is_gt, fill=fill, base=0,
                                         pattern=[[0, 4], [1, P]], channel_multiplier=-1)
            def soft(h):
                eng.wait_ge(S("soft_made"), h + 1)
                select(ls[h % 2], 0.0).then_inc(S("soft_masked"), 1)
            soft(0)
            for h in range(NH):
                eng.wait_ge(S("exponents"), h + 1)
                select(zs[h % 2], MASKED).then_inc(S("exponents_masked"), 1)
                if h + 1 < NH:
                    soft(h + 1)

        def sp_pages(eng, io):
            eng.wait_ge(*step("o_a_lo", HP))
            for kind, src in ((0, io["cache_k"]), (1, io["cache_v"])):
                with eng.Fori(0, NB // 2) as i:
                    for j in range(4):
                        regs = [eng.value_load(io["page_table"][bass.ds(i * 2 + j // 2, 1),
                                                                N_PAGES - 1 - (j % 2 * 4 + p):N_PAGES - (j % 2 * 4 + p)],
                                               min_val=0, max_val=N_PHYS - 1) for p in range(4)]
                        for p in range(4):
                            dst = pages[j][:, :, p * P:(p + 1) * P] if kind == 0 else pages[j][:, p]
                            page = src[bass.ds(regs[p], 1)].rearrange("a p h n -> (a p) h n" if kind == 0
                                                                      else "a p n -> (a p) n")
                            if p == 0:
                                eng.wait_ge(S(f"pages_used{j}"), i + (kind * (NB // 2) + 1))
                            eng.dma_start(dst, page).then_inc(S(f"pages_loaded{j}"), 16)

        def pages_ready(eng, kind, b, half):
            j = 2 * (b % 2) + half
            eng.wait_ge(S(f"pages_loaded{j}"), 64 * (kind * NB // 2 + b // 2 + 1))
            return j

        def pe_samples(eng):
            k = dict(skip_group_check=True)
            eng.wait_ge(S("qb_made"), 9)
            eng.wait_ge(S("exponents"), NH)
            for b in range(NB):
                g, rows = b // 4, slice(b % 4 * 32, b % 4 * 32 + 32)
                for half in range(2):
                    j = pages_ready(eng, 0, b, half)
                    for hp in range(HP):
                        mm = eng.matmul(psum[rows, 3 * g + half, :], qb[:, hp, b].rearrange("p h t -> p (h t)"),
                                        pages[j][:, hp], start=hp == 0, stop=hp == HP - 1, **k)
                    mm.then_inc(S(f"pages_used{j}"), 1)
                if b % 4 == 3:
                    for hp in range(HP):
                        mm = eng.matmul(psum[:, 3 * g + 2, 0:TS],
                                        qb[:, hp, 4 * g:4 * g + 4].rearrange("p b h t -> p (b h t)"),
                                        proj[:, 16 + hp, s_cols], start=hp == 0, stop=hp == HP - 1, **k)
                    mm.then_inc(S("zp_done"), 1)
            eng.wait_ge(S("o_b_lo"), HP)
            for g in range(2):
                eng.wait_ge(S("wp_made"), g + 1)
                eng.wait_ge(S("self_spread"), 4 * (g + 1))
                for q in range(2):
                    if g:
                        eng.wait_ge(S("wp_turned"), q + 1)
                    for p in range(4):
                        mm = eng.transpose(psum[:, 6 + q, p * P:(p + 1) * P],
                                           zp[:, g, DS + (4 * q + p) * P:DS + (4 * q + p + 1) * P], cc("ident"))
                    mm.then_inc(S("wp_turn"), 1)
                eng.transpose(psum[0:TS, 2 + 3 * g, 0:P], own_self[:, g].rearrange("p b t -> p (b t)"), cc("ident"))\
                   .then_inc(S("self_turn"), 1)
            for g in range(2):
                eng.wait_ge(S("self_turned"), g + 1)
                eng.wait_ge(S("wp_turned"), 2 * g + 2)
                eng.matmul(psum[:, g, :], a_self_t[:, g], vt[0:TS, NT, :], start=True, stop=False, **k)
                for b4 in range(4):
                    b = 4 * g + b4
                    rows = slice(b4 * 32, b4 * 32 + 32)
                    for half in range(2):
                        j = pages_ready(eng, 1, b, half)
                        for p in range(4):
                            mm = eng.matmul(psum[rows, g, :], a_t[:, g, 4 * half + p, rows], pages[j][:, p],
                                            start=False, stop=True, **k)
                        mm.then_inc(S(f"pages_used{j}"), 1)
                eng.wait_ge(S("zsum_made"), g + 1)
                for hp in range(HP):
                    mm = eng.matmul(psum[:, 3 + g, hp * 16:(hp + 1) * 16], zsum[:, hp * P:(hp + 1) * P], cc("pick", 16),
                                    start=hp == 0, stop=True, **k)
                mm.then_inc(S("o_s_done"), 1)

        def act_samples(eng):
            for g in range(2):
                eng.wait_ge(S("zp_made"), 5 * (g + 1))
                eng.activation(lp[:, g], zp[:, g], ACT.Abs).then_inc(S("soft_p"), 1)
                eng.wait_ge(S("soft_p"), 3 * g + 1)
                eng.activation(lp[:, g], lp[:, g], ACT.Exp, scale=-1.0).then_inc(S("soft_p"), 1)
                eng.wait_ge(S("soft_p"), 3 * g + 2)
                eng.activation(lp[:, g], lp[:, g], ACT.Ln, bias=1.0).then_inc(S("soft_p"), 1)
            for g in range(2):
                eng.wait_ge(S("exponents_p"), g + 1)
                eng.activation(zp[:, g], zp[:, g], ACT.Exp).then_inc(S("wp_made"), 1)
            for g in range(2):
                for q in range(2):
                    eng.wait_ge(S("wp_turn"), 2 * g + q + 1)
                    eng.activation(a_t[:, g, 4 * q:4 * q + 4].rearrange("p a n -> p (a n)"), psum[:, 6 + q, :], ACT.Copy)\
                       .then_inc(S("wp_turned"), 1)
                eng.wait_ge(S("self_turn"), g + 1)
                eng.activation(a_self_t[:, g], psum[0:TS, 2 + 3 * g, 0:P], ACT.Copy).then_inc(S("self_turned"), 1)
            for g in range(2):
                eng.wait_ge(S("o_s_done"), g + 1)
                eng.activation(xh[:, HP:2 * HP, SEQ + 16 * g:SEQ + 16 * g + 16],
                               psum[:, 3 + g, 0:64].rearrange("p (h n) -> p h n", h=HP), ACT.Copy)\
                   .then_inc(S("o_s_hi"), 1)

        def dve_qb(eng):
            eng.wait_ge(*step("o_a_lo", HP))
            eng.memset(qb[:], 0.0).then_inc(S("qb_made"), 1)
            eng.wait_ge(S("qb_made"), 1)
            for h in range(NH):
                r = par_rows(h)
                eng.tensor_copy(qb[r, h // 2, :, h], samples(proj[r, 12 + h // 2, s_cols])).then_inc(S("qb_made"), 1)

        def dve_samples(eng):
            c = dve_steps
            own = lambda g: cst[:, CST["own_rows"] + g * NB:CST["own_rows"] + (g + 1) * NB]
            eng.wait_ge(S("values_done"), NH)
            bias = vec("sb_bias_rows", 0)
            for g in range(2):
                eng.wait_ge(S("zp_done"), g + 1)
                zf = psum[:, 3 * g:3 * g + 2, :].rearrange("p b n -> p (b n)")
                eng.tensor_scalar(zp[:, g, DS:], zf, SCALE, bias, ALU.mult, ALU.add).then_inc(S("zp_made"), 1)
                c.up(eng.tensor_tensor(own_self[:, g], psum[:, 3 * g + 2, 0:TS].rearrange("p (b t) -> p b t", t=DS),
                                       each(own(g), DS), ALU.mult))
                c.wait(eng)
                c.up(eng.tensor_reduce(self4[:], own_self[:, g].rearrange("p b t -> p t b"), AX.X, ALU.add))
                c.wait(eng)
                for t in range(DS):
                    eng.tensor_scalar(zp[:, g, DS - 1 - t:DS - t], self4[:, t:t + 1], SCALE, bias, ALU.mult, ALU.add)\
                       .then_inc(S("zp_made"), 1)
            for g in range(2):
                eng.wait_ge(S("soft_p"), 3 * g + 3)
                c.up(eng.scalar_tensor_tensor(lp[:, g], zp[:, g], 0.0, lp[:, g], ALU.max, ALU.add))
                c.wait(eng)
                c.up(eng.tensor_tensor(lp[:, g, 0:DS], lp[:, g, 0:DS], cc("self", DS), ALU.mult))
                c.wait(eng)
                c.up(eng.tensor_tensor_scan(cp[:, g], cst[:, CST["ones"]:CST["ones"] + 1].broadcast_to([P, PAST + DS]),
                                            lp[:, g], 0.0, ALU.mult, ALU.add))
                c.wait(eng)
                c.up(eng.tensor_tensor(zp[:, g], zp[:, g], cp[:, g], ALU.subtract))
                c.wait(eng)
                eng.tensor_tensor(zp[:, g, 0:DS], zp[:, g, 0:DS], cc("cap", DS), ALU.min).then_inc(S("exponents_p"), 1)
            for g in range(2):
                eng.wait_ge(S("wp_made"), g + 1)
                for t in range(DS):
                    eng.tensor_scalar(own_self[:, g, :, t], own(g), zp[:, g, DS - 1 - t:DS - t], None, ALU.mult)\
                       .then_inc(S("self_spread"), 1)
            for g in range(2):
                for half in range(2):
                    eng.wait_ge(S(f"pages_used{2 + half}"), 1 + NB // 2 + 2 * g + 2)
                if g:
                    eng.wait_ge(S("o_s_done"), 1)
                eng.tensor_tensor(zsum[:].rearrange("p (h n) -> p h n", h=NH),
                                  psum[:, g, :].rearrange("p (h n) -> p h n", h=NH), each(cc("own_head", NH), HD),
                                  ALU.mult).then_inc(S("zsum_made"), 1)
            for g in range(2):
                eng.wait_ge(S("o_s_hi"), g + 1)
                cols = slice(SEQ + 16 * g, SEQ + 16 * g + 16)
                eng.tensor_tensor(xl[:, HP:2 * HP, cols], psum[:, 3 + g, 0:64].rearrange("p (h n) -> p h n", h=HP),
                                  xh[:, HP:2 * HP, cols].bitcast(F32), ALU.subtract).then_inc(S("o_s_lo"), 1)

        b_r = Region(big_at, 20 * TX * 4)
        mh = b_r.tensor("mh", [P, KT, T], F32R)
        ml = b_r.tensor("ml", [P, KT, T], F32R)

        def pe_branch(eng, st):
            eng.wait_ge(S("o_s_lo"), 2)
            with eng.Fori(0, st.n // 2) as i:
                for s in range(2):
                    unit_ready(eng, s, i + st.m0)
                    eng.wait_ge(S(f"gated{s}"), i * 2 + 1)
                    for t in range(2):
                        for k in range(HP):
                            w = slice((t * HP + k) * P, (t * HP + k + 1) * P)
                            mm = split_product(eng, 4 * s + 2 * t, whi[s][:, w], wlo[s][:, w],
                                               xh[:, t * HP + k, 0:T], xl[:, t * HP + k, 0:T], HALF, k == 0, k == HP - 1)
                    mm.then_inc(used[s], 1)

        def dve_branch(eng, st):
            with eng.Fori(0, st.n // 2) as i:
                for s in range(2):
                    one = lambda t, at: t[:, bass.ds(i * 2 + (at + s), 1)].rearrange("p a n -> p (a n)")
                    gate = lambda at: proj[:, bass.ds(i * 2 + (at + s), 1), 0:T].rearrange("p a (h n) -> p (a h) n", h=2)
                    eng.wait_ge(used[s], i + (st.m0 + 2))
                    eng.wait_ge(S(f"merged{s}"), i * 3 + 1)
                    eng.tensor_tensor(halves(sg[s][:]), two_halves(4 * s), gate(20), ALU.mult).then_inc(S(f"gated{s}"), 1)
                    eng.tensor_tensor(halves(u[s][:]), two_halves(4 * s + 2), gate(28), ALU.mult).then_inc(S(f"gated{s}"), 1)
                    eng.wait_ge(S(f"gated{s}"), i * 2 + 3)
                    eng.tensor_tensor(sg[s][:], sg[s][:], u[s][:], ALU.add).then_inc(S(f"merged{s}"), 1)
                    eng.wait_ge(S(f"merged{s}"), i * 3 + 2)
                    eng.tensor_copy(one(mh, 0), sg[s][:]).then_inc(S(f"merged{s}"), 1)
                    eng.wait_ge(S(f"merged{s}"), i * 3 + 3)
                    eng.tensor_tensor(one(ml, 0), sg[s][:], one(mh, 0).bitcast(F32), ALU.subtract)\
                       .then_inc(S(f"merged{s}"), 1)

        def pe_out(eng, st):
            for s in range(2):
                eng.wait_ge(S(f"merged{s}"), 3 * stages["branch"].n // 2 + 1)
            with eng.Fori(0, st.n // 2) as i:
                for s in range(2):
                    unit_ready(eng, s, i + st.m0)
                    eng.wait_ge(S(f"mixed_in{s}"), i * 2 + 1)
                    for t in range(2):
                        for k in range(KT):
                            w = slice((t * KT + k) * P, (t * KT + k + 1) * P)
                            mm = split_product(eng, 4 * s + 2 * t, whi[s][:, w], wlo[s][:, w], mh[:, k], ml[:, k],
                                               HALF, k == 0, k == KT - 1)
                    mm.then_inc(used[s], 1)

        def dve_out(eng, st):
            eng.wait_ge(S("h_back"), 16)
            with eng.Fori(0, st.n // 2) as i:
                for s in range(2):
                    eng.wait_ge(used[s], i + (st.m0 + 2))
                    for t in range(2):
                        row = y[:, bass.ds(i * 4 + (2 * s + t), 1)].rearrange("p a (h n) -> p (a h) n", h=2)
                        eng.scalar_tensor_tensor(row, two_halves(4 * s + 2 * t), 1.0 / ALPHA, row, ALU.mult, ALU.add)\
                           .then_inc(S(f"mixed_in{s}"), 1)

        block = ctx.enter_context(nc.Block())

        @block.sync
        def _(sp):
            sp.dma_start(vecs[:], io["vecs"]).then_inc(S("vecs_loaded"), 16)
            sp.dma_start(before[:], io["before"]).then_inc(S("vecs_loaded"), 16)
            for q in range(4):
                sp.dma_start(y[:, 2 * q:2 * q + 2], io["x"][:, 2 * q:2 * q + 2]).then_inc(S(f"x_loaded{q}"), 16)
            sp_stage(sp, stages["ffn1_in"], io["ffn1_w_in"])
            sp_stage(sp, stages["ffn1_out"], io["ffn1_w_out"])
            sp_stage(sp, stages["rkv"], io["w_rkv"])
            for q in range(6):
                s, m = mid_unit(q)
                src, cols = ((io["lora_wa"], KT * P), (io["lora_g"][0], KT * GL), (io["lora_g"][1], KT * GL),
                             (io["w_v"][:, 0:1536], 1536), (io["w_v"][:, 1536:3072], 1536),
                             (io["w_v"][:, 3072:4096], 1024))[q]
                load_unit(sp, s, m, src, cols)
                if q == 0:
                    sp.wait_ge(S("normed"), KT)
                    sp.dma_start(io["h"], y[:]).then_inc(S("h_stored"), 16)
                if q == 1:
                    sp.dma_start(inner2[0:HD], io["w_w2"]).then_inc(S("inner2_loaded"), 16)
                    sp.dma_start(inner2[HD:P], io["a_w2"]).then_inc(S("inner2_loaded"), 16)
                    sp.dma_start(inner2g[:], io["g_w2"]).then_inc(S("inner2_loaded"), 16)
            sp_stage(sp, stages["qkg"], io["w_qkg"])
            wait_w_in(sp)
            sp.dma_start(cst[:], io["constants"]).then_inc(S("cst_loaded"), 16)
            for s in range(2):
                sp.wait_ge(S(f"qkg_made{s}"), 7)
            sp.dma_start(io["k_rows"], proj[:, 16:20, 0:T]).then_inc(S("out_stored"), 16)
            sp.dma_start(io["v_rows"][0:SEQ].rearrange("(t p) n -> p t n", p=P), vt[:, 0:NT]).then_inc(S("out_stored"), 16)
            sp.dma_start(io["v_rows"][SEQ:T], vt[0:TS, NT]).then_inc(S("out_stored"), 16)
            sp.wait_ge(S("y_made"), NT + 1)
            sp.dma_start(state_s[:], io["state_s"]).then_inc(S("state_loaded"), 16)
            sp.wait_ge(S("state_made"), last)
            sp.dma_start(io["wkv_p"], state[:]).then_inc(S("states_stored"), 16)
            sp.wait_ge(*step("s_state", 2 * HP))
            sp.dma_start(io["wkv_s"], state_s[:]).then_inc(S("states_stored"), 16)
            sp_pages(sp, io)
            sp.wait_ge(S("o_s_lo"), 2)
            sp.wait_ge(S("h_stored"), 16)
            sp.wait_ge(S("out_stored"), 16 * 3)
            sp_stage(sp, stages["branch"], io["w_branch"])
            sp.dma_start(y[:], io["h"]).then_inc(S("h_back"), 16)
            sp_stage(sp, stages["out"], io["w_out"])
            sp_stage(sp, stages["ffn2_in"], io["ffn2_w_in"])
            sp_stage(sp, stages["ffn2_out"], io["ffn2_w_out"])
            for k in range(KT):
                sp.wait_ge(S("normed"), 2 * KT + k + 1)
                sp.dma_start(io["y"][:, k], y[:, k]).then_inc(S("y_stored"), 16)
            sp.wait_ge(S("y_stored"), 16 * KT)
            sp.wait_ge(S("states_stored"), 32)

        @block.gpsimd
        def _(pool):
            for s in range(2):
                pool.sem_inc(lo_made[s], 1)
            for name in ("ffn1_in", "ffn1_out", "rkv"):
                pool_stage(pool, stages[name])
            for q in range(6):
                make_lo(pool, *mid_unit(q), MID_COLS[q])
            pool_stage(pool, stages["qkg"])
            pool_wkv(pool)
            pool_wkv_s(pool)
            pool_stick(pool)
            for name in ("branch", "out", "ffn2_in", "ffn2_out"):
                pool_stage(pool, stages[name])

        @block.scalar
        def _(act):
            for s in range(2):
                act.sem_inc(hi_made[s], 1)
                act.sem_inc(S(f"rkv_made{s}"), 1)
                act.sem_inc(S(f"qkg_made{s}"), 1)
            act.sem_inc(S("y_made"), 1)
            act.wait_ge(S("vecs_loaded"), 32)
            make_hi(act, 0, 0, 2048)
            act_ffn_in(act, stages["ffn1_in"], 0, stages["ffn1_out"].cols)
            act_ffn_out(act, stages["ffn1_out"], stages["rkv"].cols)
            act_norm(act, 0, "ln1_g", "ln1_b", True)
            act_pairs(act, stages["rkv"], "rkv_made", 0, ACT.Copy, MID_COLS[0], (S("lora_weights"), 1))
            act_mid(act)
            st = stages["qkg"]
            qk, gates = Stage("qk", 4, st.cols, 2 * st.m0), Stage("gates", 8, st.cols, 2 * st.m0 + 4)
            act_pairs(act, qk, "qkg_made", 12, ACT.Copy, st.cols)
            act_pairs(act, gates, "qkg_made", 20, ACT.Sigmoid, 0)
            act_prep(act)
            act_wkv(act)
            act_wkv_s(act)
            act_heads(act)
            act_stick(act)
            act_samples(act)
            st = stages["branch"]
            act.wait_ge(S("o_s_lo"), 2)
            make_hi(act, 0, st.m0, st.cols)
            pipelined(act, st, lambda i, s: None, stages["out"].cols)
            pipelined(act, stages["out"], lambda i, s: None, stages["ffn2_in"].cols)
            act_norm(act, 1, "ln2_g", "ln2_b", True)
            act_ffn_in(act, stages["ffn2_in"], 1, stages["ffn2_out"].cols)
            act_ffn_out(act, stages["ffn2_out"], 0)
            act_norm(act, 2, "ln3_g", "ln3_b", False)

        @block.tensor
        def _(pe):
            for s in range(2):
                pe.sem_inc(used[s], 1)
                for j in (s, 2 + s):
                    pe.sem_inc(S(f"pages_used{j}"), 1)
            pe.wait_ge(S("x_split"), 2 * (KT + 1))
            pe_ffn_in(pe, stages["ffn1_in"], 0)
            pe_ffn_out(pe, stages["ffn1_out"], 0)
            pe.wait_ge(S("set_up"), 3)
            pe_norm(pe, 0, (S("y_added"), 2 + KT))
            pe.wait_ge(S("norm_lo"), KT)
            pe_pairs(pe, stages["rkv"], "rkv_made")
            pe_mid(pe)
            pe.wait_ge(S("v_made"), 2)
            pe_pairs(pe, stages["qkg"], "qkg_made")
            pe_prep(pe)
            pe_wkv(pe)
            pe_wkv_s(pe)
            pe_heads(pe)
            pe_stick(pe)
            pe_samples(pe)
            pe_branch(pe, stages["branch"])
            pe_out(pe, stages["out"])
            pe.wait_ge(S("mixed_in0"), 5)
            pe_norm(pe, 1, (S("mixed_in1"), 5))
            pe.wait_ge(S("norm_lo"), 2 * KT)
            pe_ffn_in(pe, stages["ffn2_in"], 1)
            pe_ffn_out(pe, stages["ffn2_out"], 1)
            pe_norm(pe, 2, (S("y_added"), 2 + 2 * KT))

        @block.vector
        def _(dve):
            for s in range(2):
                for name in ("ffn_read", "inner_split", "gated", "merged", "mixed_in"):
                    dve.sem_inc(S(f"{name}{s}"), 1)
            dve.sem_inc(S("y_added"), 2)
            dve.sem_inc(S("state_made"), 1)
            for a, value in ((mean_w[:], 1.0 / D_MODEL), (eps[:, 0:1], LN_EPS / ALPHA ** 2), (eps[:, 1:2], LNX_EPS)):
                dve.memset(a, value).then_inc(S("set_up"), 1)
            for k in range(KT + 1):
                if k < KT:
                    dve.wait_ge(S(f"x_loaded{k // 2}"), 16)
                    src, hi, lo = y[:, k], xh[:, k, 0:T], xl[:, k, 0:T]
                else:
                    dve.wait_ge(S("vecs_loaded"), 32)
                    src, hi, lo = before[:], xh[:, :, T:TX], xl[:, :, T:TX]
                dve.tensor_copy(hi, src).then_inc(S("x_split"), 1)
                dve.wait_ge(S("x_split"), 2 * k + 1)
                dve.tensor_tensor(lo, src, hi.bitcast(F32), ALU.subtract).then_inc(S("x_split"), 1)
            dve_ffn_in(dve, stages["ffn1_in"], 0)
            dve_ffn_out(dve, stages["ffn1_out"], 0)
            dve_norm(dve, 0, "ln1_g", True)
            dve_lora_weights(dve)
            dve_shift(dve).wait(dve)
            dve_lora_sum(dve)
            dve_prep(dve)
            dve_wkv(dve)
            dve_wkv_s(dve)
            dve_heads(dve)
            dve_stick(dve)
            dve_qb(dve)
            dve_samples(dve)
            dve_branch(dve, stages["branch"])
            dve_out(dve, stages["out"])
            dve_norm(dve, 1, "ln2_g", True)
            dve_ffn_in(dve, stages["ffn2_in"], 1)
            dve_ffn_out(dve, stages["ffn2_out"], 1)
            dve_norm(dve, 2, "ln3_g", False)


def tiles_of(w, k, n):
    return w.reshape(k, P, -1, n).transpose(2, 1, 0, 3)


def kernel(x_prompt, x_sample, cache_k, cache_v, state_wkv, state_shift, page_table,
           ln1_g, ln1_b, ffn1_w_in, ffn1_w_out, w_in, mu_rkv, mu_wag, w0, w_w1, w_w2,
           a0, a_w1, a_w2, g_w1, g_w2, k_k, k_a, r_k, lnx_g, lnx_b, sb_bias, w_branch, w_out,
           ln2_g, ln2_b, ffn2_w_in, ffn2_w_out, ln3_g, ln3_b):
    import concourse.bacc as bacc
    from concourse.bass_utils import run_bass_kernel_spmd

    a = {k: np.asarray(v) for k, v in locals().items() if k not in ("bacc", "run_bass_kernel_spmd")}
    cols = lambda v: v.reshape(-1, P).T
    by_feature = lambda t: t.reshape(-1, KT, P).transpose(2, 1, 0)
    tokens = np.concatenate([a["x_prompt"].reshape(SEQ, D_MODEL), a["x_sample"].reshape(TS, D_MODEL)])
    vecs = {"mu_w": a["mu_wag"][0, 0], "mu_a": a["mu_wag"][0, 1], "mu_g": a["mu_wag"][0, 2]}
    packed = [cols(vecs[n] if n in vecs else a[n].reshape(-1)) for n in VEC if not n.startswith("sb_bias")]
    bias = a["sb_bias"].reshape(NH)
    packed += [np.tile(bias[None], (P, 1)), np.tile(np.repeat(bias, DS), 4)[:, None]]

    def ffn_in(w):
        t = tiles_of(w[0], KT, P)
        return np.stack([t[:FT], t[FT:]], 2).reshape(FT, P, UNIT)

    def ffn_out(w):
        t = tiles_of(w[0], FT, P)
        return t.reshape(KT, P, 2, FH * P).transpose(0, 2, 1, 3).reshape(2 * KT, P, FH * P)

    def pairs(w):
        t = tiles_of(w, KT, P)
        return t.reshape(-1, 2, P, KT * P).transpose(0, 2, 1, 3).reshape(-1, P, UNIT)

    wi = a["w_in"][0]
    n3 = 3 * 512
    rows = lambda c: c[0].reshape(N_PHYS, PAGE, NH * HD)[:, ::-1]
    ins = {
        "vecs": np.concatenate(packed, 1), "before": by_feature(a["state_shift"][0]), "x": by_feature(tokens),
        "constants": constants(),
        "ffn1_w_in": ffn_in(a["ffn1_w_in"]), "ffn1_w_out": ffn_out(a["ffn1_w_out"]),
        "ffn2_w_in": ffn_in(a["ffn2_w_in"]), "ffn2_w_out": ffn_out(a["ffn2_w_out"]),
        "w_rkv": pairs(wi[:, :n3]),
        "lora_wa": tiles_of(np.concatenate([a["w_w1"][0], a["a_w1"][0]], 1), KT, P).reshape(P, KT * P),
        "lora_g": tiles_of(a["g_w1"][0], KT, GL).reshape(2, P, KT * GL),
        "w_v": wi[:, n3 + 1024:n3 + n3].reshape(KT, P, 512).transpose(1, 0, 2).reshape(P, KT * 512),
        "w_qkg": pairs(np.concatenate([wi[:, n3:n3 + 1024], wi[:, 2 * n3:]], 1)),
        "w_w2": a["w_w2"][0], "a_w2": a["a_w2"][0],
        "g_w2": a["g_w2"][0].reshape(2, GL, 512).transpose(1, 0, 2),
        "w_branch": tiles_of(a["w_branch"][0], KT, P).reshape(KT, P, KT * P), "w_out": pairs(a["w_out"][0]),
        "state_s": a["state_wkv"][0].reshape(NB, HP, 2, HD, HD).transpose(2, 4, 1, 0, 3).reshape(P, HP, NB, HD),
        "cache_k": rows(a["cache_k"]).reshape(N_PHYS, PAGE, HP, P).transpose(0, 3, 2, 1),
        "cache_v": rows(a["cache_v"]), "page_table": a["page_table"].astype(np.int32),
    }
    outs = {"y": [P, KT, T], "h": [P, KT, T], "k_rows": [P, HP, T], "v_rows": [T, 512],
            "wkv_p": [P, HP, P], "wkv_s": [P, HP, NB, HD]}

    nc = bacc.Bacc("TRN2", target_bir_lowering=False, num_devices=1)
    io, arrays = {}, {}
    for n, v in ins.items():
        v = np.ascontiguousarray(v)
        arrays["in_" + n] = v
        io[n] = nc.dram_tensor("in_" + n, list(v.shape), mybir.dt.from_np(v.dtype), kind="ExternalInput").ap()
    for n, shape in outs.items():
        io[n] = nc.dram_tensor("out_" + n, shape, F32, kind="ExternalOutput").ap()
    build(nc, io)
    got = run_bass_kernel_spmd(nc, [arrays], core_ids=[0]).results[0]

    y = got["out_y"].transpose(2, 1, 0).reshape(T, D_MODEL)
    k = got["out_k_rows"].transpose(2, 1, 0).reshape(T, NH, HD)
    v = got["out_v_rows"].reshape(T, NH, HD)
    shift = got["out_h"][:, :, SEQ - 1:][:, :, ::DS].transpose(2, 1, 0).reshape(1 + NB, D_MODEL)
    wp = got["out_wkv_p"].reshape(2, HD, HP, 2, HD)
    wp = np.stack([wp[0, :, :, 0], wp[1, :, :, 1]]).transpose(2, 0, 3, 1).reshape(1, 1, NH, HD, HD)
    ws = got["out_wkv_s"].reshape(2, HD, HP, NB, HD).transpose(3, 2, 0, 4, 1).reshape(1, NB, NH, HD, HD)
    return (y[:SEQ].reshape(1, SEQ, D_MODEL), y[SEQ:].reshape(NB, DS, D_MODEL),
            k[:SEQ].reshape(1, 1, SEQ, NH, HD), v[:SEQ].reshape(1, 1, SEQ, NH, HD), wp,
            shift[:1].reshape(1, 1, D_MODEL),
            k[SEQ:].reshape(1, NB, DS, NH, HD), v[SEQ:].reshape(1, NB, DS, NH, HD), ws,
            shift[1:].reshape(1, NB, D_MODEL))
```

```python
from contextlib import ExitStack

import numpy as np

import concourse.bass as bass
from concourse import mybir
from concourse.alu_op_type import AluOpType as ALU

F32 = mybir.dt.float32
F32R = mybir.dt.float32r
I32 = mybir.dt.int32
ACT = mybir.ActivationFunctionType
AX = mybir.AxisListType

P = 128
D_MODEL = 1024
KT = D_MODEL // P
SEQ = 512
NB = 8
DS = 4
TS = NB * DS
T = SEQ + TS
TX = T + NB
HALF = T // 2
HALFX = TX // 2
D_FF = 2816
FT = D_FF // P
FH = FT // 2
HD = 64
NH = 8
HP = NH // 2
PAGE = 128
N_PAGES = 8
N_PHYS = 80
PAST = PAGE * N_PAGES
CH = 64
LEVELS = 6
NT = SEQ // P
ALPHA = 2.0 ** 0.25
LN_EPS = 1e-5
LNX_EPS = 64e-5
DECAY = -float(np.exp(-0.5))
SCALE = HD ** -0.5
GL = 80
UNIT = 2048
MASKED = -30000.0

VEC = {}
NVEC = 0
for _name, _n in (("ln1_g", 8), ("ln1_b", 8), ("ln2_g", 8), ("ln2_b", 8), ("ln3_g", 8), ("ln3_b", 8),
                  ("mu_w", 8), ("mu_a", 8), ("mu_g", 8), ("mu_rkv", 12), ("w0", 4), ("a0", 4),
                  ("k_k", 4), ("k_a", 4), ("r_k", 4), ("lnx_g", 4), ("lnx_b", 4), ("sb_bias", 8),
                  ("sb_bias_rows", 1)):
    VEC[_name] = NVEC
    NVEC += _n

CST = {}
NCST = 0
for _name, _n in (("pair", P), ("ident", P), ("ones", P), ("suffix", P), ("keep", T), ("own", NB),
                  ("own_rows", 2 * NB), ("own_head", NH), ("pick", 16), ("self", DS), ("cap", DS),
                  ("score", 2 * P), ("score_s", 2 * P), ("level", LEVELS * P)):
    CST[_name] = NCST
    NCST += _n
N_MASKS = (4 + LEVELS) * P


def constants():
    c = np.zeros((P, NCST), np.float32)
    row, col = np.arange(P)[:, None], np.arange(P)[None, :]

    def put(name, a):
        c[:, CST[name]:CST[name] + a.shape[1]] = a

    put("pair", row // HD == col // HD)
    put("ident", row == col)
    put("ones", np.ones((P, P)))
    put("suffix", row >= col)
    same = row // CH == col // CH
    put("score", np.concatenate([same & (row < col), same & (row <= col)], 1))
    same = row // DS == col // DS
    put("score_s", np.concatenate([same & (row < col), same & (row <= col)], 1))
    put("level", np.concatenate(
        [(row // (2 * n) == col // (2 * n)) & (row % (2 * n) < n) & (col % (2 * n) >= n)
         for n in (2 ** l for l in range(LEVELS))], 1))
    keep = np.ones((P, T))
    keep[:, :SEQ][:, ::CH] = 0
    keep[:, SEQ:][:, ::DS] = 0
    put("keep", keep)
    put("own", (row % TS) // DS == np.arange(NB)[None])
    put("own_rows", np.concatenate([row // TS + 4 * g == np.arange(NB)[None] for g in range(2)], 1))
    put("own_head", (row % TS) // DS == np.arange(NH)[None])
    put("pick", (row // TS == np.arange(16)[None] // DS) & (row % DS == np.arange(16)[None] % DS))
    seen = (DS - 1 - np.arange(DS)[None]) < row % DS
    put("self", seen)
    put("cap", np.where(seen, 3e38, MASKED))
    return c


def build(nc, io):
    ctx = ExitStack()
    with ctx:
        sems = {}

        def S(name):
            name = STEPS[name][0] if name in STEPS else name
            if name not in sems:
                sems[name] = ctx.enter_context(nc.semaphore(name))
            return sems[name]

        STEPS = {}

        def in_a_row(shared, steps, first=0):
            for name, times in steps:
                STEPS[name] = (shared, first, 1)
                first += times

        def in_turn(shared, *steps):
            for j, name in enumerate(steps):
                STEPS[name] = (shared, j + 1 - len(steps), len(steps))

        def step(name, n=1):
            shared, first, every = STEPS[name]
            return S(shared), first + every * n

        in_a_row("prep_products", (("k_summed", HP), ("lora_second", 3 * HP)))
        in_a_row("prep_scalar", (("k_squared", HP), ("k_norm", HP), ("lora_out", 3 * HP)))
        in_a_row("s_products", (("s_scored", 2), ("s_turned", 1), ("s_with_state", 1), ("s_carry", 2),
                                ("s_grown", 1), ("s_ak", 1), ("s_sa", 1), ("s_y", 1), ("s_update", 1),
                                ("s_y_turned", 1)))
        in_a_row("s_scalar", (("s_tok", 1), ("s_carry_made", 1), ("s_sa_made", 1)))
        in_a_row("s_pool", (("s_v_copied", 1), ("s_mask_made", 2)))
        in_a_row("s_vector", (("s_scaled", 4), ("s_masked", 2), ("s_inv", 3), ("s_rhs", 1), ("s_expanded", 4),
                              ("s_y_summed", 1), ("s_state", 2 * HP)))
        in_turn("heads_products", "y_mean", "rk_summed", "y_var")
        in_turn("heads_scalar", "y_squared", "y_std", "o_a_hi")
        in_turn("heads_vector", "rk_made", "y_centred", "bonus_made", "o_a_made")
        in_a_row("heads_vector", (("o_a_lo", HP),), 4 * HP)

        base0 = nc.sbuf_base + (-nc.sbuf_base) % 32
        arena_bytes = (nc.sbuf_usable_end - base0) // 32 * 32
        ctx.enter_context(nc.sbuf_tensor("arena", [P, arena_bytes // 4], F32))

        class Region:
            def __init__(self, start, size):
                self.start, self.at, self.end = start, start, start + size

            def tensor(self, name, shape, dtype=F32):
                size = 4 * int(np.prod(shape[1:]))
                assert self.at + size <= self.end, (name, self.at + size - self.end)
                t = nc.alloc_sbuf_tensor_at(name, shape, dtype, offset=self.at)
                self.at += (size + 31) // 32 * 32
                return t

        whole = Region(base0, arena_bytes)

        def region(size):
            r = Region(whole.at, size)
            whole.at += size
            assert whole.at <= whole.end
            return r

        keepers = region((4 * (NVEC + P + KT * NB + 2 * TS) + 14 * 32 + 31) // 32 * 32 + 64)
        vecs = keepers.tensor("vecs", [P, NVEC])
        mean_w = keepers.tensor("mean_w", [P, P])
        eps = keepers.tensor("eps", [P, 2])
        spare = keepers.tensor("spare", [P, 1])
        before = keepers.tensor("before", [P, KT, NB])

        one_less = keepers.tensor("one_less", [P, HP])
        self4 = keepers.tensor("self4", [P, DS])
        own_self = keepers.tensor("own_self", [P, 2, NB, DS])
        page_of = keepers.tensor("page_of", [1, NB * N_PAGES], I32)

        split_at = whole.at
        split_r = region(2 * 4 * KT * TX)
        xh = split_r.tensor("xh", [P, KT, TX], F32R)
        xl = split_r.tensor("xl", [P, KT, TX], F32R)
        y_r = region(4 * KT * T)
        y = y_r.tensor("y", [P, KT, T])

        ring_at = whole.at
        ring_r = region(6 * 4 * UNIT)
        raw = [ring_r.tensor(f"raw{s}", [P, UNIT]) for s in range(2)]
        whi = [ring_r.tensor(f"whi{s}", [P, UNIT], F32R) for s in range(2)]
        wlo = [ring_r.tensor(f"wlo{s}", [P, UNIT], F32R) for s in range(2)]

        temp_at = whole.at
        temp_bytes = 4 * 4 * T
        temp_r = region(temp_bytes)
        sg = [temp_r.tensor(f"sg{s}", [P, T]) for s in range(2)]
        u = [temp_r.tensor(f"u{s}", [P, T]) for s in range(2)]
        temp_r.at = temp_at
        sq = [temp_r.tensor(f"sq{s}", [P, T]) for s in range(2)]
        rstd = temp_r.tensor("rstd", [P, T])
        total = temp_r.tensor("total", [P, T])

        big_at = whole.at
        big_bytes = 2 * 4 * FT * T + 128
        big_r = region(big_bytes)
        gh = big_r.tensor("gh", [P, FT, T], F32R)
        gl = big_r.tensor("gl", [P, FT, T], F32R)
        big_r.at = big_at
        proj = big_r.tensor("proj", [P, 20, TX])
        g_at = big_r.at
        big_r.at += 16 * TX * 4
        vt = big_r.tensor("vt", [P, NT + 1, 512])
        inner2 = big_r.tensor("inner2", [P, 512])
        inner2g = big_r.tensor("inner2g", [GL, 2, 512])
        big_r.at = g_at
        lora = big_r.tensor("lora", [P, 6, TX])
        temp_r.at = temp_at
        temp_diff = temp_r.tensor("temp_diff", [P, 4, T])
        G_BYTES = 16 * TX * 4
        g_r = Region(g_at, G_BYTES)
        a_b = g_r.tensor("a_b", [P, HP, T])
        g_out = g_r.tensor("g_out", [P, HP, T])
        kk = g_r.tensor("kk", [P, HP, T])
        zp_at = g_r.at
        lora_wa = g_r.tensor("lora_wa", [P, T])
        lora_g = g_r.tensor("lora_g", [GL, 2, T])
        zp = Region(zp_at, g_at + G_BYTES - zp_at).tensor("zp", [P, 2, PAST + DS])
        squares = Region(g_at, G_BYTES).tensor("squares", [P, HP, T])
        g_r = Region(g_at, G_BYTES)
        hh = g_r.tensor("hh", [P, KT, T], F32R)
        hl = g_r.tensor("hl", [P, KT, T], F32R)


        psum = ctx.enter_context(nc.psum_tensor("psum", [P, 8, 512], F32))

        def vec(name, i):
            return vecs[:, VEC[name] + i:VEC[name] + i + 1]

        class Stage:
            def __init__(self, name, n, cols, first):
                self.name, self.n, self.cols, self.m0 = name, n, cols, first // 2
                assert first % 2 == 0 and n % 2 == 0

        stages, at = {}, 0
        for name, n, cols in (("ffn1_in", FT, 2048), ("ffn1_out", 16, FH * P), ("rkv", 6, 2048),
                              ("mid", 6, None), ("qk", 4, 2048), ("merge", 2 * KT, None),
                              ("out", 4, 2048), ("ffn2_in", FT, 2048), ("ffn2_out", 16, FH * P)):
            stages[name] = Stage(name, n, cols, at)
            at += n
        MERGE_COLS = [2 * D_MODEL, D_MODEL]
        MID_COLS = [2 * 1024, 2 * 8 * GL, 2 * 8 * GL, 3 * 512, 3 * 512, 2 * 512]
        landed = [S(f"raw_landed{s}") for s in range(2)]
        hi_made = [S(f"hi_made{s}") for s in range(2)]
        lo_made = [S(f"lo_made{s}") for s in range(2)]
        used = [S(f"unit_used{s}") for s in range(2)]

        def load_unit(eng, s, m, src, cols):
            eng.wait_ge(hi_made[s], m + 1)
            eng.wait_ge(lo_made[s], m + 1)
            eng.dma_start(raw[s][:, 0:cols], src).then_inc(landed[s], 16)

        def make_hi(eng, s, m, cols, ready=None):
            if ready is None:
                eng.wait_ge(landed[s], (m + 1) * 16)
            else:
                eng.wait_ge(*ready)
            eng.wait_ge(used[s], m + 1)
            eng.activation(whi[s][:, 0:cols], raw[s][:, 0:cols], ACT.Copy).then_inc(hi_made[s], 1)

        def make_lo(eng, s, m, cols):
            eng.wait_ge(hi_made[s], m + 2)
            eng.tensor_tensor(wlo[s][:, 0:cols], raw[s][:, 0:cols], whi[s][:, 0:cols].bitcast(F32),
                              ALU.subtract).then_inc(lo_made[s], 1)

        def unit_ready(eng, s, m):
            eng.wait_ge(hi_made[s], m + 2)
            eng.wait_ge(lo_made[s], m + 2)

        def two_halves(bank, n=HALF):
            return psum[:, bank:bank + 2, 0:n]

        def halves(a):
            return a.rearrange("p (h n) -> p h n", h=2)

        def split_product(eng, bank, w_hi, w_lo, a_hi, a_lo, n, first, last, rows=P):
            mm = None
            for k, (w, a) in enumerate(((w_hi, a_hi), (w_hi, a_lo), (w_lo, a_hi))):
                for h in range(2):
                    mm = eng.matmul(psum[0:rows, bank + h, 0:n], w, a[:, h * n:(h + 1) * n],
                                    start=first and k == 0, stop=last and k == 2)
            return mm

        def cols_of(st, s):
            return st.cols if st.cols else MERGE_COLS[s]

        def sp_stage(eng, st, dram):
            with eng.Fori(0, st.n // 2) as i:
                for s in range(2):
                    load_unit(eng, s, i + st.m0, dram[bass.ds(i * 2 + s, 1)].rearrange("a p n -> (a p) n"),
                              st.cols)

        def pool_stage(eng, st):
            with eng.Fori(0, st.n // 2) as i:
                for s in range(2):
                    make_lo(eng, s, i + st.m0, cols_of(st, s))

        def pipelined(eng, st, work, next_cols, next_ready=None):
            def body(i, last):
                make_hi(eng, 1, i + st.m0, cols_of(st, 1))
                work(i, 0)
                if last:
                    if next_cols:
                        make_hi(eng, 0, i + st.m0 + 1, next_cols, next_ready)
                else:
                    make_hi(eng, 0, i + (st.m0 + 1), cols_of(st, 0))
                work(i, 1)
            with eng.Fori(0, st.n // 2 - 1) as i:
                body(i, False)
            body(st.n // 2 - 1, True)

        def pe_ffn_in(eng, st, r, tile_ready):
            with eng.Fori(0, FT // 2) as i:
                for s in range(2):
                    unit_ready(eng, s, i + st.m0)
                    eng.wait_ge(S(f"ffn_read{s}"), i + (r * (FT // 2) + 1))
                    w_hi = whi[s][:].rearrange("p (t k n) -> p t k n", t=2, k=KT)
                    w_lo = wlo[s][:].rearrange("p (t k n) -> p t k n", t=2, k=KT)
                    for t in range(2):
                        for k in range(KT):
                            if s == t == 0:
                                eng.wait_ge(*tile_ready(k))
                            mm = split_product(eng, 4 * s + 2 * t, w_hi[:, t, k], w_lo[:, t, k],
                                               xh[:, k, 0:T], xl[:, k, 0:T], HALF, k == 0, k == KT - 1)
                        mm.then_inc(S(f"gate_done{s}") if t == 0 else used[s], 1)

        def act_ffn_in(eng, st, r, next_cols):
            def work(i, s):
                eng.wait_ge(S(f"gate_done{s}"), i + (r * (FT // 2) + 1))
                eng.wait_ge(S(f"ffn_read{s}"), i + (r * (FT // 2) + 1))
                eng.activation(halves(sg[s][:]), two_halves(4 * s), ACT.Sigmoid)\
                   .then_inc(S(f"sigmoid_made{s}"), 1)
            pipelined(eng, st, work, next_cols)

        def dve_ffn_in(eng, st, r):
            with eng.Fori(0, FT // 2) as i:
                for s in range(2):
                    n = i + (r * (FT // 2) + 1)
                    f = bass.ds(i * 2 + s, 1)
                    eng.wait_ge(S(f"sigmoid_made{s}"), n)
                    eng.tensor_tensor(halves(sg[s][:]), two_halves(4 * s), halves(sg[s][:]), ALU.mult)\
                       .then_inc(S(f"silu_made{s}"), 1)
                    eng.wait_ge(used[s], i + (st.m0 + 2))
                    eng.wait_ge(S(f"silu_made{s}"), n)
                    eng.wait_ge(S(f"inner_split{s}"), n * 2 - 1)
                    eng.tensor_tensor(halves(u[s][:]), two_halves(4 * s + 2), halves(sg[s][:]), ALU.mult)\
                       .then_inc(S(f"ffn_read{s}"), 1)
                    eng.wait_ge(S(f"ffn_read{s}"), n + 1)
                    eng.tensor_copy(gh[:, f].rearrange("p a n -> p (a n)"), u[s][:])\
                       .then_inc(S(f"inner_split{s}"), 1)
                    eng.wait_ge(S(f"inner_split{s}"), n * 2)
                    eng.tensor_tensor(gl[:, f].rearrange("p a n -> p (a n)"), u[s][:],
                                      gh[:, f].rearrange("p a n -> p (a n)").bitcast(F32), ALU.subtract)\
                       .then_inc(S(f"inner_split{s}"), 1)

        def pe_ffn_out(eng, st, r):
            for s in range(2):
                eng.wait_ge(S(f"inner_split{s}"), (r + 1) * FT + 1)
            with eng.Fori(0, KT // 2) as i:
                for j in range(2):
                    eng.wait_ge(S("y_added"), i * 2 + (r * KT + j + 1))
                    for s in range(2):
                        unit_ready(eng, s, i * 2 + (st.m0 + j))
                        for k in range(FH):
                            f = s * FH + k
                            w = slice(k * P, (k + 1) * P)
                            mm = split_product(eng, 2 * j, whi[s][:, w], wlo[s][:, w], gh[:, f], gl[:, f],
                                               HALF, f == 0, f == FT - 1)
                        mm.then_inc(used[s], 1)

        def act_ffn_out(eng, st, next_cols):
            pipelined(eng, st, lambda i, s: None, next_cols)

        def dve_ffn_out(eng, st, r):
            for s in range(2):
                eng.wait_ge(S(f"inner_split{s}"), (r + 1) * FT + 1)
            eng.memset(total[:], 0.0).then_inc(S("totalled"), 1)
            with eng.Fori(0, KT // 2) as i:
                for j in range(2):
                    eng.wait_ge(used[1], i * 2 + (st.m0 + j + 2))
                    row = y[:, bass.ds(i * 2 + j, 1)].rearrange("p a (h n) -> p (a h) n", h=2)
                    eng.scalar_tensor_tensor(row, two_halves(2 * j), 0.5 / ALPHA, row, ALU.mult, ALU.add)\
                       .then_inc(S("y_added"), 1)
                    eng.wait_ge(S("y_added"), i * 2 + (r * KT + j + 3))
                    eng.wait_ge(S("totalled"), i * 2 + ((2 * r) * (KT + 1) + j + 1))
                    eng.tensor_tensor(halves(total[:]), halves(total[:]), row, ALU.add).then_inc(S("totalled"), 1)

        def pe_norm(eng, n):
            eng.wait_ge(S("totalled"), (n + 1) * (KT + 1))
            for h in range(2):
                mm = eng.matmul(psum[:, 4 + h, 0:HALF], mean_w[:], total[:, h * HALF:(h + 1) * HALF],
                                start=True, stop=True)
            mm.then_inc(S("mean_done"), 1)
            for k in range(KT):
                eng.wait_ge(S("squared"), n * KT + k + 1)
                for h in range(2):
                    mm = eng.matmul(psum[:, 6 + h, 0:HALF], mean_w[:], sq[k % 2][:, h * HALF:(h + 1) * HALF],
                                    start=k == 0, stop=k == KT - 1)
                mm.then_inc(S("square_summed"), 1)

        def act_norm(eng, n, gname, bname, split):
            eng.activation(spare[:], eps[:, 0:1], ACT.Sqrt).then_inc(S("std_made"), 1)
            for k in range(KT):
                eng.wait_ge(S("centred"), n * KT + k + 1)
                if n * KT + k >= 2:
                    eng.wait_ge(S("square_summed"), n * KT + k - 1)
                eng.activation(sq[k % 2][:], y[:, k], ACT.Square).then_inc(S("squared"), 1)
            eng.wait_ge(S("square_summed"), (n + 1) * KT)
            eng.activation(halves(total[:]), two_halves(6), ACT.Sqrt, bias=eps[:, 0:1]).then_inc(S("std_made"), 1)
            for k in range(KT):
                eng.wait_ge(S("scaled"), n * KT + k + 1)
                if split:
                    eng.activation(xh[:, k, 0:T], y[:, k], ACT.Identity, bias=vec(bname, k))\
                       .then_inc(S("norm_hi"), 1)
                    eng.wait_ge(S("norm_hi"), n * KT + k + 1)
                eng.activation(y[:, k], y[:, k], ACT.Identity, bias=vec(bname, k)).then_inc(S("normed"), 1)

        def dve_norm(eng, n, gname, split):
            eng.wait_ge(S("mean_done"), n + 1)
            for k in range(KT):
                eng.tensor_tensor(halves(y[:, k]), halves(y[:, k]), two_halves(4), ALU.subtract)\
                   .then_inc(S("centred"), 1)
            eng.wait_ge(S("square_summed"), (n + 1) * KT)
            eng.wait_ge(S("std_made"), 2 * n + 2)
            eng.reciprocal(rstd[:], total[:]).then_inc(S("rstd_made"), 1)
            eng.wait_ge(S("rstd_made"), n + 1)
            eng.wait_ge(S("centred"), (n + 1) * KT)

            def low(k):
                eng.wait_ge(S("normed"), n * KT + k + 1)
                eng.tensor_tensor(xl[:, k, 0:T], y[:, k], xh[:, k, 0:T].bitcast(F32), ALU.subtract)\
                   .then_inc(S("norm_lo"), 1)

            for k in range(KT):
                eng.scalar_tensor_tensor(y[:, k], y[:, k], vec(gname, k), rstd[:], ALU.mult, ALU.mult)\
                   .then_inc(S("scaled"), 1)
                if split and k >= 2:
                    low(k - 2)
            if split:
                low(KT - 2)
                low(KT - 1)

        n_r = Region(y_r.start, y_r.end - y_r.start)
        ldec = n_r.tensor("ldec", [P, HP, T])
        logp = n_r.tensor("logp", [P, HP, T])
        norms = Region(y_r.start + 4 * HP * T, 4 * HP * T).tensor("norms", [P, HP, T])
        c_r = Region(temp_at, temp_bytes)
        cst = c_r.tensor("cst", [P, NCST - N_MASKS])
        k_share = c_r.tensor("k_share", [P, T])
        z_r = Region(ring_at, temp_at - ring_at)
        masks = z_r.tensor("masks", [P, N_MASKS])
        prep_at = z_r.at
        scores = z_r.tensor("scores", [P, NH, 4, P])
        dm = [z_r.tensor(f"inv{g}", [P, 4, P]) for g in range(2)]
        dt = [z_r.tensor(f"inv_t{g}", [P, 4, P]) for g in range(2)]
        wm = [z_r.tensor(f"carry{g}", [P, 4, P]) for g in range(2)]
        tmp_s = z_r.tensor("tmp_s", [P, HP, P])
        e_in = z_r.tensor("e_in", [P, HP, P])
        tok = z_r.tensor("tok", [P, 3, 512])
        e_inv = z_r.tensor("e_inv", [P, HP, P])
        a_r = Region(split_at, split_r.end - split_r.start)
        ar = a_r.tensor("ar", [P, HP, 2, P])
        bk = a_r.tensor("bk", [P, 2, HP, P])
        state = a_r.tensor("state", [P, HP, P])
        end_w = a_r.tensor("end_w", [P, HP, P])
        e_ex = a_r.tensor("e_ex", [P, HP, P])
        sums_at = a_r.at
        k_pages = [a_r.tensor(f"k_pages{s}", [P, 2, HP, 2 * PAGE]) for s in range(2)]
        qb = a_r.tensor("qb", [P, HP, NB, NH, DS])
        a_r = Region(sums_at, split_r.end - sums_at)
        lp = a_r.tensor("lp", [P, 2, PAST + DS])
        cp = a_r.tensor("cp", [P, 2, PAST + DS])
        em = [e_ex, e_inv]
        xs, sas = dm[0], dm[1]
        vf = tmp_s
        t_r = Region(prep_at, z_r.end - prep_at)
        t1 = t_r.tensor("t1", [P, HP, T])
        t2 = t_r.tensor("t2", [P, HP, T])
        t3 = t_r.tensor("t3", [P, HP, T])
        t4 = t_r.tensor("t4", [P, HP, T])
        s_r = Region(prep_at + 4 * 2 * 4 * P, 4 * 6 * 4 * P)
        state_s = s_r.tensor("state_s", [P, HP, NB, HD])
        own_x = s_r.tensor("own_x", [P, 2, NB, HD])
        q_r = Region(y_r.start, 4 * HP * T)
        own_v = q_r.tensor("own_v", [P, 2, NB, HD])
        x_red = q_r.tensor("x_red", [P, 2, 2, HD])
        e_in_s = q_r.tensor("e_in_s", [P, HP, TS])
        p_r = Region(big_at, 12 * TX * 4)
        zs = [p_r.tensor(f"zs{s}", [P, 10 * P]) for s in range(2)]
        ls = [p_r.tensor(f"ls{s}", [P, 10 * P]) for s in range(2)]
        ob = [p_r.tensor(f"ob{s}", [P, SEQ]) for s in range(2)]
        k_r = Region(z_r.start, z_r.end - z_r.start)
        pages = [k_r.tensor(f"pages{s}", [P, 4, 512]) for s in range(4)]
        zsum = k_r.tensor("zsum", [P, 512])
        a_self_t = k_r.tensor("a_self_t", [TS, 2, P])
        a_t = k_r.tensor("a_t", [P, 2, N_PAGES, P])

        def cc(name, n=P, skip=0):
            at = CST[name] + skip
            return cst[:, at:at + n] if at < NCST - N_MASKS else masks[:, at - (NCST - N_MASKS):at - (NCST - N_MASKS) + n]

        def bcast(a, n):
            return a.unsqueeze(1).broadcast_to([a.shape[0], n, a.shape[1]])

        def each(a, n):
            return a.unsqueeze(2).broadcast_to([a.shape[0], a.shape[1], n])

        def samples(a):
            return a.rearrange("p (b t) -> p b t", t=DS)

        class Count:
            def __init__(self, name):
                self.name, self.n = name, 0

            def up(self, ins):
                self.n += 1
                ins.then_inc(S(self.name), 1)
                return self.n

            def wait(self, eng, n=None):
                eng.wait_ge(S(self.name), self.n if n is None else n)

        dve_steps = Count("dve_steps")

        def pe_pairs(eng, st, made, tile_ready=None):
            with eng.Fori(0, st.n // 2) as i:
                for s in range(2):
                    unit_ready(eng, s, i + st.m0)
                    eng.wait_ge(S(f"{made}{s}"), i + 1)
                    w_hi = whi[s][:].rearrange("p (t k n) -> p t k n", t=2, k=KT)
                    w_lo = wlo[s][:].rearrange("p (t k n) -> p t k n", t=2, k=KT)
                    for t in range(2):
                        for k in range(KT):
                            if tile_ready and s == t == 0:
                                eng.wait_ge(*tile_ready(k))
                            mm = split_product(eng, 4 * s + 2 * t, w_hi[:, t, k], w_lo[:, t, k],
                                               xh[:, k], xl[:, k], HALFX, k == 0, k == KT - 1)
                    mm.then_inc(used[s], 1)

        def unit_banks(s, n=HALFX, rows=P):
            return psum[0:rows, 4 * s:4 * s + 4, 0:n]

        def act_pairs(eng, st, made, tile0, func_of, next_cols, next_ready=None):
            def work(i, s):
                eng.wait_ge(used[s], i + (st.m0 + 2))
                first = i * 4 + (tile0 + 2 * s)
                tiles = bass.ds(first, 2) if not isinstance(first, int) else slice(first, first + 2)
                dst = proj[:, tiles].rearrange("p t (h n) -> p (t h) n", h=2)
                eng.activation(dst, unit_banks(s), func_of).then_inc(S(f"{made}{s}"), 1)
            pipelined(eng, st, work, next_cols, next_ready)

        def mid_unit(q):
            return q % 2, stages["mid"].m0 + q // 2

        def pe_mid(eng):
            for q in range(3):
                s, m = mid_unit(q)
                n = P if q == 0 else GL
                unit_ready(eng, s, m)
                eng.wait_ge(S(f"rkv_made{s}"), 3 + 1)
                if q == 2:
                    eng.wait_ge(S("lora_copied"), 1)
                for t in range(2):
                    for k in range(KT):
                        w = slice((t * KT + k) * n, (t * KT + k + 1) * n)
                        mm = split_product(eng, 4 * s + 2 * t, whi[s][:, w], wlo[s][:, w], xh[:, k], xl[:, k],
                                           HALFX, k == 0, k == KT - 1, rows=n)
                mm.then_inc(used[s], 1)
            eng.wait_ge(S("lora_copied"), 3)
            for q in range(3, 6):
                s, m = mid_unit(q)
                unit_ready(eng, s, m)
                for j in range(3 if q < 5 else 2):
                    k = 3 * (q - 3) + j
                    w = slice(j * 512, (j + 1) * 512)
                    for tt in range(NT + 1):
                        rows = P if tt < NT else TS
                        c = slice(tt * P, tt * P + rows)
                        for n, (a, b) in enumerate(((xh, whi), (xh, wlo), (xl, whi))):
                            mm = eng.matmul(psum[0:rows, tt, :], a[:, k, c], b[s][:, w],
                                            start=k == 0 and n == 0, stop=k == KT - 1 and n == 2)
                mm.then_inc(used[s], 1)

        def act_mid(eng):
            st = stages["mid"]
            for q in range(3):
                s, m = mid_unit(q)
                ns, nm = mid_unit(q + 1)
                if q < 2:
                    make_hi(eng, ns, nm, MID_COLS[q + 1], (S("lora_weights"), q + 2))
                else:
                    make_hi(eng, ns, nm, MID_COLS[q + 1])
                rows = P if q == 0 else GL
                eng.wait_ge(used[s], m + 2)
                eng.activation(lora[0:rows, 2 * q:2 * q + 2].rearrange("p t (h n) -> p (t h) n", h=2),
                               unit_banks(s, rows=rows), ACT.Copy).then_inc(S("lora_copied"), 1)
            for q in range(4, 6):
                s, m = mid_unit(q)
                make_hi(eng, s, m, MID_COLS[q])
            eng.wait_ge(S("lora_summed"), 8)
            eng.activation(lora_wa[0:HD], lora_wa[0:HD], ACT.Tanh).then_inc(S("lora_inner"), 1)
            eng.wait_ge(S("lora_summed"), 24)
            eng.activation(lora_g[:], lora_g[:], ACT.Sigmoid).then_inc(S("lora_inner"), 1)
            make_hi(eng, 0, stages["qk"].m0, stages["qk"].cols)
            for f in range(HP):
                eng.wait_ge(S("k_scaled"), f + 1)
                eng.activation(squares[:, f], kk[:, f], ACT.Square).then_inc(S("k_squared"), 1)
            eng.wait_ge(used[1], st.m0 + 3 + 1)
            eng.activation(vt[:, 0:NT], psum[:, 0:NT, :], ACT.Copy).then_inc(S("v_made"), 1)
            eng.activation(vt[0:TS, NT], psum[0:TS, NT, :], ACT.Copy).then_inc(S("v_made"), 1)

        def dve_lora_weights(eng):
            c = dve_steps
            for q in range(3):
                s, m = mid_unit(q)
                n = P if q == 0 else GL
                eng.wait_ge(landed[s], (m + 1) * 16)
                w = raw[s][:, 0:KT * n].rearrange("p (k n) -> p k n", k=KT)
                mw = raw[s][:, KT * n:2 * KT * n].rearrange("p (k n) -> p k n", k=KT)
                parts = (("mu_w", 0, HD), ("mu_a", HD, HD)) if q == 0 else (("mu_g", 0, GL),)
                for name, at, width in parts:
                    mu = each(vecs[:, VEC[name]:VEC[name] + KT], width)
                    c.up(eng.tensor_tensor(mw[:, :, at:at + width], w[:, :, at:at + width], mu, ALU.mult))
                c.wait(eng)
                eng.tensor_tensor(w, w, mw, ALU.subtract).then_inc(S("lora_weights"), 1)

        def dve_shift(eng):
            c = dve_steps
            for grp in range(3):
                for s in range(2):
                    eng.wait_ge(S(f"rkv_made{s}"), grp + 2)
                p = proj[:, 4 * grp:4 * grp + 4]
                c.up(eng.tensor_tensor(temp_diff[:, :, 1:SEQ], p[:, :, 0:SEQ - 1], p[:, :, 1:SEQ], ALU.subtract))
                c.up(eng.tensor_scalar(temp_diff[:, :, 0:1], p[:, :, 0:1], -1.0, None, ALU.mult))
                for f in range(4):
                    ps, d = samples(p[:, f, SEQ:T]), samples(temp_diff[:, f, SEQ:T])
                    c.up(eng.tensor_tensor(d[:, :, 1:DS], ps[:, :, 0:DS - 1], ps[:, :, 1:DS], ALU.subtract))
                    c.up(eng.tensor_tensor(d[:, :, 0], p[:, f, T:TX], ps[:, :, 0], ALU.subtract))
                c.wait(eng)
                for f in range(4):
                    c.up(eng.scalar_tensor_tensor(p[:, f, 0:T], temp_diff[:, f], vec("mu_rkv", 4 * grp + f),
                                                  p[:, f, 0:T], ALU.mult, ALU.add))
                c.wait(eng)
            return c

        def dve_lora_sum(eng):
            for q in range(3):
                eng.wait_ge(S("lora_copied"), q + 1)
                rows = P if q == 0 else GL
                a, b = lora[0:rows, 2 * q], lora[0:rows, 2 * q + 1]
                o = lora_wa[:] if q == 0 else lora_g[:, q - 1]
                sa, so = samples(a[:, SEQ:T]), samples(o[:, SEQ:T])
                sb_ = samples(b[:, SEQ:T])
                for step in (eng.tensor_tensor(o[:, 1:SEQ], a[:, 1:SEQ], b[:, 0:SEQ - 1], ALU.add),
                             eng.tensor_copy(o[:, 0:1], a[:, 0:1]),
                             eng.tensor_tensor(so[:, :, 1:DS], sa[:, :, 1:DS], sb_[:, :, 0:DS - 1], ALU.add),
                             eng.tensor_tensor(so[:, :, 0], sa[:, :, 0], b[:, T:TX], ALU.add)):
                    step.then_inc(S("lora_summed"), 2)

        def wait_w_in(eng):
            for s in range(2):
                eng.wait_ge(used[s], stages["qk"].m0 + 2 + 1)

        def prep_bank(n):
            return (6, 0, 2)[n % 3]

        def pe_prep(eng):
            def start(n):
                if n == 1:
                    eng.wait_ge(S("v_made"), 2)
                if n >= 3:
                    eng.wait_ge(*(step("k_norm", n - 2) if n - 3 < HP else step("lora_out", n - 2 - HP)))
                return prep_bank(n)
            eng.wait_ge(S("cst_loaded"), 16)
            for f in range(HP):
                bank = start(f)
                eng.wait_ge(*step("k_squared", f + 1))
                for h in range(2):
                    mm = eng.matmul(psum[:, bank + h, 0:HALF], cc("pair"), squares[:, f, h * HALF:(h + 1) * HALF],
                                    start=True, stop=True)
                mm.then_inc(S("k_summed"), 1)
            eng.wait_ge(S("lora_inner"), 2)
            eng.wait_ge(S("inner2_loaded"), 48)
            for f in range(HP):
                c = slice(f * P, (f + 1) * P)
                for q, parts in enumerate((((inner2[0:HD, c], lora_wa[0:HD]),), ((inner2[HD:P, c], lora_wa[HD:P]),),
                                           ((inner2g[:, 0, c], lora_g[:, 0]), (inner2g[:, 1, c], lora_g[:, 1])))):
                    bank = start(HP + 3 * f + q)
                    for h in range(2):
                        for n, (w, a) in enumerate(parts):
                            mm = eng.matmul(psum[:, bank + h, 0:HALF], w, a[:, h * HALF:(h + 1) * HALF],
                                            start=n == 0, stop=n == len(parts) - 1)
                    mm.then_inc(S("lora_second"), 1)
            eng.wait_ge(*step("lora_out", 3 * HP))

        def act_prep(eng):
            eng.wait_ge(S("h_stored"), 16)
            for f in range(HP):
                eng.wait_ge(*step("k_summed", f + 1))
                eng.activation(halves(norms[:, f]), two_halves(prep_bank(f)), ACT.Sqrt).then_inc(S("k_norm"), 1)
            for f in range(HP):
                for q, (dst, func, bias) in enumerate(((ldec, ACT.Sigmoid, vec("w0", f)),
                                                       (a_b, ACT.Sigmoid, vec("a0", f)), (g_out, ACT.Copy, 0.0))):
                    eng.wait_ge(*step("lora_second", 3 * f + q + 1))
                    eng.activation(halves(dst[:, f]), two_halves(prep_bank(HP + 3 * f + q)), func, bias=bias)\
                       .then_inc(S("lora_out"), 1)

        def dve_keys(eng):
            for f in range(HP):
                eng.tensor_scalar(kk[:, f], proj[:, 4 + f, 0:T], vec("k_k", f), None, ALU.mult)\
                   .then_inc(S("k_scaled"), 1)
            dve_steps.up(eng.tensor_scalar(one_less[:], vecs[:, VEC["k_a"]:VEC["k_a"] + HP], -1.0, 1.0, ALU.mult, ALU.add))

        def dve_prep(eng):
            c = dve_steps
            for f in range(HP):
                eng.wait_ge(*step("k_norm", f + 1))
                c.up(eng.tensor_scalar(norms[:, f], norms[:, f], 1e-12, None, ALU.max))
                c.wait(eng)
                c.up(eng.reciprocal(norms[:, f], norms[:, f]))
                c.wait(eng)
                c.up(eng.tensor_tensor(kk[:, f], kk[:, f], norms[:, f], ALU.mult))
            for f in range(HP):
                eng.wait_ge(*step("lora_out", 3 * f + 3))
                c.up(eng.tensor_scalar(ldec[:, f], ldec[:, f], DECAY, None, ALU.mult))
                c.wait(eng)
                c.up(eng.tensor_tensor_scan(logp[:, f], cc("keep", T), ldec[:, f], 0.0, ALU.mult, ALU.add))
                c.up(eng.tensor_scalar(k_share[:], a_b[:, f], vec("k_a", f), one_less[:, f:f + 1], ALU.mult, ALU.add))
                c.wait(eng)
                c.up(eng.tensor_tensor(ldec[:, f], logp[:, f], ldec[:, f], ALU.subtract))
                c.up(eng.tensor_tensor(proj[:, 4 + f, 0:T], proj[:, 4 + f, 0:T], k_share[:], ALU.mult))
                c.up(eng.tensor_tensor(a_b[:, f], kk[:, f], a_b[:, f], ALU.mult))
                c.wait(eng)
            wait_w_in(eng)
            eng.memset(state[:], 0.0).then_inc(S("prep_done"), 1)

        def c_rows(c):
            return slice(c * CH, (c + 1) * CH)

        def par_rows(h):
            return slice(h % 2 * HD, h % 2 * HD + HD)

        def act_wkv(eng):
            eng.wait_ge(S("prep_done"), 1)
            with eng.Fori(0, NT) as i:
                cols = bass.ds(i * P, P)
                eng.wait_ge(S("state_made"), i * 2 + 1)
                eng.activation(e_in[:], logp[:, :, cols], ACT.Exp).then_inc(S("decays"), 1)
                eng.activation(e_ex[:], ldec[:, :, cols], ACT.Exp).then_inc(S("decays"), 1)
                eng.activation(e_inv[:], logp[:, :, cols], ACT.Exp, scale=-1.0).then_inc(S("decays"), 1)
                eng.wait_ge(S("turned"), i * 3 + 3)
                for q in range(3):
                    eng.activation(tok[:, q], psum[:, 4 + q, :], ACT.Copy).then_inc(S("tok_made"), 1)
                for l in range(1, LEVELS):
                    for g in range(2):
                        eng.wait_ge(S(f"carry_done{g}"), i * LEVELS + (l + 1))
                        eng.activation(wm[g][:].rearrange("p h n -> p (h n)"), psum[:, 3 * g, :], ACT.Copy)\
                           .then_inc(S(f"carry_made{g}"), 1)
                for c in range(2):
                    eng.wait_ge(S("rhs_done"), i * 2 + (c + 1))
                    eng.activation(xs[c_rows(c)].rearrange("p h n -> p (h n)"), psum[c_rows(c), 6, :], ACT.Copy)\
                       .then_inc(S("rhs_made"), 1)
                    eng.wait_ge(S("sa_done"), i * 2 + (c + 1))
                    eng.activation(sas[c_rows(c)].rearrange("p h n -> p (h n)"), psum[c_rows(c), 3, :], ACT.Copy)\
                       .then_inc(S("sa_made"), 1)
                eng.wait_ge(S("y_done"), i + 1)
                eng.activation(kk[:, :, cols], psum[:, 0, :].rearrange("p (h n) -> p h n", h=HP), ACT.Copy)\
                   .then_inc(S("y_made"), 1)

        def pool_wkv(eng):
            eng.wait_ge(S("prep_done"), 1)
            eng.wait_ge(S("masks_loaded"), 16)
            with eng.Fori(0, NT) as i:
                cols = bass.ds(i * P, P)
                eng.wait_ge(S("state_made"), i * 2 + 1)
                eng.tensor_copy(vf[:], proj[:, 8:12, cols]).then_inc(S("v_copied"), 1)
                for l in range(LEVELS):
                    for g in range(2):
                        if l == 0:
                            eng.wait_ge(S("masked"), i * NH + (4 * g + 4))
                            eng.wait_ge(S("wkv_scaled"), i * 4 + 4)
                        else:
                            eng.wait_ge(S(f"carry_done{g}"), i * LEVELS + l)
                            if l == 1:
                                eng.wait_ge(S(f"inv_made{g}"), i * 11 + 2)
                        eng.tensor_tensor(em[g][:], scores[:, 4 * g:4 * g + 4, 0],
                                          bcast(cc("level", P, l * P), 4),
                                          ALU.mult).then_inc(S(f"mask_made{g}"), 1)
                for c in range(2):
                    eng.wait_ge(S("state_made"), i * 2 + (c + 1))
                    if c == 0:
                        eng.wait_ge(S("decays"), i * 3 + 3)
                    eng.tensor_tensor(end_w[:], bcast(cc("pair"), HP), each(e_in[:, :, c * CH + CH - 1], P),
                                      ALU.mult).then_inc(S("end_made"), 1)

        def dve_self_scores(eng):
            c = dve_steps
            eng.wait_ge(S("self_scored"), 1)
            for g in range(2):
                own = cc("own_rows", NB, g * NB)
                eng.tensor_tensor(own_self[:, g], psum[:, 7, g * TS:(g + 1) * TS].rearrange("p (b t) -> p b t", t=DS),
                                  each(own, DS), ALU.mult).then_inc(S("self_read"), 1)
                eng.wait_ge(S("self_read"), g + 1)
                c.up(eng.tensor_reduce(self4[:], own_self[:, g].rearrange("p b t -> p t b"), AX.X, ALU.add))
                c.wait(eng)
                for t in range(DS):
                    c.up(eng.tensor_scalar(zp[:, g, DS - 1 - t:DS - t], self4[:, t:t + 1], SCALE,
                                           vec("sb_bias_rows", 0), ALU.mult, ALU.add))
                c.wait(eng)
            eng.sem_inc(S("z_read"), 1)

        def dve_wkv(eng):
            dve_self_scores(eng)
            eng.wait_ge(S("masks_loaded"), 16)
            with eng.Fori(0, NT) as i:
                cols = bass.ds(i * P, P)
                eng.wait_ge(S("decays"), i * 3 + 3)
                eng.tensor_tensor(ar[:, :, 1], proj[:, 0:4, cols], e_in[:], ALU.mult).then_inc(S("wkv_scaled"), 1)
                eng.scalar_tensor_tensor(ar[:, :, 0], kk[:, :, cols], -1.0, e_ex[:], ALU.mult, ALU.mult)\
                   .then_inc(S("wkv_scaled"), 1)
                eng.tensor_tensor(bk[:, 0], a_b[:, :, cols], e_inv[:], ALU.mult).then_inc(S("wkv_scaled"), 1)
                eng.tensor_tensor(bk[:, 1], proj[:, 4:8, cols], e_inv[:], ALU.mult).then_inc(S("wkv_scaled"), 1)
                for h in range(NH):
                    eng.wait_ge(S("scored"), i * NH + (h + 1))
                    bank = h % 4
                    eng.tensor_tensor(scores[:, h].rearrange("p (x y) n -> p x (y n)", x=2),
                                      psum[:, bank, :].rearrange("p (x n) -> p x n", x=2),
                                      bcast(cc("score", 2 * P), 2), ALU.mult).then_inc(S("masked"), 1)
                ident = bcast(cc("ident"), 4)
                for g in range(2):
                    eng.wait_ge(S(f"mask_made{g}"), i * LEVELS + 1)
                    eng.tensor_tensor(dt[g][:], em[g][:], ident, ALU.add).then_inc(S(f"inv_made{g}"), 1)
                    eng.wait_ge(S(f"carry_done{g}"), i * LEVELS + 1)
                    eng.tensor_tensor(dm[g][:], psum[:, 3 * g, :].rearrange("p (h n) -> p h n", h=4), ident,
                                      ALU.add).then_inc(S(f"inv_made{g}"), 1)
                for l in range(1, LEVELS):
                    for g in range(2):
                        eng.wait_ge(S(f"grown{g}"), i * (LEVELS - 1) + l)
                        eng.wait_ge(S(f"inv_made{g}"), i * 11 + 2 * l)
                        if l < LEVELS - 1:
                            eng.tensor_tensor(dm[g][:], psum[:, 3 * g + 1, :].rearrange("p (h n) -> p h n", h=4),
                                              dm[g][:], ALU.add).then_inc(S(f"inv_made{g}"), 1)
                        eng.tensor_tensor(dt[g][:], psum[:, 3 * g + 2, :].rearrange("p (h n) -> p h n", h=4),
                                          dt[g][:], ALU.add).then_inc(S(f"inv_made{g}"), 1)
                for n in range(2):
                    eng.wait_ge(S(f"k_pages_used{n}"), i * 2 + 3)
                eng.tensor_scalar(zp[:, :, bass.ds(i * 256 + DS, 256)], psum[:, 7, :].rearrange("p (g n) -> p g n", g=2),
                                  SCALE, vec("sb_bias_rows", 0), ALU.mult, ALU.add).then_inc(S("z_read"), 1)
                for c in range(2):
                    eng.wait_ge(S("update_done"), i * 2 + (c + 1))
                    eng.tensor_tensor(tmp_s[:], psum[:, 1 + c, :].rearrange("p (h n) -> p h n", h=HP), state[:],
                                      ALU.add).then_inc(S("state_summed"), 1)
                    eng.wait_ge(S("state_summed"), i * 2 + (c + 1))
                    eng.wait_ge(S("end_made"), i * 2 + (c + 1))
                    eng.tensor_tensor(state[:], tmp_s[:], end_w[:], ALU.mult).then_inc(S("state_made"), 1)

        def pe_k_unit(eng, i, n):
            if n == 0:
                eng.wait_ge(S("z_read"), i + 1)
            eng.wait_ge(S(f"k_pages_loaded{n % 2}"), i * 128 + 64 * (n // 2 + 1))
            for b in (2 * n, 2 * n + 1):
                g, rows = b // 4, slice(b % 4 * 32, b % 4 * 32 + 32)
                for hp in range(HP):
                    mm = eng.matmul(psum[rows, 7, g * 256:(g + 1) * 256], qb[:, hp, b].rearrange("p h t -> p (h t)"),
                                    k_pages[n % 2][:, b % 2, hp], start=g == 0 and hp == 0, stop=hp == HP - 1,
                                    skip_group_check=True)
            mm.then_inc(S(f"k_pages_used{n % 2}"), 1)

        def pe_self_scores(eng):
            eng.wait_ge(S("qb_made"), 9)
            for s in range(2):
                eng.wait_ge(S(f"qk_made{s}"), 3)
            for g in range(2):
                for hp in range(HP):
                    mm = eng.matmul(psum[:, 7, g * TS:(g + 1) * TS],
                                    qb[:, hp, 4 * g:4 * g + 4].rearrange("p b h t -> p (b h t)"),
                                    proj[:, 16 + hp, SEQ:T], start=g == 0 and hp == 0, stop=hp == HP - 1,
                                    skip_group_check=True)
            mm.then_inc(S("self_scored"), 1)

        def pe_wkv(eng):
            pe_self_scores(eng)
            eng.wait_ge(S("prep_done"), 1)
            with eng.Fori(0, NT) as i:
                eng.wait_ge(S("wkv_scaled"), i * 4 + 4)
                eng.wait_ge(S("y_made"), i + 1)
                eng.wait_ge(S("state_made"), i * 2 + 1)
                for h in range(NH):
                    bank = h % 4
                    if h >= 4:
                        eng.wait_ge(S("masked"), i * NH + (h - 3))
                    r = par_rows(h)
                    rhs = ar[r, h // 2].rearrange("p x n -> p (x n)")
                    eng.matmul(psum[:, bank, 0:256], bk[r, 0, h // 2], rhs, start=True, stop=True,
                               skip_group_check=True)
                    eng.matmul(psum[:, bank, 256:512], bk[r, 1, h // 2], rhs, start=False, stop=True,
                               skip_group_check=True).then_inc(S("scored"), 1)
                pe_k_unit(eng, i, 0)
                eng.wait_ge(S("v_copied"), i + 1)
                for q, a in enumerate((vf, bk[:, 0], bk[:, 1])):
                    for hp in range(HP):
                        mm = eng.transpose(psum[:, 4 + q, hp * P:(hp + 1) * P], a[:, hp], cc("ident"))
                    mm.then_inc(S("turned"), 1)
                for g in range(2):
                    eng.wait_ge(S(f"mask_made{g}"), i * LEVELS + 1)
                    eng.wait_ge(S("masked"), i * NH + NH)
                    for j in range(4):
                        mm = eng.matmul(psum[:, 3 * g, j * P:(j + 1) * P], em[g][:, j], cc("ident"),
                                        start=j == 0, stop=True, skip_group_check=True)
                    mm.then_inc(S(f"carry_done{g}"), 1)
                eng.wait_ge(S("tok_made"), i * 3 + 3)
                for l in range(1, LEVELS):
                    if l in (1, 2, 3):
                        pe_k_unit(eng, i, l)
                    for g in range(2):
                        eng.wait_ge(S(f"mask_made{g}"), i * LEVELS + (l + 1))
                        eng.wait_ge(S(f"inv_made{g}"), i * 11 + 2 * l)
                        for j in range(4):
                            mm = eng.matmul(psum[:, 3 * g, j * P:(j + 1) * P], em[g][:, j], dm[g][:, j],
                                            start=j == 0, stop=True, skip_group_check=True)
                        mm.then_inc(S(f"carry_done{g}"), 1)
                    for g in range(2):
                        eng.wait_ge(S(f"carry_made{g}"), i * (LEVELS - 1) + l)
                        if l < LEVELS - 1:
                            for j in range(4):
                                eng.matmul(psum[:, 3 * g + 1, j * P:(j + 1) * P], dt[g][:, j], wm[g][:, j],
                                           start=j == 0, stop=True, skip_group_check=True)
                        for j in range(4):
                            mm = eng.matmul(psum[:, 3 * g + 2, j * P:(j + 1) * P], wm[g][:, j], dt[g][:, j],
                                            start=j == 0, stop=True, skip_group_check=True)
                        mm.then_inc(S(f"grown{g}"), 1)
                for g in range(2):
                    eng.wait_ge(S(f"inv_made{g}"), i * 11 + 11)
                for c in range(2):
                    cr = c_rows(c)
                    eng.wait_ge(S("state_made"), i * 2 + (c + 1))
                    for hp in range(HP):
                        eng.matmul(psum[cr, 6, hp * P:(hp + 1) * P], ar[:, hp, 0, cr], state[:, hp],
                                   start=hp == 0, stop=False, skip_group_check=True)
                    for h in range(NH):
                        n = slice(h * HD, (h + 1) * HD)
                        mm = eng.matmul(psum[cr, 6, n], scores[:, h, 2, cr], tok[:, 0, n],
                                        start=False, stop=True, skip_group_check=True)
                    mm.then_inc(S("rhs_done"), 1)
                    for hp in range(HP):
                        eng.matmul(psum[:, 0, hp * P + c * CH:hp * P + (c + 1) * CH], state[:, hp],
                                   ar[:, hp, 1, cr], start=c == 0 and hp == 0, stop=False, skip_group_check=True)
                    eng.wait_ge(S("rhs_made"), i * 2 + (c + 1))
                    for h in range(NH):
                        mm = eng.matmul(psum[cr, 3, h * HD:(h + 1) * HD], dt[h // 4][:, h % 4, cr],
                                        xs[:].rearrange("p h n -> p (h n)")[:, h * HD:(h + 1) * HD],
                                        start=h == 0, stop=True, skip_group_check=True)
                    mm.then_inc(S("sa_done"), 1)
                    eng.wait_ge(S("sa_made"), i * 2 + (c + 1))
                    for hp in range(HP):
                        n = slice(hp * P, (hp + 1) * P)
                        eng.matmul(psum[:, 1 + c, n], tok[cr, 1, n], sas[:].rearrange("p h n -> p (h n)")[cr, n],
                                   start=hp == 0, stop=False, skip_group_check=True)
                        mm = eng.matmul(psum[:, 1 + c, n], tok[cr, 2, n], tok[cr, 0, n],
                                        start=False, stop=True, skip_group_check=True)
                    mm.then_inc(S("update_done"), 1)
                for h in range(NH):
                    out = psum[par_rows(h), 0, h // 2 * P:(h // 2 + 1) * P]
                    n = slice(h * HD, (h + 1) * HD)
                    eng.matmul(out, sas[:].rearrange("p h n -> p (h n)")[:, n], scores[:, h, 1],
                               start=False, stop=False, skip_group_check=True)
                    mm = eng.matmul(out, tok[:, 0, n], scores[:, h, 3], start=False, stop=True,
                                    skip_group_check=True)
                mm.then_inc(S("y_done"), 1)
        arf = ar[:].rearrange("p a b n -> p (a b n)")
        bkf = bk[:].rearrange("p a b n -> p (a b n)")
        tokf = tok[:].rearrange("p a n -> p (a n)")
        xsf, sasf = (t[:].rearrange("p h n -> p (h n)") for t in (xs, sas))
        y_tok = wm[1][:].rearrange("p h n -> p (h n)")[:, 0:P]
        s_cols = slice(SEQ, T)
        last = 2 * NT + 1

        def act_wkv_s(eng):
            eng.wait_ge(S("state_made"), last)
            for dst, src, sc in ((e_in_s[:], logp, 1.0), (e_ex[:, :, 0:TS], ldec, 1.0), (e_inv[:, :, 0:TS], logp, -1.0)):
                eng.activation(dst, src[:, :, s_cols], ACT.Exp, scale=sc).then_inc(S("decays"), 1)
            eng.wait_ge(S("z_read"), NT + 1)
            eng.wait_ge(S("y_made"), NT + 1)
            eng.activation(cp[:], zp[:], ACT.Relu).then_inc(S("soft_p"), 1)
            eng.activation(lp[:], zp[:], ACT.Abs).then_inc(S("soft_p"), 1)
            eng.wait_ge(S("soft_p"), 2)
            eng.activation(lp[:], lp[:], ACT.Exp, scale=-1.0).then_inc(S("soft_p"), 1)
            eng.wait_ge(S("soft_p"), 3)
            eng.activation(lp[:], lp[:], ACT.Ln, bias=1.0).then_inc(S("soft_p"), 1)
            eng.wait_ge(*step("s_turned", 1))
            eng.activation(tokf[:, 0:3 * P], psum[:, 4, 0:3 * P], ACT.Copy).then_inc(S("s_tok"), 1)
            eng.wait_ge(*step("s_carry", 2))
            eng.activation(wm[0][:, 0:2].rearrange("p h n -> p (h n)"), psum[:, 5, 0:2 * P], ACT.Copy)\
               .then_inc(S("s_carry_made"), 1)
            eng.wait_ge(*step("s_sa", 1))
            eng.activation(sasf[:, 0:P], psum[:, 1, 0:P], ACT.Copy).then_inc(S("s_sa_made"), 1)
            eng.wait_ge(*step("s_y_turned", 1))
            eng.activation(kk[:, :, s_cols], psum[:, 1, 2 * P:3 * P].rearrange("p (h n) -> p h n", h=HP), ACT.Copy)\
               .then_inc(S("y_made"), 1)

        def pool_wkv_s(eng):
            eng.wait_ge(S("state_made"), last)
            eng.tensor_copy(vf[:].rearrange("p h n -> p (h n)")[:, 0:P].rearrange("p (h n) -> p h n", h=HP),
                            proj[:, 8:12, s_cols]).then_inc(S("s_v_copied"), 1)
            eng.wait_ge(*step("s_masked", 2))
            eng.wait_ge(*step("s_scaled", 4))
            for l in range(2):
                if l:
                    eng.wait_ge(*step("s_carry", 1))
                    eng.wait_ge(*step("s_inv", 2))
                eng.tensor_tensor(em[0][:, 0:2], scores[:, 0:2, 0],
                                  bcast(cc("level", P, l * P), 2),
                                  ALU.mult).then_inc(S("s_mask_made"), 1)

            eng.wait_ge(S("soft_p"), 4)
            eng.tensor_tensor(lp[:], lp[:], cp[:], ALU.add).then_inc(S("soft_p_made"), 1)
            eng.wait_ge(S("soft_p_made"), 1)
            eng.tensor_tensor(lp[:, :, 0:DS], lp[:, :, 0:DS], bcast(cc("self", DS), 2), ALU.mult)\
               .then_inc(S("soft_p_made"), 1)
            eng.wait_ge(S("sums_p"), 2)
            eng.tensor_tensor(zp[:], zp[:], cp[:], ALU.subtract).then_inc(S("soft_p_made"), 1)

        def dve_wkv_s(eng):
            r4 = lambda a: a.rearrange("p (h n) -> p h n", h=HP)
            eng.wait_ge(S("decays"), 3 * NT + 3)
            eng.scalar_tensor_tensor(r4(arf[:, 0:P]), kk[:, :, s_cols], -1.0, e_ex[:, :, 0:TS], ALU.mult, ALU.mult)\
               .then_inc(S("s_scaled"), 1)
            eng.tensor_tensor(r4(arf[:, P:2 * P]), proj[:, 0:4, s_cols], e_in_s[:], ALU.mult).then_inc(S("s_scaled"), 1)
            eng.tensor_tensor(r4(bkf[:, 0:P]), a_b[:, :, s_cols], e_inv[:, :, 0:TS], ALU.mult).then_inc(S("s_scaled"), 1)
            eng.tensor_tensor(r4(bkf[:, P:2 * P]), proj[:, 4:8, s_cols], e_inv[:, :, 0:TS], ALU.mult)\
               .then_inc(S("s_scaled"), 1)
            for pr in range(2):
                eng.wait_ge(*step("s_scored", pr + 1))
                eng.tensor_tensor(scores[:, pr].rearrange("p (x y) n -> p x (y n)", x=2),
                                  psum[:, pr, :].rearrange("p (x n) -> p x n", x=2),
                                  bcast(cc("score_s", 2 * P), 2), ALU.mult).then_inc(S("s_masked"), 1)
            ident = bcast(cc("ident"), 2)
            two = lambda a: a.rearrange("p (h n) -> p h n", h=2)
            eng.wait_ge(*step("s_mask_made", 1))
            eng.tensor_tensor(dt[0][:, 0:2], em[0][:, 0:2], ident, ALU.add).then_inc(S("s_inv"), 1)
            eng.wait_ge(*step("s_carry", 1))
            eng.tensor_tensor(dm[0][:, 0:2], two(psum[:, 5, 0:2 * P]), ident, ALU.add).then_inc(S("s_inv"), 1)
            c = dve_steps
            eng.wait_ge(*step("s_with_state", 1))
            own = each(cc("own", NB), HD)
            for kind, bank in ((0, 2), (1, 6)):
                for pr in range(2):
                    c.up(eng.tensor_tensor(own_x[:, pr], psum[:, bank + pr, :].rearrange("p (b i) -> p b i", b=NB),
                                           own, ALU.mult))
                    c.wait(eng)
                    c.up(eng.tensor_reduce(x_red[:, kind, pr], own_x[:, pr].rearrange("p b i -> p i b"), AX.X, ALU.add))
                    c.wait(eng)
            eng.wait_ge(*step("s_grown", 1))
            eng.tensor_tensor(dt[0][:, 0:2], two(psum[:, 5, 2 * P:4 * P]), dt[0][:, 0:2], ALU.add).then_inc(S("s_inv"), 1)
            eng.wait_ge(*step("s_ak", 1))
            eng.tensor_tensor(xsf[:, 0:P], psum[:, 0, 0:P], x_red[:, 0].rearrange("p a n -> p (a n)"), ALU.add)\
               .then_inc(S("s_rhs"), 1)
            eng.wait_ge(*step("s_tok", 1))
            for pr in range(2):
                eng.tensor_tensor(own_v[:, pr], bcast(tokf[:, pr * HD:(pr + 1) * HD], NB), own, ALU.mult)\
                   .then_inc(S("s_expanded"), 1)
            eng.wait_ge(*step("s_sa_made", 1))
            for pr in range(2):
                eng.tensor_tensor(own_x[:, pr], bcast(sasf[:, pr * HD:(pr + 1) * HD], NB), own, ALU.mult)\
                   .then_inc(S("s_expanded"), 1)
            eng.wait_ge(S("soft_p_made"), 2)
            for g in range(2):
                eng.tensor_tensor_scan(cp[:, g], cc("ones", 1).broadcast_to([P, PAST + DS]),
                                       lp[:, g], 0.0, ALU.mult, ALU.add).then_inc(S("sums_p"), 1)
            eng.wait_ge(*step("s_y", 1))
            eng.tensor_tensor(y_tok, psum[:, 0, P:2 * P], x_red[:, 1].rearrange("p a n -> p (a n)"), ALU.add)\
               .then_inc(S("s_y_summed"), 1)
            eng.wait_ge(*step("s_update", 1))
            for hp in range(HP):
                eng.tensor_tensor(state_s[:, hp].rearrange("p b i -> p (b i)"), psum[:, 4 + hp, :],
                                  state_s[:, hp].rearrange("p b i -> p (b i)"), ALU.add).then_inc(S("s_state"), 1)
            eng.wait_ge(*step("s_state", HP))
            for hp in range(HP):
                eng.tensor_tensor(state_s[:, hp], state_s[:, hp], each(samples(e_in_s[:, hp])[:, :, DS - 1], HD),
                                  ALU.mult).then_inc(S("s_state"), 1)

        def pe_wkv_s(eng):
            k = dict(skip_group_check=True)
            eng.wait_ge(*step("s_scaled", 4))
            eng.wait_ge(S("y_made"), NT + 1)
            for pr in range(2):
                r = par_rows(pr)
                eng.matmul(psum[:, pr, 0:256], bkf[r, 0:P], arf[r, 0:2 * P], start=True, stop=True, **k)
                eng.matmul(psum[:, pr, 256:512], bkf[r, P:2 * P], arf[r, 0:2 * P], start=False, stop=True, **k)\
                   .then_inc(S("s_scored"), 1)
            eng.wait_ge(*step("s_v_copied", 1))
            for q, a in enumerate((vf[:].rearrange("p h n -> p (h n)")[:, 0:P], bkf[:, 0:P], bkf[:, P:2 * P])):
                mm = eng.transpose(psum[:, 4, q * P:(q + 1) * P], a, cc("ident"))
            mm.then_inc(S("s_turned"), 1)
            eng.wait_ge(S("state_loaded"), 16)
            for at, bank in ((0, 2), (P, 6)):
                for pr in range(2):
                    r = par_rows(pr)
                    for hp in range(HP):
                        rows = slice(hp * TS, (hp + 1) * TS)
                        mm = eng.matmul(psum[rows, bank + pr, :], arf[r, at + hp * TS:at + (hp + 1) * TS],
                                        state_s[r, hp].rearrange("p b i -> p (b i)"), start=True, stop=True, **k)
            mm.then_inc(S("s_with_state"), 1)
            eng.wait_ge(*step("s_mask_made", 1))
            for pr in range(2):
                mm = eng.matmul(psum[:, 5, pr * P:(pr + 1) * P], em[0][:, pr], cc("ident"), start=pr == 0, stop=True, **k)
            mm.then_inc(S("s_carry"), 1)
            eng.wait_ge(*step("s_mask_made", 2))
            eng.wait_ge(*step("s_inv", 2))
            for pr in range(2):
                mm = eng.matmul(psum[:, 5, pr * P:(pr + 1) * P], em[0][:, pr], dm[0][:, pr], start=pr == 0, stop=True, **k)
            mm.then_inc(S("s_carry"), 1)
            eng.wait_ge(*step("s_carry_made", 1))
            for pr in range(2):
                mm = eng.matmul(psum[:, 5, (2 + pr) * P:(3 + pr) * P], wm[0][:, pr], dt[0][:, pr],
                                start=pr == 0, stop=True, **k)
            mm.then_inc(S("s_grown"), 1)
            eng.wait_ge(*step("s_tok", 1))
            eng.wait_ge(*step("s_masked", 2))
            for pr in range(2):
                n = slice(pr * HD, (pr + 1) * HD)
                mm = eng.matmul(psum[:, 0, n], scores[:, pr, 2], tokf[:, n], start=pr == 0, stop=True, **k)
            mm.then_inc(S("s_ak"), 1)
            eng.wait_ge(*step("s_rhs", 1))
            eng.wait_ge(*step("s_inv", 3))
            for pr in range(2):
                n = slice(pr * HD, (pr + 1) * HD)
                mm = eng.matmul(psum[:, 1, n], dt[0][:, pr], xsf[:, n], start=pr == 0, stop=True, **k)
            mm.then_inc(S("s_sa"), 1)
            eng.wait_ge(*step("s_sa_made", 1))
            for pr in range(2):
                n, o = slice(pr * HD, (pr + 1) * HD), slice(P + pr * HD, P + (pr + 1) * HD)
                eng.matmul(psum[:, 0, o], scores[:, pr, 1], sasf[:, n], start=pr == 0, stop=False, **k)
                mm = eng.matmul(psum[:, 0, o], scores[:, pr, 3], tokf[:, n], start=False, stop=True, **k)
            mm.then_inc(S("s_y"), 1)
            eng.wait_ge(*step("s_expanded", 4))
            for hp in range(HP):
                rows = slice(hp * TS, (hp + 1) * TS)
                for pr in range(2):
                    out = psum[par_rows(pr), 4 + hp, :]
                    b = slice(P + pr * HD, P + (pr + 1) * HD)
                    kc = slice(2 * P + pr * HD, 2 * P + (pr + 1) * HD)
                    eng.matmul(out, tokf[rows, b], own_x[rows, pr].rearrange("p b i -> p (b i)"),
                               start=True, stop=False, **k)
                    mm = eng.matmul(out, tokf[rows, kc], own_v[rows, pr].rearrange("p b i -> p (b i)"),
                                    start=False, stop=True, **k)
            mm.then_inc(S("s_update"), 1)
            eng.wait_ge(*step("s_y_summed", 1))
            eng.transpose(psum[:, 1, 2 * P:3 * P], y_tok, cc("ident")).then_inc(S("s_y_turned"), 1)

        def pe_heads(eng):
            eng.wait_ge(S("y_made"), NT + 2)
            eng.wait_ge(*step("s_state", 2 * HP))
            def pair(bank, a):
                for h in range(2):
                    mm = eng.matmul(psum[:, bank + h, 0:HALF], cc("pair"), a[:, h * HALF:(h + 1) * HALF],
                                    start=True, stop=True)
                return mm
            for f in range(HP):
                if f >= 2:
                    eng.wait_ge(*step("y_centred", f - 1))
                pair(2 * (f % 2), kk[:, f]).then_inc(S("y_mean"), 1)
                eng.wait_ge(*step("rk_made", f + 1))
                if f:
                    eng.wait_ge(*step("bonus_made", f))
                pair(6, t3[:, f]).then_inc(S("rk_summed"), 1)
                eng.wait_ge(*step("y_squared", f + 1))
                if f:
                    eng.wait_ge(*step("y_std", f))
                pair(4, t1[:, f]).then_inc(S("y_var"), 1)

        def act_heads(eng):
            for f in range(HP):
                eng.wait_ge(*step("y_centred", f + 1))
                eng.activation(t1[:, f], kk[:, f], ACT.Square).then_inc(S("y_squared"), 1)
                eng.wait_ge(*step("y_var", f + 1))
                eng.activation(halves(t2[:, f]), two_halves(4), ACT.Sqrt, bias=eps[:, 1:2], scale=1.0 / HD)\
                   .then_inc(S("y_std"), 1)
                eng.wait_ge(*step("o_a_made", f + 1))
                eng.wait_ge(S("soft_p_made"), 3)
                eng.activation(xh[:, f, 0:T], kk[:, f], ACT.Copy).then_inc(S("o_a_hi"), 1)

        def dve_heads(eng):
            c = dve_steps
            eng.wait_ge(S("states_stored"), 32)
            eng.wait_ge(S("y_made"), NT + 2)
            for f in range(HP):
                eng.scalar_tensor_tensor(t3[:, f], proj[:, f, 0:T], vec("r_k", f), proj[:, 4 + f, 0:T],
                                         ALU.mult, ALU.mult).then_inc(S("rk_made"), 1)
                eng.wait_ge(*step("y_mean", f + 1))
                eng.scalar_tensor_tensor(halves(kk[:, f]), two_halves(2 * (f % 2)), -1.0 / HD, halves(kk[:, f]),
                                         ALU.mult, ALU.add).then_inc(S("y_centred"), 1)
                eng.wait_ge(*step("rk_summed", f + 1))
                eng.tensor_tensor(halves(t3[:, f]), two_halves(6), halves(proj[:, 8 + f, 0:T]), ALU.mult)\
                   .then_inc(S("bonus_made"), 1)
                eng.wait_ge(*step("y_std", f + 1))
                c.up(eng.reciprocal(t4[:, f], t2[:, f]))
                c.wait(eng)
                eng.wait_ge(*step("y_centred", f + 1))
                eng.wait_ge(*step("y_squared", f + 1))
                c.up(eng.scalar_tensor_tensor(kk[:, f], kk[:, f], vec("lnx_g", f), t4[:, f], ALU.mult, ALU.mult))
                c.wait(eng)
                eng.wait_ge(*step("bonus_made", f + 1))
                c.up(eng.scalar_tensor_tensor(kk[:, f], kk[:, f], vec("lnx_b", f), t3[:, f], ALU.add, ALU.add))
                c.wait(eng)
                eng.tensor_tensor(kk[:, f], kk[:, f], g_out[:, f], ALU.mult).then_inc(S("o_a_made"), 1)
            for f in range(HP):
                eng.wait_ge(*step("o_a_hi", f + 1))
                eng.tensor_tensor(xl[:, f, 0:T], kk[:, f], xh[:, f, 0:T].bitcast(F32), ALU.subtract)\
                   .then_inc(S("o_a_lo"), 1)

        OFF = {0: 4 * P, 2: 7 * P, 1: 8 * P}
        flat = psum[:].rearrange("p b n -> p (b n)")
        C_AT = 3 * 512

        def pe_scores(eng, h):
            if h:
                eng.wait_ge(S("z_made"), h)
            r, hp = par_rows(h), h // 2
            q, key = proj[r, 12 + hp], proj[r, 16 + hp]
            for kt in range(NT):
                mm = eng.matmul(flat[:, kt * P:(kt + 1) * P], key[:, kt * P:(kt + 1) * P], q[:, kt * P:(kt + 1) * P],
                                start=kt == 0, stop=True, skip_group_check=True)
            for n, kt in enumerate((0, 2, 1)):
                w = SEQ - (kt + 1) * P
                mm = eng.matmul(flat[:, OFF[kt]:OFF[kt] + w], key[:, kt * P:(kt + 1) * P], q[:, (kt + 1) * P:SEQ],
                                start=kt != 2, stop=True, skip_group_check=True)
            mm.then_inc(S("z_done"), 1)

        def pe_sums(eng, h):
            l = ls[h % 2]
            eng.wait_ge(S("soft_masked"), h + 1)
            if h:
                eng.wait_ge(S("exponents"), h)
            def add(at, src, n, first=False):
                return eng.matmul(flat[:, C_AT + at:C_AT + at + n], cc("suffix") if first else cc("ones"),
                                  l[:, src:src + n], start=first, stop=not first, skip_group_check=True)
            add(0, 0, 512, True)
            add(4 * P, 4 * P, 512, True)
            add(8 * P, 8 * P, 256, True)
            add(4 * P, P, P)
            add(5 * P, 8 * P, 2 * P)
            add(5 * P, 2 * P, 2 * P)
            add(6 * P, 7 * P, P)
            add(7 * P, 3 * P, P)
            add(8 * P, 2 * P, 2 * P)
            add(9 * P, 7 * P, P).then_inc(S("sums_done"), 1)

        def pe_values(eng, h):
            a, hp = zs[h % 2], h // 2
            eng.wait_ge(S("weights_made"), h + 1)
            if h % 2 == 0 and hp:
                eng.wait_ge(S("o_b_read"), 2 * hp)
            out = psum[par_rows(h), 6, :]
            v = lambda kt: vt[:, kt, h * HD:(h + 1) * HD]
            for kt in range(NT):
                eng.matmul(out[:, kt * P:(kt + 1) * P], v(kt), a[:, kt * P:(kt + 1) * P],
                           start=kt == 0, stop=False, skip_group_check=True)
            for kt in range(NT - 1):
                w = SEQ - (kt + 1) * P
                mm = eng.matmul(out[:, (kt + 1) * P:SEQ], v(kt), a[:, OFF[kt]:OFF[kt] + w],
                                start=False, stop=kt == NT - 2, skip_group_check=True)
            mm.then_inc(S("values_done"), 1)

        def pe_stick(eng):
            eng.wait_ge(*step("o_a_lo", HP))
            eng.wait_ge(S("v_made"), 2)
            pe_scores(eng, 0)
            for h in range(NH + 1):
                if h + 1 < NH:
                    pe_scores(eng, h + 1)
                pe_samples(eng, h, "a")
                if h < NH:
                    pe_sums(eng, h)
                pe_samples(eng, h, "b")
                if h:
                    pe_values(eng, h - 1)
                pe_samples(eng, h, "c")

        def act_stick(eng):
            def soft(h):
                l = ls[h % 2]
                eng.wait_ge(S("z_made"), h + 1)
                if h >= 2:
                    eng.wait_ge(S("sums_done"), h - 1)
                eng.activation(l[:], zs[h % 2][:], ACT.Abs).then_inc(S("soft"), 1)
                eng.wait_ge(S("soft"), 3 * h + 1)
                eng.activation(l[:], l[:], ACT.Exp, scale=-1.0).then_inc(S("soft"), 1)
                eng.wait_ge(S("soft"), 3 * h + 2)
                eng.activation(l[:], l[:], ACT.Ln, bias=1.0).then_inc(S("soft"), 1)

            def weights(h):
                eng.wait_ge(S("exponents_masked"), h + 1)
                eng.activation(zs[h % 2][:], zs[h % 2][:], ACT.Exp).then_inc(S("weights_made"), 1)

            def output(hp):
                eng.wait_ge(S("values_done"), 2 * hp + 2)
                if hp >= 2:
                    eng.wait_ge(S("o_b_lo"), hp - 1)
                eng.activation(ob[hp % 2][:], psum[:, 6, :], ACT.Copy).then_inc(S("o_b_read"), 1)
                eng.activation(xh[:, HP + hp, 0:SEQ], psum[:, 6, :], ACT.Copy).then_inc(S("o_b_read"), 1)

            act_samples(eng, -1)
            soft(0)
            for h in range(NH):
                act_samples(eng, h, "start")
                if h + 1 < NH:
                    soft(h + 1)
                act_samples(eng, h, "mid")
                weights(h)
                if h >= 2 and h % 2 == 0:
                    output(h // 2 - 1)
            output(HP - 1)

        def dve_stick(eng):
            def scaled(h):
                eng.wait_ge(S("z_done"), h + 1)
                if h >= 2:
                    eng.wait_ge(S("values_done"), h - 1)
                eng.tensor_scalar(zs[h % 2][:], flat[:, 0:10 * P], SCALE, vec("sb_bias", h), ALU.mult, ALU.add)\
                   .then_inc(S("z_made"), 1)

            def soft(h):
                eng.wait_ge(S("soft"), 3 * h + 3)
                eng.scalar_tensor_tensor(ls[h % 2][:], zs[h % 2][:], 0.0, ls[h % 2][:], ALU.max, ALU.add)\
                   .then_inc(S("soft_made"), 1)

            def exponents(h):
                eng.wait_ge(S("sums_done"), h + 1)
                eng.tensor_tensor(zs[h % 2][:], zs[h % 2][:], flat[:, C_AT:C_AT + 10 * P], ALU.subtract)\
                   .then_inc(S("exponents"), 1)

            dve_samples(eng, -1)
            scaled(0)
            soft(0)
            for h in range(NH):
                dve_samples(eng, h, "start")
                if h + 1 < NH:
                    scaled(h + 1)
                dve_samples(eng, h, "mid")
                exponents(h)
                if h + 1 < NH:
                    soft(h + 1)

        def pool_stick(eng):
            def select(a, fill):
                b = a[:, 0:4 * P].rearrange("p (k n) -> p k n", k=4)
                return eng.affine_select(out=b, in_=b, compare_op=ALU.is_gt, fill=fill, base=0,
                                         pattern=[[0, 4], [1, P]], channel_multiplier=-1)
            def soft(h):
                eng.wait_ge(S("soft_made"), h + 1)
                select(ls[h % 2], 0.0).then_inc(S("soft_masked"), 1)
            def low(hp):
                eng.wait_ge(S("o_b_read"), 2 * hp + 2)
                eng.tensor_tensor(xl[:, HP + hp, 0:SEQ], ob[hp % 2][:], xh[:, HP + hp, 0:SEQ].bitcast(F32),
                                  ALU.subtract).then_inc(S("o_b_lo"), 1)

            def h_low(q):
                eng.wait_ge(S("hh_made"), q + 1)
                two = slice(2 * q, 2 * q + 2)
                eng.tensor_tensor(hl[:, two], y[:, two], hh[:, two].bitcast(F32), ALU.subtract).then_inc(S("hl_made"), 1)

            soft(0)
            for h in range(NH):
                eng.wait_ge(S("exponents"), h + 1)
                select(zs[h % 2], MASKED).then_inc(S("exponents_masked"), 1)
                if h + 1 < NH:
                    soft(h + 1)
                if h >= 3 and h % 2 == 1:
                    low(h // 2 - 1)
                for q in {5: (0,), 6: (1, 2), 7: (3,)}.get(h, ()):
                    h_low(q)
            low(HP - 1)

        def page_registers(eng, places):
            return [eng.value_load(page_of[:, bass.ds(at, 1)], min_val=0, max_val=N_PHYS - 1) for at in places]

        def sp_k_pages(eng, io):
            eng.wait_ge(S("page_table_loaded"), 16)
            wait_w_in(eng)
            with eng.Fori(0, NT) as i:
                for n in range(4):
                    regs = page_registers(eng, [i * -2 + ((2 * n + b) * N_PAGES + N_PAGES - 1 - p)
                                                for b in range(2) for p in range(2)])
                    for q, reg in enumerate(regs):
                        if q == 0:
                            eng.wait_ge(S(f"k_pages_used{n % 2}"), i * 2 + (n // 2 + 1))
                        eng.dma_start(k_pages[n % 2][:, q // 2, :, q % 2 * PAGE:(q % 2 + 1) * PAGE],
                                      io["cache_k"][bass.ds(reg, 1)].rearrange("a p h n -> (a p) h n"))\
                           .then_inc(S(f"k_pages_loaded{n % 2}"), 16)

        def sp_v_pages(eng, io):
            eng.wait_ge(*step("o_a_lo", HP))
            with eng.Fori(0, NB // 2) as i:
                for j in range(4):
                    regs = page_registers(eng, [i * (2 * N_PAGES) + (j // 2 * N_PAGES + N_PAGES - 1 - (j % 2 * 4 + p))
                                                for p in range(4)])
                    for p, reg in enumerate(regs):
                        if p == 0:
                            eng.wait_ge(S(f"pages_used{j}"), i + 1)
                        eng.dma_start(pages[j][:, p], io["cache_v"][bass.ds(reg, 1)].rearrange("a p n -> (a p) n"))\
                           .then_inc(S(f"pages_loaded{j}"), 16)

        def dve_qb(eng):
            for s in range(2):
                eng.wait_ge(S(f"qk_made{s}"), 3)
            eng.memset(qb[:], 0.0).then_inc(S("qb_made"), 1)
            eng.wait_ge(S("qb_made"), 1)
            for h in range(NH):
                r = par_rows(h)
                eng.tensor_copy(qb[r, h // 2, :, h], samples(proj[r, 12 + h // 2, s_cols])).then_inc(S("qb_made"), 1)

        SAMPLE_STEPS = {(0, "c"): ("turn", 0, 0), (1, "a"): ("turn", 0, 1), (1, "c"): ("turn_self", 0),
                        (2, "a"): ("values", 0), (2, "b"): ("values", 1), (2, "c"): ("values", 2),
                        (3, "a"): ("values", 3), (3, "c"): ("pick", 0),
                        (4, "a"): ("turn", 1, 0), (4, "c"): ("turn", 1, 1), (5, "a"): ("turn_self", 1),
                        (5, "c"): ("values", 4), (6, "a"): ("values", 5), (6, "b"): ("values", 6),
                        (6, "c"): ("values", 7), (7, "a"): ("pick", 1)}

        def pe_samples(eng, h, place):
            k = dict(skip_group_check=True)
            kind, *at = SAMPLE_STEPS.get((h, place), (None,))
            if kind == "turn":
                g, q = at
                eng.wait_ge(S("wp_made"), 1)
                if q:
                    eng.wait_ge(S("wp_turned"), 2 * g + 1)
                elif g:
                    eng.wait_ge(S("o_s_lo"), 1)
                for p in range(4):
                    mm = eng.transpose(psum[:, 7, p * P:(p + 1) * P],
                                       zp[:, g, DS + (4 * q + p) * P:DS + (4 * q + p + 1) * P], cc("ident"))
                mm.then_inc(S("wp_turn"), 1)
            elif kind == "turn_self":
                g, = at
                eng.wait_ge(S("self_spread"), 8)
                eng.wait_ge(S("wp_turned"), 2 * g + 2)
                eng.transpose(psum[0:TS, 7, 0:P], own_self[:, g].rearrange("p b t -> p (b t)"), cc("ident"))\
                   .then_inc(S("self_turn"), 1)
            elif kind == "values":
                b, = at
                g, rows = b // 4, slice(b % 4 * 32, b % 4 * 32 + 32)
                if b % 4 == 0:
                    eng.wait_ge(S("self_turned"), g + 1)
                    eng.matmul(psum[:, 7, :], a_self_t[:, g], vt[0:TS, NT, :], start=True, stop=False, **k)
                for half in range(2):
                    j = 2 * (b % 2) + half
                    eng.wait_ge(S(f"pages_loaded{j}"), 64 * (b // 2 + 1))
                    for p in range(4):
                        mm = eng.matmul(psum[rows, 7, :], a_t[:, g, 4 * half + p, rows], pages[j][:, p],
                                        start=False, stop=True, **k)
                    mm.then_inc(S(f"pages_used{j}"), 1)
            elif kind == "pick":
                g, = at
                eng.wait_ge(S("zsum_made"), g + 1)
                for hp in range(HP):
                    mm = eng.matmul(psum[:, 7, hp * 16:(hp + 1) * 16], zsum[:, hp * P:(hp + 1) * P], cc("pick", 16),
                                    start=hp == 0, stop=True, **k)
                mm.then_inc(S("o_s_done"), 1)

        def act_samples(eng, h, place=None):
            def turned(g, q):
                eng.wait_ge(S("wp_turn"), 2 * g + q + 1)
                eng.activation(a_t[:, g, 4 * q:4 * q + 4].rearrange("p a n -> p (a n)"), psum[:, 7, :], ACT.Copy)\
                   .then_inc(S("wp_turned"), 1)

            def self_turned(g):
                eng.wait_ge(S("self_turn"), g + 1)
                eng.activation(a_self_t[:, g], psum[0:TS, 7, 0:P], ACT.Copy).then_inc(S("self_turned"), 1)

            def output(g):
                eng.wait_ge(S("o_s_done"), g + 1)
                eng.activation(xh[:, HP:2 * HP, SEQ + 16 * g:SEQ + 16 * g + 16],
                               psum[:, 7, 0:64].rearrange("p (h n) -> p h n", h=HP), ACT.Copy).then_inc(S("o_s_hi"), 1)

            def h_high(q):
                if q == 0:
                    eng.wait_ge(S("h_back"), 16)
                two = slice(2 * q, 2 * q + 2)
                eng.activation(hh[:, two], y[:, two], ACT.Copy).then_inc(S("hh_made"), 1)

            if h == -1:
                eng.wait_ge(S("exponents_p"), 1)
                eng.activation(zp[:], zp[:], ACT.Exp).then_inc(S("wp_made"), 1)
            elif (h, place) == (1, "start"):
                turned(0, 0)
            elif (h, place) == (1, "mid"):
                turned(0, 1)
            elif (h, place) == (2, "start"):
                self_turned(0)
            elif (h, place) == (4, "start"):
                output(0)
            elif (h, place) == (4, "mid"):
                turned(1, 0)
            elif (h, place) == (5, "start"):
                turned(1, 1)
            elif (h, place) == (5, "mid"):
                self_turned(1)
                h_high(0)
                h_high(1)
            elif (h, place) == (6, "start"):
                h_high(2)
                h_high(3)
            elif (h, place) == (7, "mid"):
                output(1)

        def dve_samples(eng, h, place=None):
            def zsums(g):
                for half in range(2):
                    eng.wait_ge(S(f"pages_used{2 + half}"), 1 + 2 * g + 2)
                eng.tensor_tensor(zsum[:].rearrange("p (h n) -> p h n", h=NH),
                                  psum[:, 7, :].rearrange("p (h n) -> p h n", h=NH), each(cc("own_head", NH), HD),
                                  ALU.mult).then_inc(S("zsum_made"), 1)

            def output(g):
                eng.wait_ge(S("o_s_hi"), g + 1)
                cols = slice(SEQ + 16 * g, SEQ + 16 * g + 16)
                eng.tensor_tensor(xl[:, HP:2 * HP, cols], psum[:, 7, 0:64].rearrange("p (h n) -> p h n", h=HP),
                                  xh[:, HP:2 * HP, cols].bitcast(F32), ALU.subtract).then_inc(S("o_s_lo"), 1)

            if h == -1:
                eng.wait_ge(S("soft_p_made"), 3)
                eng.tensor_tensor(zp[:, :, 0:DS], zp[:, :, 0:DS], bcast(cc("cap", DS), 2), ALU.min)\
                   .then_inc(S("exponents_p"), 1)
            elif (h, place) == (0, "start"):
                eng.wait_ge(S("wp_made"), 1)
                for g in range(2):
                    own = cc("own_rows", NB, g * NB)
                    for t in range(DS):
                        eng.tensor_scalar(own_self[:, g, :, t], own, zp[:, g, DS - 1 - t:DS - t], None, ALU.mult)\
                           .then_inc(S("self_spread"), 1)
            elif (h, place) == (3, "mid"):
                zsums(0)
            elif (h, place) == (4, "start"):
                output(0)
            elif (h, place) == (7, "start"):
                zsums(1)
            elif (h, place) == (7, "mid"):
                output(1)

        b_r = Region(big_at, 20 * TX * 4)
        mh = b_r.tensor("mh", [P, KT, T], F32R)
        ml = b_r.tensor("ml", [P, KT, T], F32R)

        def pe_merge(eng, st):
            eng.wait_ge(S("o_b_lo"), HP)
            eng.wait_ge(S("o_s_lo"), 2)
            eng.wait_ge(S("hl_made"), 4)
            with eng.Fori(0, KT) as i:
                for s in range(2):
                    unit_ready(eng, s, i + st.m0)
                    eng.wait_ge(*((S("gates_made"), i + 1) if s == 0 else (S("gated"), i * 2 + 1)))
                    a_hi, a_lo, n = (hh, hl, KT) if s == 0 else (xh, xl, HP)
                    for t in range(2):
                        for k in range(n):
                            w = slice((t * n + k) * P, (t * n + k + 1) * P)
                            f = k if s == 0 else t * HP + k
                            mm = split_product(eng, 4 * s + 2 * t, whi[s][:, w], wlo[s][:, w],
                                               a_hi[:, f, 0:T], a_lo[:, f, 0:T], HALF, k == 0, k == n - 1)
                    mm.then_inc(used[s], 1)

        def act_merge(eng, st, next_cols):
            def work(i, s):
                if s == 0:
                    eng.wait_ge(used[0], i + (st.m0 + 2))
                    eng.wait_ge(S("gated"), i * 2 + 1)
                    for t in range(2):
                        gates = eng.activation(halves(sg[t][:]), two_halves(2 * t), ACT.Sigmoid)
                        if t:
                            gates.then_inc(S("gates_made"), 1)
            pipelined(eng, st, work, next_cols)

        def dve_merge(eng, st):
            with eng.Fori(0, KT) as i:
                one = lambda a: a[:, bass.ds(i, 1)].rearrange("p a n -> p (a n)")
                eng.wait_ge(used[1], i + (st.m0 + 2))
                eng.wait_ge(S("gates_made"), i + 2)
                eng.wait_ge(S("merged"), i * 3 + 1)
                for t in range(2):
                    eng.tensor_tensor(halves(u[t][:]), two_halves(4 + 2 * t), halves(sg[t][:]), ALU.mult)\
                       .then_inc(S("gated"), 1)
                eng.wait_ge(S("gated"), i * 2 + 3)
                eng.tensor_tensor(u[0][:], u[0][:], u[1][:], ALU.add).then_inc(S("merged"), 1)
                eng.wait_ge(S("merged"), i * 3 + 2)
                eng.tensor_copy(one(mh), u[0][:]).then_inc(S("merged"), 1)
                eng.wait_ge(S("merged"), i * 3 + 3)
                eng.tensor_tensor(one(ml), u[0][:], one(mh).bitcast(F32), ALU.subtract).then_inc(S("merged"), 1)

        def pe_out(eng, st):
            eng.wait_ge(S("merged"), 3 * KT + 1)
            with eng.Fori(0, st.n // 2) as i:
                for s in range(2):
                    unit_ready(eng, s, i + st.m0)
                    eng.wait_ge(S(f"mixed_in{s}"), i * 2 + 1)
                    for t in range(2):
                        for k in range(KT):
                            w = slice((t * KT + k) * P, (t * KT + k + 1) * P)
                            mm = split_product(eng, 4 * s + 2 * t, whi[s][:, w], wlo[s][:, w], mh[:, k], ml[:, k],
                                               HALF, k == 0, k == KT - 1)
                    mm.then_inc(used[s], 1)

        def dve_out(eng, st):
            eng.wait_ge(S("merged"), 3 * KT + 1)
            eng.memset(total[:], 0.0).then_inc(S("totalled"), 1)
            eng.wait_ge(S("h_back"), 16)
            with eng.Fori(0, st.n // 2) as i:
                for s in range(2):
                    eng.wait_ge(used[s], i + (st.m0 + 2))
                    for t in range(2):
                        row = y[:, bass.ds(i * 4 + (2 * s + t), 1)].rearrange("p a (h n) -> p (a h) n", h=2)
                        eng.scalar_tensor_tensor(row, two_halves(4 * s + 2 * t), 1.0 / ALPHA, row, ALU.mult, ALU.add)\
                           .then_inc(S(f"mixed_in{s}"), 1)
                        eng.wait_ge(S(f"mixed_in{s}"), i * 2 + (t + 2))
                        eng.wait_ge(S("totalled"), i * 4 + (KT + 1 + 2 * s + t + 1))
                        eng.tensor_tensor(halves(total[:]), halves(total[:]), row, ALU.add).then_inc(S("totalled"), 1)

        block = ctx.enter_context(nc.Block())

        @block.sync
        def _(sp):
            sp_stage(sp, stages["ffn1_in"], io["ffn1_w_in"])
            sp_stage(sp, stages["ffn1_out"], io["ffn1_w_out"])
            sp_stage(sp, stages["rkv"], io["w_rkv"])
            for q in range(6):
                s, m = mid_unit(q)
                src, cols = ((io["lora_wa"], KT * P), (io["lora_g"][0], KT * GL), (io["lora_g"][1], KT * GL),
                             (io["w_v"][:, 0:1536], 1536), (io["w_v"][:, 1536:3072], 1536),
                             (io["w_v"][:, 3072:4096], 1024))[q]
                load_unit(sp, s, m, src, cols)
                if q == 0:
                    sp.wait_ge(S("normed"), KT)
                    sp.dma_start(io["h"], y[:]).then_inc(S("h_stored"), 16)
                if q == 1:
                    sp.dma_start(inner2[0:HD], io["w_w2"]).then_inc(S("inner2_loaded"), 16)
                    sp.dma_start(inner2[HD:P], io["a_w2"]).then_inc(S("inner2_loaded"), 16)
                    sp.dma_start(inner2g[:], io["g_w2"]).then_inc(S("inner2_loaded"), 16)
            sp.wait_ge(S("k_scaled"), HP)
            sp.dma_start(cst[:], io["constants"][:, 0:NCST - N_MASKS]).then_inc(S("cst_loaded"), 16)
            sp_stage(sp, stages["qk"], io["w_qk"])
            wait_w_in(sp)
            sp.dma_start(masks[:], io["constants"][:, NCST - N_MASKS:NCST]).then_inc(S("masks_loaded"), 16)
            for s in range(2):
                sp.wait_ge(S(f"qk_made{s}"), 3)
            sp.dma_start(io["k_rows"], proj[:, 16:20, 0:T]).then_inc(S("out_stored"), 16)
            sp.dma_start(io["v_rows"][0:SEQ].rearrange("(t p) n -> p t n", p=P), vt[:, 0:NT]).then_inc(S("out_stored"), 16)
            sp.dma_start(io["v_rows"][SEQ:T], vt[0:TS, NT]).then_inc(S("out_stored"), 16)
            sp_k_pages(sp, io)
            sp.wait_ge(S("y_made"), NT + 1)
            sp.dma_start(state_s[:], io["state_s"]).then_inc(S("state_loaded"), 16)
            sp.wait_ge(S("state_made"), last)
            sp.dma_start(io["wkv_p"], state[:]).then_inc(S("states_stored"), 16)
            sp.wait_ge(*step("s_state", 2 * HP))
            sp.dma_start(io["wkv_s"], state_s[:]).then_inc(S("states_stored"), 16)
            sp.wait_ge(S("states_stored"), 32)
            sp.dma_start(y[:], io["h"]).then_inc(S("h_back"), 16)
            sp_v_pages(sp, io)
            sp.wait_ge(S("o_s_lo"), 2)
            sp.wait_ge(S("out_stored"), 16 * 3)
            st = stages["merge"]
            with sp.Fori(0, KT) as i:
                for s, name in enumerate(("w_gates", "w_branch")):
                    load_unit(sp, s, i + st.m0, io[name][bass.ds(i, 1)].rearrange("a p n -> (a p) n"), MERGE_COLS[s])
            sp_stage(sp, stages["out"], io["w_out"])
            sp_stage(sp, stages["ffn2_in"], io["ffn2_w_in"])
            sp_stage(sp, stages["ffn2_out"], io["ffn2_w_out"])
            for k in range(KT):
                sp.wait_ge(S("normed"), 2 * KT + k + 1)
                sp.dma_start(io["y"][:, k], y[:, k]).then_inc(S("y_stored"), 16)
            sp.wait_ge(S("y_stored"), 16 * KT)
            sp.wait_ge(S("states_stored"), 32)

        @block.gpsimd
        def _(pool):
            for s in range(2):
                pool.sem_inc(lo_made[s], 1)
            for name in ("ffn1_in", "ffn1_out", "rkv"):
                pool_stage(pool, stages[name])
            for q in range(6):
                make_lo(pool, *mid_unit(q), MID_COLS[q])
            pool_stage(pool, stages["qk"])
            pool_wkv(pool)
            pool_wkv_s(pool)
            pool_stick(pool)
            for name in ("merge", "out", "ffn2_in", "ffn2_out"):
                pool_stage(pool, stages[name])

        @block.scalar
        def _(act):
            for s in range(2):
                act.sem_inc(hi_made[s], 1)
                act.sem_inc(S(f"rkv_made{s}"), 1)
                act.sem_inc(S(f"qk_made{s}"), 1)
            act.sem_inc(S("y_made"), 1)
            for q in range(4):
                act.dma_start(y[:, 2 * q:2 * q + 2], io["x"][:, 2 * q:2 * q + 2]).then_inc(S(f"x_loaded{q}"), 16)
            act.dma_start(vecs[:], io["vecs"]).then_inc(S("vecs_loaded"), 16)
            act.dma_start(before[:], io["before"]).then_inc(S("vecs_loaded"), 16)
            act.dma_start(page_of[:], io["page_table"]).then_inc(S("page_table_loaded"), 16)
            make_hi(act, 0, 0, 2048)
            act_ffn_in(act, stages["ffn1_in"], 0, stages["ffn1_out"].cols)
            act_ffn_out(act, stages["ffn1_out"], stages["rkv"].cols)
            act.wait_ge(S("set_up"), 3)
            act.wait_ge(S("vecs_loaded"), 32)
            act_norm(act, 0, "ln1_g", "ln1_b", True)
            act_pairs(act, stages["rkv"], "rkv_made", 0, ACT.Copy, MID_COLS[0], (S("lora_weights"), 1))
            act_mid(act)
            act_prep(act)
            act_pairs(act, stages["qk"], "qk_made", 12, ACT.Copy, 0)
            act_wkv(act)
            act_wkv_s(act)
            act_heads(act)
            act_stick(act)
            act.sem_inc(S("gates_made"), 1)
            make_hi(act, 0, stages["merge"].m0, MERGE_COLS[0])
            act_merge(act, stages["merge"], stages["out"].cols)
            pipelined(act, stages["out"], lambda i, s: None, stages["ffn2_in"].cols)
            act_norm(act, 1, "ln2_g", "ln2_b", True)
            act_ffn_in(act, stages["ffn2_in"], 1, stages["ffn2_out"].cols)
            act_ffn_out(act, stages["ffn2_out"], 0)
            act_norm(act, 2, "ln3_g", "ln3_b", False)

        @block.tensor
        def _(pe):
            for s in range(2):
                pe.sem_inc(used[s], 1)
                pe.sem_inc(S(f"k_pages_used{s}"), 1)
                for j in (s, 2 + s):
                    pe.sem_inc(S(f"pages_used{j}"), 1)
            pe_ffn_in(pe, stages["ffn1_in"], 0, lambda k: (S("x_split"), 2 * (k + 1)))
            pe_ffn_out(pe, stages["ffn1_out"], 0)
            pe.wait_ge(S("set_up"), 3)
            pe_norm(pe, 0)
            pe.wait_ge(S("x_split"), 2 * (KT + 1))
            pe_pairs(pe, stages["rkv"], "rkv_made", lambda k: (S("norm_lo"), k + 1))
            pe_mid(pe)
            pe_prep(pe)
            pe_pairs(pe, stages["qk"], "qk_made")
            pe_wkv(pe)
            pe_wkv_s(pe)
            pe_heads(pe)
            pe_stick(pe)
            pe_merge(pe, stages["merge"])
            pe_out(pe, stages["out"])
            pe_norm(pe, 1)
            pe_ffn_in(pe, stages["ffn2_in"], 1, lambda k: (S("norm_lo"), KT + k + 1))
            pe_ffn_out(pe, stages["ffn2_out"], 1)
            pe_norm(pe, 2)

        @block.vector
        def _(dve):
            for s in range(2):
                for name in ("ffn_read", "inner_split", "mixed_in"):
                    dve.sem_inc(S(f"{name}{s}"), 1)
            dve.sem_inc(S("gated"), 1)
            dve.sem_inc(S("merged"), 1)
            dve.sem_inc(S("y_added"), 2)
            dve.sem_inc(S("state_made"), 1)
            for a, value in ((mean_w[:], 1.0 / D_MODEL), (eps[:, 0:1], LN_EPS / ALPHA ** 2), (eps[:, 1:2], LNX_EPS)):
                dve.memset(a, value).then_inc(S("set_up"), 1)
            for k in range(KT + 1):
                if k < KT:
                    dve.wait_ge(S(f"x_loaded{k // 2}"), 16)
                    src, hi, lo = y[:, k], xh[:, k, 0:T], xl[:, k, 0:T]
                else:
                    dve.wait_ge(S("vecs_loaded"), 32)
                    src, hi, lo = before[:], xh[:, :, T:TX], xl[:, :, T:TX]
                dve.tensor_copy(hi, src).then_inc(S("x_split"), 1)
                dve.wait_ge(S("x_split"), 2 * k + 1)
                dve.tensor_tensor(lo, src, hi.bitcast(F32), ALU.subtract).then_inc(S("x_split"), 1)
            dve_ffn_in(dve, stages["ffn1_in"], 0)
            dve_ffn_out(dve, stages["ffn1_out"], 0)
            dve_norm(dve, 0, "ln1_g", True)
            dve_lora_weights(dve)
            dve_shift(dve).wait(dve)
            dve_keys(dve)
            dve_lora_sum(dve)
            dve_prep(dve)
            dve_qb(dve)
            dve_wkv(dve)
            dve_wkv_s(dve)
            dve_heads(dve)
            dve_stick(dve)
            dve_merge(dve, stages["merge"])
            dve_out(dve, stages["out"])
            dve_norm(dve, 1, "ln2_g", True)
            dve_ffn_in(dve, stages["ffn2_in"], 1)
            dve_ffn_out(dve, stages["ffn2_out"], 1)
            dve_norm(dve, 2, "ln3_g", False)


def tiles_of(w, k, n):
    return w.reshape(k, P, -1, n).transpose(2, 1, 0, 3)


def kernel(x_prompt, x_sample, cache_k, cache_v, state_wkv, state_shift, page_table,
           ln1_g, ln1_b, ffn1_w_in, ffn1_w_out, w_in, mu_rkv, mu_wag, w0, w_w1, w_w2,
           a0, a_w1, a_w2, g_w1, g_w2, k_k, k_a, r_k, lnx_g, lnx_b, sb_bias, w_branch, w_out,
           ln2_g, ln2_b, ffn2_w_in, ffn2_w_out, ln3_g, ln3_b):
    import concourse.bacc as bacc
    from concourse.bass_utils import run_bass_kernel_spmd

    a = {k: np.asarray(v) for k, v in locals().items() if k not in ("bacc", "run_bass_kernel_spmd")}
    cols = lambda v: v.reshape(-1, P).T
    by_feature = lambda t: t.reshape(-1, KT, P).transpose(2, 1, 0)
    tokens = np.concatenate([a["x_prompt"].reshape(SEQ, D_MODEL), a["x_sample"].reshape(TS, D_MODEL)])
    vecs = {"mu_w": a["mu_wag"][0, 0], "mu_a": a["mu_wag"][0, 1], "mu_g": a["mu_wag"][0, 2]}
    packed = [cols(vecs[n] if n in vecs else a[n].reshape(-1)) for n in VEC if not n.startswith("sb_bias")]
    bias = a["sb_bias"].reshape(NH)
    packed += [np.tile(bias[None], (P, 1)), np.tile(np.repeat(bias, DS), 4)[:, None]]

    def ffn_in(w):
        t = tiles_of(w[0], KT, P)
        return np.stack([t[:FT], t[FT:]], 2).reshape(FT, P, UNIT)

    def ffn_out(w):
        t = tiles_of(w[0], FT, P)
        return t.reshape(KT, P, 2, FH * P).transpose(0, 2, 1, 3).reshape(2 * KT, P, FH * P)

    def pairs(w):
        t = tiles_of(w, KT, P)
        return t.reshape(-1, 2, P, KT * P).transpose(0, 2, 1, 3).reshape(-1, P, UNIT)

    wi = a["w_in"][0]
    n3 = 3 * 512
    rows = lambda c: c[0].reshape(N_PHYS, PAGE, NH * HD)[:, ::-1]
    ins = {
        "vecs": np.concatenate(packed, 1), "before": by_feature(a["state_shift"][0]), "x": by_feature(tokens),
        "constants": constants(),
        "ffn1_w_in": ffn_in(a["ffn1_w_in"]), "ffn1_w_out": ffn_out(a["ffn1_w_out"]),
        "ffn2_w_in": ffn_in(a["ffn2_w_in"]), "ffn2_w_out": ffn_out(a["ffn2_w_out"]),
        "w_rkv": pairs(wi[:, :n3]),
        "lora_wa": tiles_of(np.concatenate([a["w_w1"][0], a["a_w1"][0]], 1), KT, P).reshape(P, KT * P),
        "lora_g": tiles_of(a["g_w1"][0], KT, GL).reshape(2, P, KT * GL),
        "w_v": wi[:, n3 + 1024:n3 + n3].reshape(KT, P, 512).transpose(1, 0, 2).reshape(P, KT * 512),
        "w_qk": pairs(wi[:, n3:n3 + 1024]),
        "w_gates": tiles_of(wi[:, 2 * n3:], KT, P).reshape(2, KT, P, KT * P).transpose(1, 2, 0, 3).reshape(KT, P, UNIT),
        "w_w2": a["w_w2"][0], "a_w2": a["a_w2"][0],
        "g_w2": a["g_w2"][0].reshape(2, GL, 512).transpose(1, 0, 2),
        "w_branch": tiles_of(a["w_branch"][0], KT, P).reshape(KT, P, KT * P), "w_out": pairs(a["w_out"][0]),
        "state_s": a["state_wkv"][0].reshape(NB, HP, 2, HD, HD).transpose(2, 4, 1, 0, 3).reshape(P, HP, NB, HD),
        "cache_k": rows(a["cache_k"]).reshape(N_PHYS, PAGE, HP, P).transpose(0, 3, 2, 1),
        "cache_v": rows(a["cache_v"]), "page_table": a["page_table"].reshape(1, -1),
    }
    outs = {"y": [P, KT, T], "h": [P, KT, T], "k_rows": [P, HP, T], "v_rows": [T, 512],
            "wkv_p": [P, HP, P], "wkv_s": [P, HP, NB, HD]}

    nc = bacc.Bacc("TRN2", target_bir_lowering=False, num_devices=1)
    io, arrays = {}, {}
    for n, v in ins.items():
        v = np.ascontiguousarray(v)
        arrays["in_" + n] = v
        io[n] = nc.dram_tensor("in_" + n, list(v.shape), mybir.dt.from_np(v.dtype), kind="ExternalInput").ap()
    for n, shape in outs.items():
        io[n] = nc.dram_tensor("out_" + n, shape, F32, kind="ExternalOutput").ap()
    build(nc, io)
    got = run_bass_kernel_spmd(nc, [arrays], core_ids=[0]).results[0]

    y = got["out_y"].transpose(2, 1, 0).reshape(T, D_MODEL)
    k = got["out_k_rows"].transpose(2, 1, 0).reshape(T, NH, HD)
    v = got["out_v_rows"].reshape(T, NH, HD)
    shift = got["out_h"][:, :, SEQ - 1:][:, :, ::DS].transpose(2, 1, 0).reshape(1 + NB, D_MODEL)
    wp = got["out_wkv_p"].reshape(2, HD, HP, 2, HD)
    wp = np.stack([wp[0, :, :, 0], wp[1, :, :, 1]]).transpose(2, 0, 3, 1).reshape(1, 1, NH, HD, HD)
    ws = got["out_wkv_s"].reshape(2, HD, HP, NB, HD).transpose(3, 2, 0, 4, 1).reshape(1, NB, NH, HD, HD)
    return (y[:SEQ].reshape(1, SEQ, D_MODEL), y[SEQ:].reshape(NB, DS, D_MODEL),
            k[:SEQ].reshape(1, 1, SEQ, NH, HD), v[:SEQ].reshape(1, 1, SEQ, NH, HD), wp,
            shift[:1].reshape(1, 1, D_MODEL),
            k[SEQ:].reshape(1, NB, DS, NH, HD), v[SEQ:].reshape(1, NB, DS, NH, HD), ws,
            shift[1:].reshape(1, NB, D_MODEL))
```

```python
from contextlib import ExitStack

import numpy as np

import concourse.bass as bass
from concourse import mybir
from concourse.alu_op_type import AluOpType as ALU

F32 = mybir.dt.float32
F32R = mybir.dt.float32r
I32 = mybir.dt.int32
ACT = mybir.ActivationFunctionType
AX = mybir.AxisListType

P = 128
D_MODEL = 1024
KT = D_MODEL // P
SEQ = 512
NB = 8
DS = 4
TS = NB * DS
T = SEQ + TS
TX = T + NB
HALF = T // 2
HALFX = TX // 2
D_FF = 2816
FT = D_FF // P
FH = FT // 2
HD = 64
NH = 8
HP = NH // 2
PAGE = 128
N_PAGES = 8
N_PHYS = 80
PAST = PAGE * N_PAGES
CH = 64
LEVELS = 6
NT = SEQ // P
ALPHA = 2.0 ** 0.25
LN_EPS = 1e-5
LNX_EPS = 64e-5
DECAY = -float(np.exp(-0.5))
SCALE = HD ** -0.5
GL = 80
LOG_EXP = "natural_log_exp_and_others"
UNIT = 2048
MASKED = -30000.0

VEC = {}
NVEC = 0
for _name, _n in (("ln1_g", 8), ("ln1_b", 8), ("ln2_g", 8), ("ln2_b", 8), ("ln3_g", 8), ("ln3_b", 8),
                  ("mu_w", 8), ("mu_a", 8), ("mu_g", 8), ("mu_rkv", 12), ("w0", 4), ("a0", 4),
                  ("k_k", 4), ("k_a", 4), ("r_k", 4), ("lnx_g", 4), ("lnx_b", 4), ("sb_bias", 8),
                  ("sb_bias_rows", 1)):
    VEC[_name] = NVEC
    NVEC += _n

CST = {}
NCST = 0
for _name, _n in (("pair", P), ("ident", P), ("ones", P), ("suffix", P), ("keep", T), ("own", NB),
                  ("own_rows", 2 * NB), ("own_head", NH), ("pick", 16), ("self", DS), ("cap", DS),
                  ("score", 2 * P), ("score_s", 2 * P), ("level", LEVELS * P)):
    CST[_name] = NCST
    NCST += _n
N_MASKS = (4 + LEVELS) * P


def constants():
    c = np.zeros((P, NCST), np.float32)
    row, col = np.arange(P)[:, None], np.arange(P)[None, :]

    def put(name, a):
        c[:, CST[name]:CST[name] + a.shape[1]] = a

    put("pair", row // HD == col // HD)
    put("ident", row == col)
    put("ones", np.ones((P, P)))
    put("suffix", row >= col)
    same = row // CH == col // CH
    put("score", np.concatenate([same & (row < col), same & (row <= col)], 1))
    same = row // DS == col // DS
    put("score_s", np.concatenate([same & (row < col), same & (row <= col)], 1))
    put("level", np.concatenate(
        [(row // (2 * n) == col // (2 * n)) & (row % (2 * n) < n) & (col % (2 * n) >= n)
         for n in (2 ** l for l in range(LEVELS))], 1))
    keep = np.ones((P, T))
    keep[:, :SEQ][:, ::CH] = 0
    keep[:, SEQ:][:, ::DS] = 0
    put("keep", keep)
    put("own", (row % TS) // DS == np.arange(NB)[None])
    put("own_rows", np.concatenate([row // TS + 4 * g == np.arange(NB)[None] for g in range(2)], 1))
    put("own_head", (row % TS) // DS == np.arange(NH)[None])
    put("pick", (row // TS == np.arange(16)[None] // DS) & (row % DS == np.arange(16)[None] % DS))
    seen = (DS - 1 - np.arange(DS)[None]) < row % DS
    put("self", seen)
    put("cap", np.where(seen, 3e38, MASKED))
    return c


def build(nc, io):
    ctx = ExitStack()
    with ctx:
        sems = {}

        def S(name):
            name = STEPS[name][0] if name in STEPS else name
            if name not in sems:
                sems[name] = ctx.enter_context(nc.semaphore(name))
            return sems[name]

        STEPS = {}

        def in_a_row(shared, steps, first=0):
            for name, times in steps:
                STEPS[name] = (shared, first, 1)
                first += times

        def in_turn(shared, *steps):
            for j, name in enumerate(steps):
                STEPS[name] = (shared, j + 1 - len(steps), len(steps))

        def step(name, n=1):
            shared, first, every = STEPS[name]
            return S(shared), first + every * n

        in_a_row("prep_products", (("k_summed", HP), ("lora_second", 3 * HP)))
        in_a_row("prep_scalar", (("k_squared", HP), ("k_norm", HP), ("lora_out", 3 * HP)))
        in_a_row("s_products", (("s_scored", 2), ("s_turned", 1), ("s_with_state", 1), ("s_carry", 2),
                                ("s_grown", 1), ("s_ak", 1), ("s_sa", 1), ("s_y", 1), ("s_y_turned", 1),
                                ("s_update", HP)))
        in_a_row("s_scalar", (("s_tok", 1), ("s_carry_made", 1), ("s_sa_made", 1)))
        in_a_row("s_pool", (("s_v_copied", 1), ("s_mask_made", 2), ("s_state_final", HP)))
        in_a_row("s_vector", (("s_scaled", 4), ("s_masked", 2), ("s_inv", 3), ("s_rhs", 1), ("s_expanded", 4),
                              ("s_y_summed", 1), ("s_state", HP)))
        in_turn("heads_sums", "y_mean", "rk_summed")
        in_turn("heads_roots", "y_log", "y_rstd")
        in_turn("heads_first", "rk_made", "y_centred")

        base0 = nc.sbuf_base + (-nc.sbuf_base) % 32
        arena_bytes = (nc.sbuf_usable_end - base0) // 32 * 32
        ctx.enter_context(nc.sbuf_tensor("arena", [P, arena_bytes // 4], F32))

        class Region:
            def __init__(self, start, size):
                self.start, self.at, self.end = start, start, start + size

            def tensor(self, name, shape, dtype=F32):
                size = 4 * int(np.prod(shape[1:]))
                assert self.at + size <= self.end, (name, self.at + size - self.end)
                t = nc.alloc_sbuf_tensor_at(name, shape, dtype, offset=self.at)
                self.at += (size + 31) // 32 * 32
                return t

        whole = Region(base0, arena_bytes)

        def region(size):
            r = Region(whole.at, size)
            whole.at += size
            assert whole.at <= whole.end
            return r

        keepers = region((4 * (NVEC + P + KT * NB + 2 * TS) + 15 * 32 + 31) // 32 * 32 + 64)
        vecs = keepers.tensor("vecs", [P, NVEC])
        mean_w = keepers.tensor("mean_w", [P, P])
        eps = keepers.tensor("eps", [P, 2])
        before = keepers.tensor("before", [P, KT, NB])

        one_less = keepers.tensor("one_less", [P, HP])
        self4 = keepers.tensor("self4", [P, DS])
        ends = keepers.tensor("ends", [P, HP, 2])
        own_self = keepers.tensor("own_self", [P, 2, NB, DS])
        page_of = keepers.tensor("page_of", [1, NB * N_PAGES], I32)

        split_at = whole.at
        split_r = region(2 * 4 * KT * TX)
        xh = split_r.tensor("xh", [P, KT, TX], F32R)
        xl = split_r.tensor("xl", [P, KT, TX], F32R)
        y_r = region(4 * KT * T)
        y = y_r.tensor("y", [P, KT, T])

        ring_at = whole.at
        ring_r = region(6 * 4 * UNIT)
        raw = [ring_r.tensor(f"raw{s}", [P, UNIT]) for s in range(2)]
        whi = [ring_r.tensor(f"whi{s}", [P, UNIT], F32R) for s in range(2)]
        wlo = [ring_r.tensor(f"wlo{s}", [P, UNIT], F32R) for s in range(2)]

        temp_at = whole.at
        temp_bytes = 4 * 4 * T
        temp_r = region(temp_bytes)
        sg = [temp_r.tensor(f"sg{s}", [P, T]) for s in range(2)]
        u = [temp_r.tensor(f"u{s}", [P, T]) for s in range(2)]
        temp_r.at = temp_at
        sq = [temp_r.tensor(f"sq{s}", [P, T]) for s in range(2)]
        rstd = temp_r.tensor("rstd", [P, T])
        total = temp_r.tensor("total", [P, T])

        big_at = whole.at
        big_bytes = 2 * 4 * FT * T + 128
        big_r = region(big_bytes)
        gh = big_r.tensor("gh", [P, FT, T], F32R)
        gl = big_r.tensor("gl", [P, FT, T], F32R)
        big_r.at = big_at
        proj = big_r.tensor("proj", [P, 20, TX])
        g_at = big_r.at
        big_r.at += 16 * TX * 4
        vt = big_r.tensor("vt", [P, NT + 1, 512])
        inner2 = big_r.tensor("inner2", [P, 512])
        inner2g = big_r.tensor("inner2g", [GL, 2, 512])
        big_end = big_r.at
        big_r.at -= 4 * 1536
        ar_late = big_r.tensor("ar_late", [P, HP, 2, P])
        e_ex = big_r.tensor("e_ex", [P, HP, P])
        big_r.at = g_at
        lora = big_r.tensor("lora", [P, 6, TX])
        temp_r.at = temp_at
        temp_diff = temp_r.tensor("temp_diff", [P, 4, T])
        G_BYTES = 16 * TX * 4
        g_r = Region(g_at, G_BYTES)
        a_b = g_r.tensor("a_b", [P, HP, T])
        g_out = g_r.tensor("g_out", [P, HP, T])
        kk = g_r.tensor("kk", [P, HP, T])
        zp_at = g_r.at
        lora_wa = g_r.tensor("lora_wa", [P, T])
        lora_g = g_r.tensor("lora_g", [GL, 2, T])
        zp = Region(zp_at, g_at + G_BYTES - zp_at).tensor("zp", [P, 2, PAST + DS])
        squares = Region(g_at, G_BYTES).tensor("squares", [P, HP, T])
        g_r = Region(g_at, G_BYTES)
        hh = g_r.tensor("hh", [P, KT, T], F32R)
        hl = g_r.tensor("hl", [P, KT, T], F32R)


        psum = ctx.enter_context(nc.psum_tensor("psum", [P, 8, 512], F32))

        def vec(name, i):
            return vecs[:, VEC[name] + i:VEC[name] + i + 1]

        class Stage:
            def __init__(self, name, n, cols, first):
                self.name, self.n, self.cols, self.m0 = name, n, cols, first // 2
                assert first % 2 == 0 and n % 2 == 0

        MERGE_COLS = D_MODEL + 512
        stages, at = {}, 0
        for name, n, cols in (("ffn1_in", FT, 2048), ("ffn1_out", 16, FH * P), ("rkv", 6, 2048),
                              ("mid", 6, None), ("qk", 4, 2048), ("merge", 2 * KT, MERGE_COLS),
                              ("out", 4, 2048), ("ffn2_in", FT, 2048), ("ffn2_out", 16, FH * P)):
            stages[name] = Stage(name, n, cols, at)
            at += n
        MID_COLS = [2 * 1024, 2 * 8 * GL, 2 * 8 * GL, 3 * 512, 3 * 512, 2 * 512]
        landed = [S(f"raw_landed{s}") for s in range(2)]
        hi_made = [S(f"hi_made{s}") for s in range(2)]
        lo_made = [S(f"lo_made{s}") for s in range(2)]
        used = [S(f"unit_used{s}") for s in range(2)]

        def load_unit(eng, s, m, src, cols):
            eng.wait_ge(hi_made[s], m + 1)
            eng.wait_ge(lo_made[s], m + 1)
            eng.dma_start(raw[s][:, 0:cols], src).then_inc(landed[s], 16)

        def make_hi(eng, s, m, cols, ready=None):
            if ready is None:
                eng.wait_ge(landed[s], (m + 1) * 16)
            else:
                eng.wait_ge(*ready)
            eng.wait_ge(used[s], m + 1)
            eng.activation(whi[s][:, 0:cols], raw[s][:, 0:cols], ACT.Copy).then_inc(hi_made[s], 1)

        def make_lo(eng, s, m, cols):
            eng.wait_ge(hi_made[s], m + 2)
            eng.tensor_tensor(wlo[s][:, 0:cols], raw[s][:, 0:cols], whi[s][:, 0:cols].bitcast(F32),
                              ALU.subtract).then_inc(lo_made[s], 1)

        def unit_ready(eng, s, m):
            eng.wait_ge(hi_made[s], m + 2)
            eng.wait_ge(lo_made[s], m + 2)

        def two_halves(bank, n=HALF):
            return psum[:, bank:bank + 2, 0:n]

        def halves(a):
            return a.rearrange("p (h n) -> p h n", h=2)

        def split_product(eng, bank, w_hi, w_lo, a_hi, a_lo, n, first, last, rows=P):
            mm = None
            for k, (w, a) in enumerate(((w_hi, a_hi), (w_hi, a_lo), (w_lo, a_hi))):
                for h in range(2):
                    mm = eng.matmul(psum[0:rows, bank + h, 0:n], w, a[:, h * n:(h + 1) * n],
                                    start=first and k == 0, stop=last and k == 2)
            return mm

        def sp_stage(eng, st, dram):
            with eng.Fori(0, st.n // 2) as i:
                for s in range(2):
                    load_unit(eng, s, i + st.m0, dram[bass.ds(i * 2 + s, 1)].rearrange("a p n -> (a p) n"),
                              st.cols)

        def pool_stage(eng, st):
            with eng.Fori(0, st.n // 2) as i:
                for s in range(2):
                    make_lo(eng, s, i + st.m0, st.cols)

        def pipelined(eng, st, work, next_cols, next_ready=None):
            def body(i, last):
                make_hi(eng, 1, i + st.m0, st.cols)
                work(i, 0)
                if last:
                    if next_cols:
                        make_hi(eng, 0, i + st.m0 + 1, next_cols, next_ready)
                else:
                    make_hi(eng, 0, i + (st.m0 + 1), st.cols)
                work(i, 1)
            with eng.Fori(0, st.n // 2 - 1) as i:
                body(i, False)
            body(st.n // 2 - 1, True)

        def pe_ffn_in(eng, st, r, tile_ready):
            with eng.Fori(0, FT // 2) as i:
                for s in range(2):
                    unit_ready(eng, s, i + st.m0)
                    eng.wait_ge(S(f"ffn_read{s}"), i + (r * (FT // 2) + 1))
                    w_hi = whi[s][:].rearrange("p (t k n) -> p t k n", t=2, k=KT)
                    w_lo = wlo[s][:].rearrange("p (t k n) -> p t k n", t=2, k=KT)
                    for t in range(2):
                        for k in range(KT):
                            if s == t == 0:
                                eng.wait_ge(*tile_ready(k))
                            mm = split_product(eng, 4 * s + 2 * t, w_hi[:, t, k], w_lo[:, t, k],
                                               xh[:, k, 0:T], xl[:, k, 0:T], HALF, k == 0, k == KT - 1)
                        mm.then_inc(S(f"gate_done{s}") if t == 0 else used[s], 1)

        def act_ffn_in(eng, st, r, next_cols):
            def work(i, s):
                eng.wait_ge(S(f"gate_done{s}"), i + (r * (FT // 2) + 1))
                eng.wait_ge(S(f"ffn_read{s}"), i + (r * (FT // 2) + 1))
                eng.activation(halves(sg[s][:]), two_halves(4 * s), ACT.Sigmoid)\
                   .then_inc(S(f"sigmoid_made{s}"), 1)
            pipelined(eng, st, work, next_cols)

        def dve_ffn_in(eng, st, r):
            with eng.Fori(0, FT // 2) as i:
                for s in range(2):
                    n = i + (r * (FT // 2) + 1)
                    f = bass.ds(i * 2 + s, 1)
                    eng.wait_ge(S(f"sigmoid_made{s}"), n)
                    eng.tensor_tensor(halves(sg[s][:]), two_halves(4 * s), halves(sg[s][:]), ALU.mult)\
                       .then_inc(S(f"silu_made{s}"), 1)
                    eng.wait_ge(used[s], i + (st.m0 + 2))
                    eng.wait_ge(S(f"silu_made{s}"), n)
                    eng.wait_ge(S(f"inner_split{s}"), n * 2 - 1)
                    eng.tensor_tensor(halves(u[s][:]), two_halves(4 * s + 2), halves(sg[s][:]), ALU.mult)\
                       .then_inc(S(f"ffn_read{s}"), 1)
                    eng.wait_ge(S(f"ffn_read{s}"), n + 1)
                    eng.tensor_copy(gh[:, f].rearrange("p a n -> p (a n)"), u[s][:])\
                       .then_inc(S(f"inner_split{s}"), 1)
                    eng.wait_ge(S(f"inner_split{s}"), n * 2)
                    eng.tensor_tensor(gl[:, f].rearrange("p a n -> p (a n)"), u[s][:],
                                      gh[:, f].rearrange("p a n -> p (a n)").bitcast(F32), ALU.subtract)\
                       .then_inc(S(f"inner_split{s}"), 1)

        def pe_ffn_out(eng, st, r):
            for s in range(2):
                eng.wait_ge(S(f"inner_split{s}"), r * FT + FH + 2)
            eng.wait_ge(S("ffn_read0"), (r + 1) * (FT // 2) + 1)
            with eng.Fori(0, KT // 2) as i:
                for j in range(2):
                    eng.wait_ge(S("y_added"), i * 2 + (r * KT + j + 1))
                    for s in range(2):
                        unit_ready(eng, s, i * 2 + (st.m0 + j))
                        if s:
                            for parity in range(2):
                                eng.wait_ge(S(f"inner_split{parity}"), (r + 1) * FT + 1)
                        for k in range(FH):
                            f = s * FH + k
                            w = slice(k * P, (k + 1) * P)
                            mm = split_product(eng, 2 * j, whi[s][:, w], wlo[s][:, w], gh[:, f], gl[:, f],
                                               HALF, f == 0, f == FT - 1)
                        mm.then_inc(used[s], 1)

        def act_ffn_out(eng, st, next_cols):
            pipelined(eng, st, lambda i, s: None, next_cols)

        def dve_ffn_out(eng, st, r):
            for s in range(2):
                eng.wait_ge(S(f"inner_split{s}"), (r + 1) * FT + 1)
            eng.memset(total[:], 0.0).then_inc(S("totalled"), 1)
            with eng.Fori(0, KT // 2) as i:
                for j in range(2):
                    eng.wait_ge(used[1], i * 2 + (st.m0 + j + 2))
                    row = y[:, bass.ds(i * 2 + j, 1)].rearrange("p a (h n) -> p (a h) n", h=2)
                    eng.scalar_tensor_tensor(row, two_halves(2 * j), 0.5 / ALPHA, row, ALU.mult, ALU.add)\
                       .then_inc(S("y_added"), 1)
                    eng.wait_ge(S("y_added"), i * 2 + (r * KT + j + 3))
                    eng.wait_ge(S("totalled"), i * 2 + ((2 * r) * (KT + 1) + j + 1))
                    eng.tensor_tensor(halves(total[:]), halves(total[:]), row, ALU.add).then_inc(S("totalled"), 1)

        def pe_norm(eng, n):
            eng.wait_ge(S("totalled"), (n + 1) * (KT + 1))
            for h in range(2):
                mm = eng.matmul(psum[:, 4 + h, 0:HALF], mean_w[:], total[:, h * HALF:(h + 1) * HALF],
                                start=True, stop=True)
            mm.then_inc(S("mean_done"), 1)
            for k in range(KT):
                eng.wait_ge(S("squared"), n * KT + k + 1)
                for h in range(2):
                    mm = eng.matmul(psum[:, 6 + h, 0:HALF], mean_w[:], sq[k % 2][:, h * HALF:(h + 1) * HALF],
                                    start=k == 0, stop=k == KT - 1)
                mm.then_inc(S("square_summed"), 1)

        def act_norm(eng, n, gname, bname, split):
            eng.preload_act_table_set(LOG_EXP)
            for k in range(KT):
                eng.wait_ge(S("centred"), n * KT + k + 1)
                if n * KT + k >= 2:
                    eng.wait_ge(S("square_summed"), n * KT + k - 1)
                eng.activation(sq[k % 2][:], y[:, k], ACT.Square).then_inc(S("squared"), 1)
            eng.wait_ge(S("square_summed"), (n + 1) * KT)
            eng.activation(halves(total[:]), two_halves(6), ACT.Ln, bias=eps[:, 0:1]).then_inc(S("log_made"), 1)
            eng.wait_ge(S("log_made"), n + 1)
            eng.activation(rstd[:], total[:], ACT.Exp, scale=-0.5).then_inc(S("rstd_made"), 1)
            for k in range(KT):
                eng.wait_ge(S("scaled"), n * KT + k + 1)
                if split:
                    eng.activation(xh[:, k, 0:T], y[:, k], ACT.Identity, bias=vec(bname, k))\
                       .then_inc(S("norm_hi"), 1)
                    eng.wait_ge(S("norm_hi"), n * KT + k + 1)
                eng.activation(y[:, k], y[:, k], ACT.Identity, bias=vec(bname, k)).then_inc(S("normed"), 1)

        def dve_norm(eng, n, gname, split):
            eng.wait_ge(S("mean_done"), n + 1)
            for k in range(KT):
                eng.tensor_tensor(halves(y[:, k]), halves(y[:, k]), two_halves(4), ALU.subtract)\
                   .then_inc(S("centred"), 1)
            eng.wait_ge(S("rstd_made"), n + 1)
            eng.wait_ge(S("centred"), (n + 1) * KT)

            def low(k):
                eng.wait_ge(S("normed"), n * KT + k + 1)
                eng.tensor_tensor(xl[:, k, 0:T], y[:, k], xh[:, k, 0:T].bitcast(F32), ALU.subtract)\
                   .then_inc(S("norm_lo"), 1)

            for k in range(KT):
                eng.scalar_tensor_tensor(y[:, k], y[:, k], vec(gname, k), rstd[:], ALU.mult, ALU.mult)\
                   .then_inc(S("scaled"), 1)
                if split and k >= 2:
                    low(k - 2)
            if split:
                low(KT - 2)
                low(KT - 1)

        n_r = Region(y_r.start, y_r.end - y_r.start)
        ldec = n_r.tensor("ldec", [P, HP, T])
        logp = n_r.tensor("logp", [P, HP, T])
        norms = Region(y_r.start + 4 * HP * T, 4 * HP * T).tensor("norms", [P, HP, T])
        y_scale = Region(y_r.start + 4 * HP * T, 4 * HP * T).tensor("y_scale", [P, HP, T])
        c_r = Region(temp_at, temp_bytes)
        cst = c_r.tensor("cst", [P, NCST - N_MASKS])
        k_share_at = c_r.at
        k_share = c_r.tensor("k_share", [P, T])
        e_inv = c_r.tensor("e_inv", [P, HP, P])
        z_r = Region(ring_at, temp_at - ring_at)
        masks = z_r.tensor("masks", [P, N_MASKS])
        prep_at = z_r.at
        scores = z_r.tensor("scores", [P, NH, 4, P])
        dm = [z_r.tensor(f"inv{g}", [P, 4, P]) for g in range(2)]
        dt = [z_r.tensor(f"inv_t{g}", [P, 4, P]) for g in range(2)]
        wm = [z_r.tensor(f"carry{g}", [P, 4, P]) for g in range(2)]
        em = [z_r.tensor(f"blocks{g}", [P, 4, P]) for g in range(2)]
        e_in = z_r.tensor("e_in", [P, HP, P])
        tok = z_r.tensor("tok", [P, 3, 512])
        qb_even = z_r.tensor("qb_even", [P, 2, NB, NH, DS])
        tmp_s = wm[0]
        a_r = Region(split_at, split_r.end - split_r.start)
        ar = a_r.tensor("ar", [P, HP, 2, 2, P])
        bk = a_r.tensor("bk", [P, 2, HP, P])
        state = a_r.tensor("state", [P, HP, P])
        end_w = a_r.tensor("end_w", [P, HP, P])
        vf = end_w
        sums_at = a_r.at
        k_pages = [a_r.tensor(f"k_pages{s}", [P, 2, HP, 2 * PAGE]) for s in range(2)]
        qb_odd = a_r.tensor("qb_odd", [P, 2, NB, NH, DS])
        qb = [q[:, n] for n in range(2) for q in (qb_even, qb_odd)]
        a_r = Region(sums_at, split_r.end - sums_at)
        lp = a_r.tensor("lp", [P, 2, PAST + DS])
        cp = a_r.tensor("cp", [P, 2, PAST + DS])
        xs, sas = dm[0], dm[1]
        t_r = Region(prep_at, z_r.end - prep_at)
        t2 = t_r.tensor("t2", [P, HP, T])
        t_r.at += 4 * HP * T
        t3 = t_r.tensor("t3", [P, HP, T])
        t1 = t_r.tensor("t1", [P, HP, T])
        s_r = Region(prep_at + 4 * 2 * 4 * P, 4 * 6 * 4 * P)
        state_s = s_r.tensor("state_s", [P, HP, NB, HD])
        own_x = s_r.tensor("own_x", [P, 2, NB, HD])
        q_r = Region(y_r.start, 4 * HP * T)
        own_v = q_r.tensor("own_v", [P, 2, NB, HD])
        x_red = q_r.tensor("x_red", [P, 2, 2, HD])
        e_in_s = q_r.tensor("e_in_s", [P, HP, TS])
        p_r = Region(big_at, 12 * TX * 4)
        zs = [p_r.tensor(f"zs{s}", [P, 10 * P]) for s in range(2)]
        ls_at = p_r.at
        ls = [p_r.tensor(f"ls{s}", [P, 10 * P]) for s in range(2)]
        p_r.at = ls_at
        l_lo = [p_r.tensor(f"l_lo{s}", [P, 10 * P], F32R) for s in range(2)]
        ob = [p_r.tensor(f"ob{s}", [P, SEQ]) for s in range(2)]
        k_r = Region(z_r.start, z_r.end - z_r.start)
        pages = [k_r.tensor(f"pages{s}", [P, 4, 512]) for s in range(4)]
        zsum = k_r.tensor("zsum", [P, 512])
        a_self_t = k_r.tensor("a_self_t", [TS, 2, P])
        a_t = k_r.tensor("a_t", [P, 2, N_PAGES, P])
        zs.append(k_r.tensor("zs2", [P, 10 * P]))
        q_r = Region(big_end - 4 * 1536, 4 * 1536)
        q_pad = [q_r.tensor(f"q_pad{s}", [P, SEQ]) for s in range(2)]
        l_hi_diag = q_r.tensor("l_hi_diag", [P, 4 * P], F32R)
        l_hi_rest = Region(k_share_at, temp_at + temp_bytes - k_share_at).tensor("l_hi_rest", [P, 6 * P], F32R)
        ones_suffix = p_r.tensor("ones_suffix", [P, 2 * P], F32R)

        def cc(name, n=P, skip=0):
            at = CST[name] + skip
            return cst[:, at:at + n] if at < NCST - N_MASKS else masks[:, at - (NCST - N_MASKS):at - (NCST - N_MASKS) + n]

        def bcast(a, n):
            return a.unsqueeze(1).broadcast_to([a.shape[0], n, a.shape[1]])

        def each(a, n):
            return a.unsqueeze(2).broadcast_to([a.shape[0], a.shape[1], n])

        def samples(a):
            return a.rearrange("p (b t) -> p b t", t=DS)

        class Count:
            def __init__(self, name):
                self.name, self.n = name, 0

            def up(self, ins):
                self.n += 1
                ins.then_inc(S(self.name), 1)
                return self.n

            def wait(self, eng, n=None):
                eng.wait_ge(S(self.name), self.n if n is None else n)

        dve_steps = Count("dve_steps")

        def pe_pairs(eng, st, made, tile_ready=None):
            with eng.Fori(0, st.n // 2) as i:
                for s in range(2):
                    unit_ready(eng, s, i + st.m0)
                    eng.wait_ge(S(f"{made}{s}"), i + 1)
                    w_hi = whi[s][:].rearrange("p (t k n) -> p t k n", t=2, k=KT)
                    w_lo = wlo[s][:].rearrange("p (t k n) -> p t k n", t=2, k=KT)
                    for t in range(2):
                        for k in range(KT):
                            if tile_ready and s == t == 0:
                                eng.wait_ge(*tile_ready(k))
                            mm = split_product(eng, 4 * s + 2 * t, w_hi[:, t, k], w_lo[:, t, k],
                                               xh[:, k], xl[:, k], HALFX, k == 0, k == KT - 1)
                    mm.then_inc(used[s], 1)

        def unit_banks(s, n=HALFX, rows=P):
            return psum[0:rows, 4 * s:4 * s + 4, 0:n]

        def act_pairs(eng, st, made, tile0, func_of, next_cols, next_ready=None):
            def work(i, s):
                eng.wait_ge(used[s], i + (st.m0 + 2))
                first = i * 4 + (tile0 + 2 * s)
                tiles = bass.ds(first, 2) if not isinstance(first, int) else slice(first, first + 2)
                dst = proj[:, tiles].rearrange("p t (h n) -> p (t h) n", h=2)
                eng.activation(dst, unit_banks(s), func_of).then_inc(S(f"{made}{s}"), 1)
            pipelined(eng, st, work, next_cols, next_ready)

        def mid_unit(q):
            return q % 2, stages["mid"].m0 + q // 2

        def pe_mid(eng):
            for q in range(3):
                s, m = mid_unit(q)
                n = P if q == 0 else GL
                unit_ready(eng, s, m)
                eng.wait_ge(S(f"rkv_made{s}"), 3 + 1)
                if q == 2:
                    eng.wait_ge(S("lora_copied"), 1)
                for t in range(2):
                    for k in range(KT):
                        w = slice((t * KT + k) * n, (t * KT + k + 1) * n)
                        mm = split_product(eng, 4 * s + 2 * t, whi[s][:, w], wlo[s][:, w], xh[:, k], xl[:, k],
                                           HALFX, k == 0, k == KT - 1, rows=n)
                mm.then_inc(used[s], 1)
            eng.wait_ge(S("lora_copied"), 3)
            for q in range(3, 6):
                s, m = mid_unit(q)
                unit_ready(eng, s, m)
                for j in range(3 if q < 5 else 2):
                    k = 3 * (q - 3) + j
                    w = slice(j * 512, (j + 1) * 512)
                    for tt in range(NT + 1):
                        rows = P if tt < NT else TS
                        c = slice(tt * P, tt * P + rows)
                        for n, (a, b) in enumerate(((xh, whi), (xh, wlo), (xl, whi))):
                            mm = eng.matmul(psum[0:rows, tt, :], a[:, k, c], b[s][:, w],
                                            start=k == 0 and n == 0, stop=k == KT - 1 and n == 2)
                mm.then_inc(used[s], 1)

        def act_mid(eng):
            st = stages["mid"]
            for q in range(3):
                s, m = mid_unit(q)
                ns, nm = mid_unit(q + 1)
                if q < 2:
                    make_hi(eng, ns, nm, MID_COLS[q + 1], (S("lora_weights"), q + 2))
                else:
                    make_hi(eng, ns, nm, MID_COLS[q + 1])
                rows = P if q == 0 else GL
                eng.wait_ge(used[s], m + 2)
                eng.activation(lora[0:rows, 2 * q:2 * q + 2].rearrange("p t (h n) -> p (t h) n", h=2),
                               unit_banks(s, rows=rows), ACT.Copy).then_inc(S("lora_copied"), 1)
            for q in range(4, 6):
                s, m = mid_unit(q)
                make_hi(eng, s, m, MID_COLS[q])
            eng.wait_ge(S("lora_summed"), 8)
            eng.activation(lora_wa[0:HD], lora_wa[0:HD], ACT.Tanh).then_inc(S("lora_inner"), 1)
            eng.wait_ge(S("lora_summed"), 24)
            eng.activation(lora_g[:], lora_g[:], ACT.Sigmoid).then_inc(S("lora_inner"), 1)
            make_hi(eng, 0, stages["qk"].m0, stages["qk"].cols)
            for f in range(HP):
                eng.wait_ge(S("k_scaled"), f + 1)
                eng.activation(squares[:, f], kk[:, f], ACT.Square).then_inc(S("k_squared"), 1)
            eng.wait_ge(used[1], st.m0 + 3 + 1)
            eng.activation(vt[:, 0:NT], psum[:, 0:NT, :], ACT.Copy).then_inc(S("v_made"), 1)
            eng.activation(vt[0:TS, NT], psum[0:TS, NT, :], ACT.Copy).then_inc(S("v_made"), 1)

        def dve_lora_weights(eng):
            c = dve_steps
            for q in range(3):
                s, m = mid_unit(q)
                n = P if q == 0 else GL
                eng.wait_ge(landed[s], (m + 1) * 16)
                w = raw[s][:, 0:KT * n].rearrange("p (k n) -> p k n", k=KT)
                mw = raw[s][:, KT * n:2 * KT * n].rearrange("p (k n) -> p k n", k=KT)
                parts = (("mu_w", 0, HD), ("mu_a", HD, HD)) if q == 0 else (("mu_g", 0, GL),)
                for name, at, width in parts:
                    mu = each(vecs[:, VEC[name]:VEC[name] + KT], width)
                    c.up(eng.tensor_tensor(mw[:, :, at:at + width], w[:, :, at:at + width], mu, ALU.mult))
                c.wait(eng)
                eng.tensor_tensor(w, w, mw, ALU.subtract).then_inc(S("lora_weights"), 1)

        def dve_shift(eng):
            c = dve_steps
            for grp in range(3):
                for s in range(2):
                    eng.wait_ge(S(f"rkv_made{s}"), grp + 2)
                p = proj[:, 4 * grp:4 * grp + 4]
                c.up(eng.tensor_tensor(temp_diff[:, :, 1:SEQ], p[:, :, 0:SEQ - 1], p[:, :, 1:SEQ], ALU.subtract))
                c.up(eng.tensor_scalar(temp_diff[:, :, 0:1], p[:, :, 0:1], -1.0, None, ALU.mult))
                for f in range(4):
                    ps, d = samples(p[:, f, SEQ:T]), samples(temp_diff[:, f, SEQ:T])
                    c.up(eng.tensor_tensor(d[:, :, 1:DS], ps[:, :, 0:DS - 1], ps[:, :, 1:DS], ALU.subtract))
                    c.up(eng.tensor_tensor(d[:, :, 0], p[:, f, T:TX], ps[:, :, 0], ALU.subtract))
                c.wait(eng)
                for f in range(4):
                    c.up(eng.scalar_tensor_tensor(p[:, f, 0:T], temp_diff[:, f], vec("mu_rkv", 4 * grp + f),
                                                  p[:, f, 0:T], ALU.mult, ALU.add))
                c.wait(eng)
            return c

        def dve_lora_sum(eng):
            for q in range(3):
                eng.wait_ge(S("lora_copied"), q + 1)
                rows = P if q == 0 else GL
                a, b = lora[0:rows, 2 * q], lora[0:rows, 2 * q + 1]
                o = lora_wa[:] if q == 0 else lora_g[:, q - 1]
                sa, so = samples(a[:, SEQ:T]), samples(o[:, SEQ:T])
                sb_ = samples(b[:, SEQ:T])
                for step in (eng.tensor_tensor(o[:, 1:SEQ], a[:, 1:SEQ], b[:, 0:SEQ - 1], ALU.add),
                             eng.tensor_copy(o[:, 0:1], a[:, 0:1]),
                             eng.tensor_tensor(so[:, :, 1:DS], sa[:, :, 1:DS], sb_[:, :, 0:DS - 1], ALU.add),
                             eng.tensor_tensor(so[:, :, 0], sa[:, :, 0], b[:, T:TX], ALU.add)):
                    step.then_inc(S("lora_summed"), 2)

        def wait_w_in(eng):
            for s in range(2):
                eng.wait_ge(used[s], stages["qk"].m0 + 2 + 1)

        def prep_bank(n):
            return (6, 0, 2)[n % 3]

        def pe_prep(eng):
            def start(n):
                if n == 1:
                    eng.wait_ge(S("v_made"), 2)
                if n >= 3:
                    eng.wait_ge(*(step("k_norm", n - 2) if n - 3 < HP else step("lora_out", n - 2 - HP)))
                return prep_bank(n)
            eng.wait_ge(S("cst_loaded"), 16)
            for f in range(HP):
                bank = start(f)
                eng.wait_ge(*step("k_squared", f + 1))
                for h in range(2):
                    mm = eng.matmul(psum[:, bank + h, 0:HALF], cc("pair"), squares[:, f, h * HALF:(h + 1) * HALF],
                                    start=True, stop=True)
                mm.then_inc(S("k_summed"), 1)
            eng.wait_ge(S("lora_inner"), 2)
            eng.wait_ge(S("inner2_loaded"), 48)
            for f in range(HP):
                c = slice(f * P, (f + 1) * P)
                for q, parts in enumerate((((inner2[0:HD, c], lora_wa[0:HD]),), ((inner2[HD:P, c], lora_wa[HD:P]),),
                                           ((inner2g[:, 0, c], lora_g[:, 0]), (inner2g[:, 1, c], lora_g[:, 1])))):
                    bank = start(HP + 3 * f + q)
                    for h in range(2):
                        for n, (w, a) in enumerate(parts):
                            mm = eng.matmul(psum[:, bank + h, 0:HALF], w, a[:, h * HALF:(h + 1) * HALF],
                                            start=n == 0, stop=n == len(parts) - 1)
                    mm.then_inc(S("lora_second"), 1)
            eng.wait_ge(*step("lora_out", 3 * HP))

        def act_prep(eng):
            eng.wait_ge(S("h_stored"), 16)
            for f in range(HP):
                eng.wait_ge(*step("k_summed", f + 1))
                eng.activation(halves(norms[:, f]), two_halves(prep_bank(f)), ACT.Sqrt).then_inc(S("k_norm"), 1)
            for f in range(HP):
                for q, (dst, func, bias) in enumerate(((ldec, ACT.Sigmoid, vec("w0", f)),
                                                       (a_b, ACT.Sigmoid, vec("a0", f)), (g_out, ACT.Copy, 0.0))):
                    eng.wait_ge(*step("lora_second", 3 * f + q + 1))
                    eng.activation(halves(dst[:, f]), two_halves(prep_bank(HP + 3 * f + q)), func, bias=bias)\
                       .then_inc(S("lora_out"), 1)

        def dve_keys(eng):
            for f in range(HP):
                eng.tensor_scalar(kk[:, f], proj[:, 4 + f, 0:T], vec("k_k", f), None, ALU.mult)\
                   .then_inc(S("k_scaled"), 1)
            dve_steps.up(eng.tensor_scalar(one_less[:], vecs[:, VEC["k_a"]:VEC["k_a"] + HP], -1.0, 1.0, ALU.mult, ALU.add))

        def dve_prep(eng):
            c = dve_steps
            for f in range(HP):
                eng.wait_ge(*step("k_norm", f + 1))
                c.up(eng.tensor_scalar(norms[:, f], norms[:, f], 1e-12, None, ALU.max))
                c.wait(eng)
                c.up(eng.reciprocal(norms[:, f], norms[:, f]))
                c.wait(eng)
                c.up(eng.tensor_tensor(kk[:, f], kk[:, f], norms[:, f], ALU.mult))
            for f in range(HP):
                eng.wait_ge(*step("lora_out", 3 * f + 3))
                c.up(eng.tensor_scalar(ldec[:, f], ldec[:, f], DECAY, None, ALU.mult))
                c.wait(eng)
                c.up(eng.tensor_tensor_scan(logp[:, f], cc("keep", T), ldec[:, f], 0.0, ALU.mult, ALU.add))
                c.up(eng.tensor_scalar(k_share[:], a_b[:, f], vec("k_a", f), one_less[:, f:f + 1], ALU.mult, ALU.add))
                c.wait(eng)
                c.up(eng.tensor_tensor(ldec[:, f], logp[:, f], ldec[:, f], ALU.subtract))
                c.up(eng.tensor_tensor(proj[:, 4 + f, 0:T], proj[:, 4 + f, 0:T], k_share[:], ALU.mult))
                c.up(eng.tensor_tensor(a_b[:, f], kk[:, f], a_b[:, f], ALU.mult))
                c.wait(eng)
            wait_w_in(eng)
            c.up(eng.memset(ar[:], 0.0))
            c.wait(eng)
            eng.memset(state[:], 0.0).then_inc(S("prep_done"), 1)

        def c_rows(c):
            return slice(c * CH, (c + 1) * CH)

        def par_rows(h):
            return slice(h % 2 * HD, h % 2 * HD + HD)

        def over_tiles(eng, body):
            with eng.Fori(0, NT - 1) as i:
                body(i, False)
            body(NT - 1, True)

        def cols_at(at, n=P):
            return slice(at, at + n) if isinstance(at, int) else bass.ds(at, n)

        SCORE_BANKS = (4, 5, 3, 6)
        SCALED = 6

        def act_wkv(eng):
            def decays(tile):
                cols = cols_at(tile * P)
                eng.activation(e_in[:], logp[:, :, cols], ACT.Exp).then_inc(S("decays"), 1)
                eng.activation(e_ex[:], ldec[:, :, cols], ACT.Exp).then_inc(S("decays"), 1)
                eng.activation(e_inv[:], logp[:, :, cols], ACT.Exp, scale=-1.0).then_inc(S("decays"), 1)

            def body(i, last_tile):
                for n, q in enumerate((0, 1, 2)):
                    eng.wait_ge(S("turned"), i * 3 + (n + 1))
                    eng.activation(tok[:, q], psum[:, q, :], ACT.Copy).then_inc(S("tok_made"), 1)
                for l in range(1, LEVELS):
                    for g in range(2):
                        eng.wait_ge(S(f"carry_done{g}"), i * LEVELS + (l + 1))
                        eng.activation(wm[g][:].rearrange("p h n -> p (h n)"), psum[:, 3 * g, :], ACT.Copy)\
                           .then_inc(S(f"carry_made{g}"), 1)
                eng.wait_ge(S("state_made"), i * 2 + 1)
                eng.activation(ends[:], logp[:, :, cols_at(i * P)].rearrange("p h (c n) -> p h c n", c=2)[:, :, :, CH - 1],
                               ACT.Exp).then_inc(S("ends_made"), 1)
                if not last_tile:
                    eng.wait_ge(S("wkv_scaled"), i * SCALED + SCALED)
                    decays(i + 1)
                for c in range(2):
                    eng.wait_ge(S("rhs_done"), i * 2 + (c + 1))
                    eng.activation(xs[c_rows(c)].rearrange("p h n -> p (h n)"), psum[c_rows(c), 6, :], ACT.Copy)\
                       .then_inc(S("rhs_made"), 1)
                    eng.wait_ge(S("sa_done"), i * 2 + (c + 1))
                    eng.activation(sas[c_rows(c)].rearrange("p h n -> p (h n)"), psum[c_rows(c), 3, :], ACT.Copy)\
                       .then_inc(S("sa_made"), 1)
                eng.wait_ge(S("y_done"), i + 2)
                eng.activation(kk[:, :, cols_at(i * P)], psum[:, 0, :].rearrange("p (h n) -> p h n", h=HP), ACT.Copy)\
                   .then_inc(S("y_made"), 1)

            eng.wait_ge(S("prep_done"), 1)
            decays(0)
            over_tiles(eng, body)

        def pool_wkv(eng):
            def body(i, last_tile):
                eng.wait_ge(S("state_made"), i * 2 + 1)
                eng.tensor_copy(vf[:], proj[:, 8:12, cols_at(i * P)]).then_inc(S("v_copied"), 1)
                for l in range(LEVELS):
                    for g in range(2):
                        if l == 0:
                            eng.wait_ge(S("masked"), i * NH + (4 * g + 4))
                        else:
                            eng.wait_ge(S(f"carry_done{g}"), i * LEVELS + l)
                            if l == 1:
                                eng.wait_ge(S(f"inv_made{g}"), i * 11 + 1)
                        eng.tensor_tensor(em[g][:], scores[:, 4 * g:4 * g + 4, 0], bcast(cc("level", P, l * P), 4),
                                          ALU.mult).then_inc(S(f"mask_made{g}"), 1)
                    if l == 1:
                        eng.wait_ge(S("wkv_scaled"), i * SCALED + SCALED)
                        eng.wait_ge(S("y_done"), i + 1)
                        eng.tensor_tensor(ar_late[:], ar[:, :, 0], ar[:, :, 1], ALU.add).then_inc(S("ar_copied"), 1)
                for c in range(2):
                    eng.wait_ge(S("state_made"), i * 2 + (c + 1))
                    eng.wait_ge(S("turned"), i * 3 + 3)
                    eng.wait_ge(S("ends_made"), i + 1)
                    eng.tensor_tensor(end_w[:], bcast(cc("pair"), HP), each(ends[:, :, c], P),
                                      ALU.mult).then_inc(S("end_made"), 1)

            eng.wait_ge(S("prep_done"), 1)
            eng.wait_ge(S("masks_loaded"), 16)
            over_tiles(eng, body)

        def dve_self_scores(eng):
            c = dve_steps
            eng.wait_ge(S("self_scored"), 1)
            for g in range(2):
                own = cc("own_rows", NB, g * NB)
                eng.tensor_tensor(own_self[:, g], psum[:, 7, g * TS:(g + 1) * TS].rearrange("p (b t) -> p b t", t=DS),
                                  each(own, DS), ALU.mult).then_inc(S("self_read"), 1)
                eng.wait_ge(S("self_read"), g + 1)
                c.up(eng.tensor_reduce(self4[:], own_self[:, g].rearrange("p b t -> p t b"), AX.X, ALU.add))
                c.wait(eng)
                for t in range(DS):
                    c.up(eng.tensor_scalar(zp[:, g, DS - 1 - t:DS - t], self4[:, t:t + 1], SCALE,
                                           vec("sb_bias_rows", 0), ALU.mult, ALU.add))
                c.wait(eng)
            eng.sem_inc(S("z_read"), 1)

        def dve_wkv(eng):
            def scaled(tile):
                cols = cols_at(tile * P)
                eng.wait_ge(S("decays"), tile * 3 + 3)
                for par in range(2):
                    rows = par_rows(par)
                    eng.tensor_tensor(ar[rows, :, par, 1], proj[rows, 0:4, cols], e_in[rows], ALU.mult)\
                       .then_inc(S("wkv_scaled"), 1)
                    eng.scalar_tensor_tensor(ar[rows, :, par, 0], kk[rows, :, cols], -1.0, e_ex[rows], ALU.mult,
                                             ALU.mult).then_inc(S("wkv_scaled"), 1)
                eng.tensor_tensor(bk[:, 0], a_b[:, :, cols], e_inv[:], ALU.mult).then_inc(S("wkv_scaled"), 1)
                eng.tensor_tensor(bk[:, 1], proj[:, 4:8, cols], e_inv[:], ALU.mult).then_inc(S("wkv_scaled"), 1)

            def body(i, last_tile):
                for n in range(NH):
                    hp, x = n // 2, n % 2
                    eng.wait_ge(S("scored"), i * NH + (n + 1))
                    eng.tensor_tensor(scores[:, 2 * hp:2 * hp + 2, 2 * x:2 * x + 2].rearrange("p h y n -> p h (y n)"),
                                      psum[:, SCORE_BANKS[n % 4], :].rearrange("p (h n) -> p h n", h=2),
                                      bcast(cc("score", 2 * P), 2), ALU.mult).then_inc(S("masked"), 1)
                ident = bcast(cc("ident"), 4)
                for g in range(2):
                    eng.wait_ge(S(f"mask_made{g}"), i * LEVELS + 1)
                    eng.tensor_tensor(dt[g][:], em[g][:], ident, ALU.add).then_inc(S(f"inv_made{g}"), 1)
                    eng.wait_ge(S(f"carry_done{g}"), i * LEVELS + 1)
                    eng.tensor_tensor(dm[g][:], psum[:, 3 * g, :].rearrange("p (h n) -> p h n", h=4), ident,
                                      ALU.add).then_inc(S(f"inv_made{g}"), 1)
                for l in range(1, LEVELS):
                    for g in range(2):
                        eng.wait_ge(S(f"grown{g}"), i * (LEVELS - 1) + l)
                        eng.wait_ge(S(f"inv_made{g}"), i * 11 + 2 * l)
                        if l < LEVELS - 1:
                            eng.tensor_tensor(dm[g][:], psum[:, 3 * g + 1, :].rearrange("p (h n) -> p h n", h=4),
                                              dm[g][:], ALU.add).then_inc(S(f"inv_made{g}"), 1)
                        eng.tensor_tensor(dt[g][:], psum[:, 3 * g + 2, :].rearrange("p (h n) -> p h n", h=4),
                                          dt[g][:], ALU.add).then_inc(S(f"inv_made{g}"), 1)
                if not last_tile:
                    eng.wait_ge(S("ar_copied"), i + 1)
                    eng.wait_ge(S("turned"), i * 3 + 3)
                    scaled(i + 1)
                for c in range(2):
                    eng.wait_ge(S("update_done"), i * 2 + (c + 1))
                    eng.tensor_tensor(tmp_s[:], psum[:, 1 + c, :].rearrange("p (h n) -> p h n", h=HP), state[:],
                                      ALU.add).then_inc(S("state_summed"), 1)
                    eng.wait_ge(S("state_summed"), i * 2 + (c + 1))
                    eng.wait_ge(S("end_made"), i * 2 + (c + 1))
                    eng.tensor_tensor(state[:], tmp_s[:], end_w[:], ALU.mult).then_inc(S("state_made"), 1)
                    if c == 1:
                        for n in range(2):
                            eng.wait_ge(S(f"k_pages_used{n}"), i * 2 + 3)
                        eng.tensor_scalar(zp[:, :, cols_at(i * 256 + DS, 256)],
                                          psum[:, 7, :].rearrange("p (g n) -> p g n", g=2),
                                          SCALE, vec("sb_bias_rows", 0), ALU.mult, ALU.add).then_inc(S("z_read"), 1)

            scaled(0)
            dve_self_scores(eng)
            eng.wait_ge(S("masks_loaded"), 16)
            over_tiles(eng, body)

        def pe_k_unit(eng, i, n):
            if n == 0:
                eng.wait_ge(S("z_read"), i + 1)
            eng.wait_ge(S(f"k_pages_loaded{n % 2}"), i * 128 + 64 * (n // 2 + 1))
            for b in (2 * n, 2 * n + 1):
                g, rows = b // 4, slice(b % 4 * 32, b % 4 * 32 + 32)
                for hp in range(HP):
                    mm = eng.matmul(psum[rows, 7, g * 256:(g + 1) * 256], qb[hp][:, b].rearrange("p h t -> p (h t)"),
                                    k_pages[n % 2][:, b % 2, hp], start=g == 0 and hp == 0, stop=hp == HP - 1,
                                    skip_group_check=True)
            mm.then_inc(S(f"k_pages_used{n % 2}"), 1)

        def pe_self_scores(eng):
            eng.wait_ge(S("qb_made"), 2 + NH)
            for s in range(2):
                eng.wait_ge(S(f"qk_made{s}"), 3)
            for g in range(2):
                for hp in range(HP):
                    mm = eng.matmul(psum[:, 7, g * TS:(g + 1) * TS],
                                    qb[hp][:, 4 * g:4 * g + 4].rearrange("p b h t -> p (b h t)"),
                                    proj[:, 16 + hp, SEQ:T], start=g == 0 and hp == 0, stop=hp == HP - 1,
                                    skip_group_check=True)
            mm.then_inc(S("self_scored"), 1)

        def pe_wkv(eng):
            pe_self_scores(eng)
            eng.wait_ge(S("prep_done"), 1)
            k = dict(skip_group_check=True)
            flat_of = lambda a: a[:].rearrange("p h n -> p (h n)")

            def body(i, last_tile):
                eng.wait_ge(S("wkv_scaled"), i * SCALED + SCALED)
                for n in range(NH):
                    hp, x = n // 2, n % 2
                    if n >= 4:
                        eng.wait_ge(S("masked"), i * NH + (n - 3))
                    eng.matmul(psum[:, SCORE_BANKS[n % 4], :], bk[:, x, hp], ar[:, hp].rearrange("p a b n -> p (a b n)"),
                               start=True, stop=True, **k).then_inc(S("scored"), 1)
                pe_k_unit(eng, i, 0)
                eng.wait_ge(S("v_copied"), i + 1)
                eng.wait_ge(S("y_made"), i + 1)
                eng.wait_ge(S("state_made"), i * 2 + 1)
                for q, a in enumerate((vf, bk[:, 0], bk[:, 1])):
                    for hp in range(HP):
                        mm = eng.transpose(psum[:, q, hp * P:(hp + 1) * P], a[:, hp], cc("ident"))
                    mm.then_inc(S("turned"), 1)
                for g in range(2):
                    eng.wait_ge(S(f"mask_made{g}"), i * LEVELS + 1)
                    eng.wait_ge(S("masked"), i * NH + NH)
                    eng.wait_ge(S("tok_made"), i * 3 + 1)
                    for j in range(4):
                        mm = eng.matmul(psum[:, 3 * g, j * P:(j + 1) * P], em[g][:, j], cc("ident"),
                                        start=j == 0, stop=True, **k)
                    mm.then_inc(S(f"carry_done{g}"), 1)
                eng.wait_ge(S("tok_made"), i * 3 + 3)
                for l in range(1, LEVELS):
                    if l == 1:
                        pe_k_unit(eng, i, 1)
                    for g in range(2):
                        eng.wait_ge(S(f"mask_made{g}"), i * LEVELS + (l + 1))
                        eng.wait_ge(S(f"inv_made{g}"), i * 11 + (2 * l - (l > 1)))
                        for j in range(4):
                            mm = eng.matmul(psum[:, 3 * g, j * P:(j + 1) * P], em[g][:, j], dm[g][:, j],
                                            start=j == 0, stop=True, **k)
                        mm.then_inc(S(f"carry_done{g}"), 1)
                    if l == LEVELS - 1:
                        for h in range(NH):
                            n = slice(h * HD, (h + 1) * HD)
                            eng.matmul(psum[:, 6, n], scores[:, h, 2], tok[:, 0, n], start=h == 0, stop=False, **k)
                    for g in range(2):
                        eng.wait_ge(S(f"carry_made{g}"), i * (LEVELS - 1) + l)
                        eng.wait_ge(S(f"inv_made{g}"), i * 11 + 2 * l)
                        if l < LEVELS - 1:
                            for j in range(4):
                                eng.matmul(psum[:, 3 * g + 1, j * P:(j + 1) * P], dt[g][:, j], wm[g][:, j],
                                           start=j == 0, stop=True, **k)
                        for j in range(4):
                            mm = eng.matmul(psum[:, 3 * g + 2, j * P:(j + 1) * P], wm[g][:, j], dt[g][:, j],
                                            start=j == 0, stop=True, **k)
                        mm.then_inc(S(f"grown{g}"), 1)
                eng.wait_ge(S("ar_copied"), i + 1)
                for c in range(2):
                    cr = c_rows(c)
                    eng.wait_ge(S("state_made"), i * 2 + (c + 1))
                    for hp in range(HP):
                        mm = eng.matmul(psum[cr, 6, hp * P:(hp + 1) * P], ar_late[:, hp, 0, cr], state[:, hp],
                                        start=False, stop=True, **k)
                    mm.then_inc(S("rhs_done"), 1)
                    for hp in range(HP):
                        eng.matmul(psum[:, 0, hp * P + c * CH:hp * P + (c + 1) * CH], state[:, hp],
                                   ar_late[:, hp, 1, cr], start=c == 0 and hp == 0, stop=False, **k)
                    if c == 0:
                        for h in range(NH):
                            eng.matmul(psum[par_rows(h), 0, h // 2 * P:(h // 2 + 1) * P],
                                       tok[:, 0, h * HD:(h + 1) * HD], scores[:, h, 3], start=False, stop=False, **k)
                        for g in range(2):
                            eng.wait_ge(S(f"inv_made{g}"), i * 11 + 11)
                    eng.wait_ge(S("rhs_made"), i * 2 + (c + 1))
                    for h in range(NH):
                        mm = eng.matmul(psum[cr, 3, h * HD:(h + 1) * HD], dt[h // 4][:, h % 4, cr],
                                        flat_of(xs)[:, h * HD:(h + 1) * HD], start=h == 0, stop=True, **k)
                    mm.then_inc(S("sa_done"), 1)
                    for hp in range(HP):
                        n = slice(hp * P, (hp + 1) * P)
                        eng.matmul(psum[:, 1 + c, n], tok[cr, 2, n], tok[cr, 0, n], start=hp == 0, stop=False, **k)
                    eng.wait_ge(S("sa_made"), i * 2 + (c + 1))
                    for hp in range(HP):
                        n = slice(hp * P, (hp + 1) * P)
                        mm = eng.matmul(psum[:, 1 + c, n], tok[cr, 1, n], flat_of(sas)[cr, n], start=False, stop=True, **k)
                    mm.then_inc(S("update_done"), 1)
                    if c == 0:
                        pe_k_unit(eng, i, 2)
                        pe_k_unit(eng, i, 3)
                for h in range(NH):
                    mm = eng.matmul(psum[par_rows(h), 0, h // 2 * P:(h // 2 + 1) * P],
                                    flat_of(sas)[:, h * HD:(h + 1) * HD], scores[:, h, 1],
                                    start=False, stop=True, **k)
                mm.then_inc(S("y_done"), 1)

            over_tiles(eng, body)

        arf = ar_late[:].rearrange("p a b n -> p (a b n)")
        bkf = bk[:].rearrange("p a b n -> p (a b n)")
        tokf = tok[:].rearrange("p a n -> p (a n)")
        xsf, sasf = (t[:].rearrange("p h n -> p (h n)") for t in (xs, sas))
        y_tok = wm[1][:].rearrange("p h n -> p (h n)")[:, 0:P]
        s_cols = slice(SEQ, T)
        last = 2 * NT + 1

        def act_wkv_s(eng):
            eng.wait_ge(S("state_made"), last)
            for dst, src, sc in ((e_in_s[:], logp, 1.0), (e_ex[:, :, 0:TS], ldec, 1.0), (e_inv[:, :, 0:TS], logp, -1.0)):
                eng.activation(dst, src[:, :, s_cols], ACT.Exp, scale=sc).then_inc(S("decays"), 1)
            eng.preload_act_table_set(LOG_EXP)
            eng.wait_ge(S("z_read"), NT + 1)
            eng.wait_ge(S("y_made"), NT + 1)
            eng.activation(cp[:], zp[:], ACT.Relu).then_inc(S("soft_p"), 1)
            eng.activation(lp[:], zp[:], ACT.Abs).then_inc(S("soft_p"), 1)
            eng.wait_ge(S("soft_p"), 2)
            eng.activation(lp[:], lp[:], ACT.Exp, scale=-1.0).then_inc(S("soft_p"), 1)
            eng.wait_ge(S("soft_p"), 3)
            eng.activation(lp[:], lp[:], ACT.Ln, bias=1.0).then_inc(S("soft_p"), 1)
            eng.wait_ge(*step("s_turned", 1))
            eng.activation(tokf[:, 0:3 * P], psum[:, 4, 0:3 * P], ACT.Copy).then_inc(S("s_tok"), 1)
            eng.wait_ge(*step("s_carry", 2))
            eng.activation(wm[0][:, 0:2].rearrange("p h n -> p (h n)"), psum[:, 5, 0:2 * P], ACT.Copy)\
               .then_inc(S("s_carry_made"), 1)
            eng.wait_ge(*step("s_sa", 1))
            eng.activation(sasf[:, 0:P], psum[:, 1, 0:P], ACT.Copy).then_inc(S("s_sa_made"), 1)
            eng.wait_ge(*step("s_y_turned", 1))
            eng.activation(kk[:, :, s_cols], psum[:, 1, 2 * P:3 * P].rearrange("p (h n) -> p h n", h=HP), ACT.Copy)\
               .then_inc(S("y_made"), 1)

        def pool_wkv_s(eng):
            eng.wait_ge(S("state_made"), last)
            eng.tensor_copy(vf[:].rearrange("p h n -> p (h n)")[:, 0:P].rearrange("p (h n) -> p h n", h=HP),
                            proj[:, 8:12, s_cols]).then_inc(S("s_v_copied"), 1)
            eng.wait_ge(*step("s_masked", 2))
            eng.wait_ge(*step("s_scaled", 4))
            for l in range(2):
                if l:
                    eng.wait_ge(*step("s_carry", 1))
                    eng.wait_ge(*step("s_inv", 2))
                eng.tensor_tensor(em[0][:, 0:2], scores[:, 0:2, 0],
                                  bcast(cc("level", P, l * P), 2),
                                  ALU.mult).then_inc(S("s_mask_made"), 1)

            eng.wait_ge(S("soft_p"), 4)
            eng.tensor_tensor(lp[:], lp[:], cp[:], ALU.add).then_inc(S("soft_p_made"), 1)
            eng.wait_ge(S("soft_p_made"), 1)
            eng.tensor_tensor(lp[:, :, 0:DS], lp[:, :, 0:DS], bcast(cc("self", DS), 2), ALU.mult)\
               .then_inc(S("soft_p_made"), 1)
            eng.wait_ge(S("sums_p"), 2)
            eng.tensor_tensor(zp[:], zp[:], cp[:], ALU.subtract).then_inc(S("soft_p_made"), 1)
            for q in q_pad:
                eng.memset(q[:], 0.0).then_inc(S("q_padded"), 1)
            eng.wait_ge(*step("s_state", HP))
            for hp in range(HP):
                eng.tensor_tensor(state_s[:, hp], state_s[:, hp], each(samples(e_in_s[:, hp])[:, :, DS - 1], HD),
                                  ALU.mult).then_inc(S("s_state_final"), 1)

        def dve_wkv_s(eng):
            r4 = lambda a: a.rearrange("p (h n) -> p h n", h=HP)
            eng.wait_ge(S("decays"), 3 * NT + 3)
            eng.scalar_tensor_tensor(r4(arf[:, 0:P]), kk[:, :, s_cols], -1.0, e_ex[:, :, 0:TS], ALU.mult, ALU.mult)\
               .then_inc(S("s_scaled"), 1)
            eng.tensor_tensor(r4(arf[:, P:2 * P]), proj[:, 0:4, s_cols], e_in_s[:], ALU.mult).then_inc(S("s_scaled"), 1)
            eng.tensor_tensor(r4(bkf[:, 0:P]), a_b[:, :, s_cols], e_inv[:, :, 0:TS], ALU.mult).then_inc(S("s_scaled"), 1)
            eng.tensor_tensor(r4(bkf[:, P:2 * P]), proj[:, 4:8, s_cols], e_inv[:, :, 0:TS], ALU.mult)\
               .then_inc(S("s_scaled"), 1)
            for pr in range(2):
                eng.wait_ge(*step("s_scored", pr + 1))
                eng.tensor_tensor(scores[:, pr].rearrange("p (x y) n -> p x (y n)", x=2),
                                  psum[:, pr, :].rearrange("p (x n) -> p x n", x=2),
                                  bcast(cc("score_s", 2 * P), 2), ALU.mult).then_inc(S("s_masked"), 1)
            ident = bcast(cc("ident"), 2)
            two = lambda a: a.rearrange("p (h n) -> p h n", h=2)
            eng.wait_ge(*step("s_mask_made", 1))
            eng.tensor_tensor(dt[0][:, 0:2], em[0][:, 0:2], ident, ALU.add).then_inc(S("s_inv"), 1)
            eng.wait_ge(*step("s_carry", 1))
            eng.tensor_tensor(dm[0][:, 0:2], two(psum[:, 5, 0:2 * P]), ident, ALU.add).then_inc(S("s_inv"), 1)
            c = dve_steps
            eng.wait_ge(*step("s_with_state", 1))
            own = each(cc("own", NB), HD)
            for kind, bank in ((0, 2), (1, 6)):
                for pr in range(2):
                    c.up(eng.tensor_tensor(own_x[:, pr], psum[:, bank + pr, :].rearrange("p (b i) -> p b i", b=NB),
                                           own, ALU.mult))
                    c.wait(eng)
                    c.up(eng.tensor_reduce(x_red[:, kind, pr], own_x[:, pr].rearrange("p b i -> p i b"), AX.X, ALU.add))
                    c.wait(eng)
            eng.wait_ge(*step("s_grown", 1))
            eng.tensor_tensor(dt[0][:, 0:2], two(psum[:, 5, 2 * P:4 * P]), dt[0][:, 0:2], ALU.add).then_inc(S("s_inv"), 1)
            eng.wait_ge(*step("s_ak", 1))
            eng.tensor_tensor(xsf[:, 0:P], psum[:, 0, 0:P], x_red[:, 0].rearrange("p a n -> p (a n)"), ALU.add)\
               .then_inc(S("s_rhs"), 1)
            eng.wait_ge(*step("s_tok", 1))
            for pr in range(2):
                eng.tensor_tensor(own_v[:, pr], bcast(tokf[:, pr * HD:(pr + 1) * HD], NB), own, ALU.mult)\
                   .then_inc(S("s_expanded"), 1)
            eng.wait_ge(*step("s_sa_made", 1))
            for pr in range(2):
                eng.tensor_tensor(own_x[:, pr], bcast(sasf[:, pr * HD:(pr + 1) * HD], NB), own, ALU.mult)\
                   .then_inc(S("s_expanded"), 1)
            eng.wait_ge(*step("s_y", 1))
            eng.tensor_tensor(y_tok, psum[:, 0, P:2 * P], x_red[:, 1].rearrange("p a n -> p (a n)"), ALU.add)\
               .then_inc(S("s_y_summed"), 1)
            eng.wait_ge(S("soft_p_made"), 2)
            for g in range(2):
                eng.tensor_tensor_scan(cp[:, g], cc("ones", 1).broadcast_to([P, PAST + DS]),
                                       lp[:, g], 0.0, ALU.mult, ALU.add).then_inc(S("sums_p"), 1)

        def dve_state_s(eng, hp):
            eng.wait_ge(*step("s_update", hp + 1))
            eng.tensor_tensor(state_s[:, hp].rearrange("p b i -> p (b i)"), psum[:, 4 + hp % 2, :],
                              state_s[:, hp].rearrange("p b i -> p (b i)"), ALU.add).then_inc(S("s_state"), 1)

        def pe_wkv_s(eng):
            k = dict(skip_group_check=True)
            eng.wait_ge(*step("s_scaled", 4))
            eng.wait_ge(S("y_made"), NT + 1)
            for pr in range(2):
                r = par_rows(pr)
                eng.matmul(psum[:, pr, 0:256], bkf[r, 0:P], arf[r, 0:2 * P], start=True, stop=True, **k)
                eng.matmul(psum[:, pr, 256:512], bkf[r, P:2 * P], arf[r, 0:2 * P], start=False, stop=True, **k)\
                   .then_inc(S("s_scored"), 1)
            eng.wait_ge(*step("s_v_copied", 1))
            for q, a in enumerate((vf[:].rearrange("p h n -> p (h n)")[:, 0:P], bkf[:, 0:P], bkf[:, P:2 * P])):
                mm = eng.transpose(psum[:, 4, q * P:(q + 1) * P], a, cc("ident"))
            mm.then_inc(S("s_turned"), 1)
            eng.wait_ge(S("state_loaded"), 16)
            for at, bank in ((0, 2), (P, 6)):
                for pr in range(2):
                    r = par_rows(pr)
                    for hp in range(HP):
                        rows = slice(hp * TS, (hp + 1) * TS)
                        mm = eng.matmul(psum[rows, bank + pr, :], arf[r, at + hp * TS:at + (hp + 1) * TS],
                                        state_s[r, hp].rearrange("p b i -> p (b i)"), start=True, stop=True, **k)
            mm.then_inc(S("s_with_state"), 1)
            eng.wait_ge(*step("s_mask_made", 1))
            for pr in range(2):
                mm = eng.matmul(psum[:, 5, pr * P:(pr + 1) * P], em[0][:, pr], cc("ident"), start=pr == 0, stop=True, **k)
            mm.then_inc(S("s_carry"), 1)
            eng.wait_ge(*step("s_mask_made", 2))
            eng.wait_ge(*step("s_inv", 2))
            for pr in range(2):
                mm = eng.matmul(psum[:, 5, pr * P:(pr + 1) * P], em[0][:, pr], dm[0][:, pr], start=pr == 0, stop=True, **k)
            mm.then_inc(S("s_carry"), 1)
            eng.wait_ge(*step("s_carry_made", 1))
            for pr in range(2):
                mm = eng.matmul(psum[:, 5, (2 + pr) * P:(3 + pr) * P], wm[0][:, pr], dt[0][:, pr],
                                start=pr == 0, stop=True, **k)
            mm.then_inc(S("s_grown"), 1)
            eng.wait_ge(*step("s_tok", 1))
            eng.wait_ge(*step("s_masked", 2))
            for pr in range(2):
                n = slice(pr * HD, (pr + 1) * HD)
                mm = eng.matmul(psum[:, 0, n], scores[:, pr, 2], tokf[:, n], start=pr == 0, stop=True, **k)
            mm.then_inc(S("s_ak"), 1)
            eng.wait_ge(*step("s_rhs", 1))
            eng.wait_ge(*step("s_inv", 3))
            for pr in range(2):
                n = slice(pr * HD, (pr + 1) * HD)
                mm = eng.matmul(psum[:, 1, n], dt[0][:, pr], xsf[:, n], start=pr == 0, stop=True, **k)
            mm.then_inc(S("s_sa"), 1)
            eng.wait_ge(*step("s_sa_made", 1))
            for pr in range(2):
                n, o = slice(pr * HD, (pr + 1) * HD), slice(P + pr * HD, P + (pr + 1) * HD)
                eng.matmul(psum[:, 0, o], scores[:, pr, 1], sasf[:, n], start=pr == 0, stop=False, **k)
                mm = eng.matmul(psum[:, 0, o], scores[:, pr, 3], tokf[:, n], start=False, stop=True, **k)
            mm.then_inc(S("s_y"), 1)
            eng.wait_ge(*step("s_y_summed", 1))
            eng.transpose(psum[:, 1, 2 * P:3 * P], y_tok, cc("ident")).then_inc(S("s_y_turned"), 1)

        def pe_update_s(eng, hp):
            k = dict(skip_group_check=True)
            if hp == 0:
                eng.wait_ge(*step("s_expanded", 4))
            if hp >= 2:
                eng.wait_ge(*step("s_state", hp - 1))
            rows = slice(hp * TS, (hp + 1) * TS)
            for pr in range(2):
                out = psum[par_rows(pr), 4 + hp % 2, :]
                b = slice(P + pr * HD, P + (pr + 1) * HD)
                kc = slice(2 * P + pr * HD, 2 * P + (pr + 1) * HD)
                eng.matmul(out, tokf[rows, b], own_x[rows, pr].rearrange("p b i -> p (b i)"),
                           start=True, stop=False, **k)
                mm = eng.matmul(out, tokf[rows, kc], own_v[rows, pr].rearrange("p b i -> p (b i)"),
                                start=False, stop=True, **k)
            mm.then_inc(S("s_update"), 1)

        def pe_heads(eng):
            def pair(bank, a):
                for h in range(2):
                    mm = eng.matmul(psum[:, bank + h, 0:HALF], cc("pair"), a[:, h * HALF:(h + 1) * HALF],
                                    start=True, stop=True)
                return mm
            def mean(f):
                if f >= 2:
                    eng.wait_ge(*step("y_log", f - 1))
                pair(2 * (f % 2), kk[:, f]).then_inc(S("y_mean"), 1)
                eng.wait_ge(*step("rk_made", f + 1))
                if f:
                    eng.wait_ge(S("bonus_made"), f)
                pair(6, t3[:, f]).then_inc(S("rk_summed"), 1)

            def variance(f):
                eng.wait_ge(S("y_squared"), f + 1)
                pair(2 * (f % 2), t1[:, f]).then_inc(S("y_var"), 1)

            eng.wait_ge(S("y_made"), NT + 2)
            mean(0)
            pe_update_s(eng, 0)
            mean(1)
            pe_update_s(eng, 1)
            for f in range(HP):
                variance(f)
                if f + 2 < HP:
                    mean(f + 2)
                    pe_update_s(eng, f + 2)

        def act_heads(eng):
            def square(f):
                eng.wait_ge(*step("y_centred", f + 1))
                eng.activation(t1[:, f], kk[:, f], ACT.Square).then_inc(S("y_squared"), 1)

            def high(f):
                eng.wait_ge(S("o_a_made"), f + 1)
                eng.wait_ge(S("soft_p_made"), 3)
                eng.activation(xh[:, f, 0:T], kk[:, f], ACT.Copy).then_inc(S("o_a_hi"), 1)

            def pad(h):
                r = par_rows(h)
                eng.activation(q_pad[h % 2][r], proj[r, 12 + h // 2, 0:SEQ], ACT.Copy).then_inc(S("q_padded"), 1)

            square(0)
            eng.wait_ge(S("q_padded"), 2)
            for h in range(2):
                pad(h)
            square(1)
            for f in range(HP):
                eng.wait_ge(S("y_var"), f + 1)
                eng.activation(halves(y_scale[:, f]), two_halves(2 * (f % 2)), ACT.Ln, bias=eps[:, 1:2], scale=1.0 / HD)\
                   .then_inc(S("y_log"), 1)
                eng.wait_ge(*step("y_log", f + 1))
                eng.activation(y_scale[:, f], y_scale[:, f], ACT.Exp, scale=-0.5).then_inc(S("y_rstd"), 1)
                if f + 2 < HP:
                    square(f + 2)
                if f:
                    high(f - 1)
            high(HP - 1)

        def dve_heads(eng):
            c = dve_steps

            eng.wait_ge(S("y_made"), NT + 2)

            def centre(f):
                eng.scalar_tensor_tensor(t3[:, f], proj[:, f, 0:T], vec("r_k", f), proj[:, 4 + f, 0:T],
                                         ALU.mult, ALU.mult).then_inc(S("rk_made"), 1)
                eng.wait_ge(*step("y_mean", f + 1))
                eng.scalar_tensor_tensor(halves(kk[:, f]), two_halves(2 * (f % 2)), -1.0 / HD, halves(kk[:, f]),
                                         ALU.mult, ALU.add).then_inc(S("y_centred"), 1)

            def bonus(f):
                eng.wait_ge(*step("rk_summed", f + 1))
                eng.tensor_tensor(halves(t3[:, f]), two_halves(6), halves(proj[:, 8 + f, 0:T]), ALU.mult)\
                   .then_inc(S("bonus_made"), 1)

            centre(0)
            bonus(0)
            centre(1)
            dve_state_s(eng, 0)
            for f in range(HP):
                if f + 1 < HP:
                    bonus(f + 1)
                if f + 2 < HP:
                    centre(f + 2)
                    dve_state_s(eng, f + 1)
                eng.wait_ge(*step("y_rstd", f + 1))
                eng.wait_ge(*step("y_centred", f + 1))
                eng.wait_ge(S("y_squared"), f + 1)
                if f == 2:
                    dve_state_s(eng, HP - 1)
                c.up(eng.scalar_tensor_tensor(kk[:, f], kk[:, f], vec("lnx_g", f), y_scale[:, f], ALU.mult, ALU.mult))
                c.wait(eng)
                eng.wait_ge(S("bonus_made"), f + 1)
                c.up(eng.scalar_tensor_tensor(kk[:, f], kk[:, f], vec("lnx_b", f), t3[:, f], ALU.add, ALU.add))
                c.wait(eng)
                eng.tensor_tensor(kk[:, f], kk[:, f], g_out[:, f], ALU.mult).then_inc(S("o_a_made"), 1)

        def pool_heads(eng):
            for f in range(HP):
                eng.wait_ge(S("o_a_hi"), f + 1)
                eng.tensor_tensor(xl[:, f, 0:T], kk[:, f], xh[:, f, 0:T].bitcast(F32), ALU.subtract)\
                   .then_inc(S("o_a_lo"), 1)

        OFF = {0: 4 * P, 2: 7 * P, 1: 8 * P}
        flat = psum[:].rearrange("p b n -> p (b n)")
        C_AT = 3 * 512

        def pe_scores(eng, h):
            if h:
                eng.wait_ge(S("z_made"), h)
            hp = h // 2
            eng.wait_ge(S("q_padded"), h + 3)
            q, key = q_pad[h % 2], proj[:, 16 + hp]
            for kt in range(NT):
                mm = eng.matmul(flat[:, kt * P:(kt + 1) * P], key[:, kt * P:(kt + 1) * P], q[:, kt * P:(kt + 1) * P],
                                start=kt == 0, stop=True, skip_group_check=True)
            for n, kt in enumerate((0, 2, 1)):
                w = SEQ - (kt + 1) * P
                mm = eng.matmul(flat[:, OFF[kt]:OFF[kt] + w], key[:, kt * P:(kt + 1) * P], q[:, (kt + 1) * P:SEQ],
                                start=kt != 2, stop=True, skip_group_check=True)
            mm.then_inc(S("z_done"), 1)

        def pe_sums(eng, h):
            low = l_lo[h % 2]
            if h:
                eng.wait_ge(S("exponents"), h)
            else:
                eng.wait_ge(S("ones_made"), 1)
            eng.wait_ge(S("soft_lo"), h + 1)
            eng.wait_ge(S("soft_lo_diag"), h + 1)
            def add(at, src, n, first=False):
                high = l_hi_diag[:, src:src + n] if src < 4 * P else l_hi_rest[:, src - 4 * P:src - 4 * P + n]
                for part in (high, low[:, src:src + n]):
                    mm = eng.matmul(flat[:, C_AT + at:C_AT + at + n], ones_suffix[:, P * first:P * first + P],
                                    part, start=first and part is high, stop=not first, skip_group_check=True)
                return mm
            add(0, 0, 512, True)
            add(4 * P, 4 * P, 512, True)
            add(8 * P, 8 * P, 256, True)
            add(4 * P, P, P)
            add(5 * P, 8 * P, 2 * P)
            add(5 * P, 2 * P, 2 * P)
            add(6 * P, 7 * P, P)
            add(7 * P, 3 * P, P)
            add(8 * P, 2 * P, 2 * P)
            add(9 * P, 7 * P, P).then_inc(S("sums_done"), 1)

        def pe_values(eng, h):
            a, hp = zs[h % 3], h // 2
            eng.wait_ge(S("weights_made"), h + 1)
            if h % 2 == 0 and hp:
                eng.wait_ge(S("o_b_read"), 2 * hp)
            out = psum[par_rows(h), 6, :]
            v = lambda kt: vt[:, kt, h * HD:(h + 1) * HD]
            for kt in range(NT):
                eng.matmul(out[:, kt * P:(kt + 1) * P], v(kt), a[:, kt * P:(kt + 1) * P],
                           start=kt == 0, stop=False, skip_group_check=True)
            for kt in range(NT - 1):
                w = SEQ - (kt + 1) * P
                mm = eng.matmul(out[:, (kt + 1) * P:SEQ], v(kt), a[:, OFF[kt]:OFF[kt] + w],
                                start=False, stop=kt == NT - 2, skip_group_check=True)
            mm.then_inc(S("values_done"), 1)

        def pe_stick(eng):
            eng.wait_ge(S("v_made"), 2)
            eng.wait_ge(*step("y_log", HP))
            pe_scores(eng, 0)
            eng.wait_ge(S("bonus_made"), HP)
            for h in range(NH + 1):
                if h + 1 < NH:
                    pe_scores(eng, h + 1)
                pe_samples(eng, h, "a")
                if h < NH:
                    pe_sums(eng, h)
                pe_samples(eng, h, "b")
                if h:
                    pe_values(eng, h - 1)
                pe_samples(eng, h, "c")

        def act_stick(eng):
            def soft(h):
                l = ls[h % 2]
                eng.wait_ge(S("z_made"), h + 1)
                if h >= 2:
                    eng.wait_ge(S("sums_done"), h - 1)
                eng.activation(l[:], zs[h % 3][:], ACT.Abs).then_inc(S("soft"), 1)
                eng.wait_ge(S("soft"), 3 * h + 1)
                eng.activation(l[:], l[:], ACT.Exp, scale=-1.0).then_inc(S("soft"), 1)
                eng.wait_ge(S("soft"), 3 * h + 2)
                eng.activation(l[:], l[:], ACT.Ln, bias=1.0).then_inc(S("soft"), 1)

            def weights(h):
                eng.wait_ge(S("exponents_masked"), h + 1)
                eng.activation(zs[h % 3][:], zs[h % 3][:], ACT.Exp).then_inc(S("weights_made"), 1)

            def output(hp):
                eng.wait_ge(S("values_done"), 2 * hp + 2)
                if hp >= 2:
                    eng.wait_ge(S("o_b_lo"), hp - 1)
                eng.activation(ob[hp % 2][:], psum[:, 6, :], ACT.Copy).then_inc(S("o_b_read"), 1)
                eng.activation(xh[:, HP + hp, 0:SEQ], psum[:, 6, :], ACT.Copy).then_inc(S("o_b_read"), 1)

            act_samples(eng, io, -1)
            eng.wait_ge(S("z_made"), 1)
            at = CST["ones"]
            eng.activation(ones_suffix[:], cst[:, at:at + 2 * P], ACT.Copy).then_inc(S("ones_made"), 1)
            soft(0)
            for h in range(NH):
                act_samples(eng, io, h, "start")
                if h + 1 < NH:
                    soft(h + 1)
                act_samples(eng, io, h, "mid")
                weights(h)
                if h >= 2 and h % 2 == 0:
                    output(h // 2 - 1)
            eng.wait_ge(S("pages_used2"), NB // 2 + 1)
            make_hi(eng, 0, stages["merge"].m0, MERGE_COLS)
            act_samples(eng, io, NH - 1, "end")
            output(HP - 1)

        def dve_stick(eng):
            def scaled(h):
                eng.wait_ge(S("z_done"), h + 1)
                if h >= 3:
                    eng.wait_ge(S("values_done"), h - 2)
                eng.tensor_scalar(zs[h % 3][:], flat[:, 0:10 * P], SCALE, vec("sb_bias", h), ALU.mult, ALU.add)\
                   .then_inc(S("z_made"), 1)

            def soft(h):
                eng.wait_ge(S("soft"), 3 * h + 3)
                eng.scalar_tensor_tensor(ls[h % 2][:], zs[h % 3][:], 0.0, ls[h % 2][:], ALU.max, ALU.add)\
                   .then_inc(S("soft_made"), 1)

            def high(h, rest):
                if h:
                    eng.wait_ge(S("sums_done"), h)
                if rest:
                    eng.wait_ge(S("soft_made"), h + 1)
                    eng.tensor_copy(l_hi_rest[:], ls[h % 2][:, 4 * P:10 * P]).then_inc(S("soft_hi"), 1)
                else:
                    eng.wait_ge(S("soft_masked"), h + 1)
                    eng.tensor_copy(l_hi_diag[:], ls[h % 2][:, 0:4 * P]).then_inc(S("soft_hi"), 1)

            def low_diag(h):
                eng.wait_ge(S("soft_hi"), 2 * h + 2)
                eng.tensor_tensor(l_lo[h % 2][:, 0:4 * P], ls[h % 2][:, 0:4 * P], l_hi_diag[:].bitcast(F32),
                                  ALU.subtract).then_inc(S("soft_lo_diag"), 1)

            def exponents(h):
                eng.wait_ge(S("sums_done"), h + 1)
                eng.tensor_tensor(zs[h % 3][:], zs[h % 3][:], flat[:, C_AT:C_AT + 10 * P], ALU.subtract)\
                   .then_inc(S("exponents"), 1)

            dve_samples(eng, -1)
            scaled(0)
            soft(0)
            high(0, True)
            high(0, False)
            low_diag(0)
            for h in range(NH):
                dve_samples(eng, h, "start")
                if h + 1 < NH:
                    scaled(h + 1)
                if h + 2 < NH:
                    eng.wait_ge(S("z_done"), h + 1)
                    r = par_rows(h)
                    eng.tensor_copy(q_pad[h % 2][r], proj[r, 12 + h // 2 + 1, 0:SEQ]).then_inc(S("q_padded"), 1)
                dve_samples(eng, h, "mid")
                exponents(h)
                if h + 1 < NH:
                    soft(h + 1)
                    high(h + 1, True)
                    high(h + 1, False)
                    low_diag(h + 1)
                dve_samples(eng, h, "end")
            eng.wait_ge(S("o_b_read"), 2 * HP)
            eng.tensor_tensor(xl[:, 2 * HP - 1, 0:SEQ], ob[(HP - 1) % 2][:], xh[:, 2 * HP - 1, 0:SEQ].bitcast(F32),
                              ALU.subtract).then_inc(S("o_b_lo"), 1)

        def pool_stick(eng):
            def select(a, fill):
                b = a[:, 0:4 * P].rearrange("p (k n) -> p k n", k=4)
                return eng.affine_select(out=b, in_=b, compare_op=ALU.is_gt, fill=fill, base=0,
                                         pattern=[[0, 4], [1, P]], channel_multiplier=-1)
            def soft(h):
                eng.wait_ge(S("soft_made"), h + 1)
                select(ls[h % 2], 0.0).then_inc(S("soft_masked"), 1)
            def soft_low(h):
                eng.wait_ge(S("soft_hi"), 2 * h + 1)
                rest = slice(4 * P, 10 * P)
                eng.tensor_tensor(l_lo[h % 2][:, rest], ls[h % 2][:, rest], l_hi_rest[:].bitcast(F32), ALU.subtract)\
                   .then_inc(S("soft_lo"), 1)
            def low(hp):
                eng.wait_ge(S("o_b_read"), 2 * hp + 2)
                eng.tensor_tensor(xl[:, HP + hp, 0:SEQ], ob[hp % 2][:], xh[:, HP + hp, 0:SEQ].bitcast(F32),
                                  ALU.subtract).then_inc(S("o_b_lo"), 1)

            def h_low(q):
                eng.wait_ge(S("hh_made"), q + 1)
                two = slice(2 * q, 2 * q + 2)
                eng.tensor_tensor(hl[:, two], y[:, two], hh[:, two].bitcast(F32), ALU.subtract).then_inc(S("hl_made"), 1)

            soft(0)
            soft_low(0)
            for h in range(NH):
                eng.wait_ge(S("exponents"), h + 1)
                select(zs[h % 3], MASKED).then_inc(S("exponents_masked"), 1)
                if h + 1 < NH:
                    soft(h + 1)
                    soft_low(h + 1)
                if h >= 3 and h % 2 == 1:
                    low(h // 2 - 1)
                if 3 <= h < 7:
                    h_low(h - 3)

        def page_registers(eng, places):
            return [eng.value_load(page_of[:, bass.ds(at, 1)], min_val=0, max_val=N_PHYS - 1) for at in places]

        def sp_k_pages(eng, io):
            eng.wait_ge(S("page_table_loaded"), 16)
            wait_w_in(eng)
            with eng.Fori(0, NT) as i:
                for n in range(4):
                    regs = page_registers(eng, [i * -2 + ((2 * n + b) * N_PAGES + N_PAGES - 1 - p)
                                                for b in range(2) for p in range(2)])
                    for q, reg in enumerate(regs):
                        if q == 0:
                            eng.wait_ge(S(f"k_pages_used{n % 2}"), i * 2 + (n // 2 + 1))
                        eng.dma_start(k_pages[n % 2][:, q // 2, :, q % 2 * PAGE:(q % 2 + 1) * PAGE],
                                      io["cache_k"][bass.ds(reg, 1)].rearrange("a p h n -> (a p) h n"))\
                           .then_inc(S(f"k_pages_loaded{n % 2}"), 16)

        def sp_v_pages(eng, io):
            eng.wait_ge(S("o_a_lo"), HP)
            with eng.Fori(0, NB // 2) as i:
                for j in range(4):
                    regs = page_registers(eng, [i * (2 * N_PAGES) + (j // 2 * N_PAGES + N_PAGES - 1 - (j % 2 * 4 + p))
                                                for p in range(4)])
                    for p, reg in enumerate(regs):
                        if p == 0:
                            eng.wait_ge(S(f"pages_used{j}"), i + 1)
                        eng.dma_start(pages[j][:, p], io["cache_v"][bass.ds(reg, 1)].rearrange("a p n -> (a p) n"))\
                           .then_inc(S(f"pages_loaded{j}"), 16)

        def dve_qb(eng):
            for s in range(2):
                eng.wait_ge(S(f"qk_made{s}"), 3)
            for q in (qb_even, qb_odd):
                eng.memset(q[:], 0.0).then_inc(S("qb_made"), 1)
            eng.wait_ge(S("qb_made"), 2)
            for h in range(NH):
                r = par_rows(h)
                eng.tensor_copy(qb[h // 2][r, :, h], samples(proj[r, 12 + h // 2, s_cols])).then_inc(S("qb_made"), 1)

        SAMPLE_STEPS = {(0, "a"): ("turn", 0, 0), (0, "b"): ("turn", 0, 1), (0, "c"): ("turn", 1, 0),
                        (1, "a"): ("turn", 1, 1), (1, "c"): ("turn_self",),
                        (2, "a"): ("values", 0), (2, "c"): ("values", 1), (3, "b"): ("values", 2),
                        (4, "a"): ("values", 3), (4, "b"): ("pick", 0),
                        (5, "a"): ("values", 4), (5, "c"): ("values", 5), (6, "b"): ("values", 6),
                        (7, "b"): ("values", 7), (8, "a"): ("pick", 1)}

        def pe_samples(eng, h, place):
            k = dict(skip_group_check=True)
            kind, *at = SAMPLE_STEPS.get((h, place), (None,))
            if kind == "turn":
                g, q = at
                eng.wait_ge(S("wp_made"), 1)
                if g or q:
                    eng.wait_ge(S("wp_turned"), 2 * g + q)
                for p in range(4):
                    mm = eng.transpose(psum[:, 7, p * P:(p + 1) * P],
                                       zp[:, g, DS + (4 * q + p) * P:DS + (4 * q + p + 1) * P], cc("ident"))
                mm.then_inc(S("wp_turn"), 1)
            elif kind == "turn_self":
                eng.wait_ge(S("self_spread"), 8)
                eng.wait_ge(S("wp_turned"), 4)
                for g in range(2):
                    mm = eng.transpose(psum[0:TS, 7, g * P:(g + 1) * P], own_self[:, g].rearrange("p b t -> p (b t)"),
                                       cc("ident"))
                mm.then_inc(S("self_turn"), 1)
            elif kind == "values":
                b, = at
                g, rows = b // 4, slice(b % 4 * 32, b % 4 * 32 + 32)
                if b % 4 == 0:
                    eng.wait_ge(S("self_turned"), 1)
                    if g:
                        eng.wait_ge(S("o_s_lo"), 1)
                    eng.matmul(psum[:, 7, :], a_self_t[:, g], vt[0:TS, NT, :], start=True, stop=False, **k)
                for half in range(2):
                    j = 2 * (b % 2) + half
                    eng.wait_ge(S(f"pages_loaded{j}"), 64 * (b // 2 + 1))
                    for p in range(4):
                        mm = eng.matmul(psum[rows, 7, :], a_t[:, g, 4 * half + p, rows], pages[j][:, p],
                                        start=False, stop=True, **k)
                    mm.then_inc(S(f"pages_used{j}"), 1)
            elif kind == "pick":
                g, = at
                eng.wait_ge(S("zsum_made"), g + 1)
                for hp in range(HP):
                    mm = eng.matmul(psum[:, 7, hp * 16:(hp + 1) * 16], zsum[:, hp * P:(hp + 1) * P], cc("pick", 16),
                                    start=hp == 0, stop=True, **k)
                mm.then_inc(S("o_s_done"), 1)

        def act_samples(eng, io, h, place=None):
            def turned(g, q):
                eng.wait_ge(S("wp_turn"), 2 * g + q + 1)
                eng.activation(a_t[:, g, 4 * q:4 * q + 4].rearrange("p a n -> p (a n)"), psum[:, 7, :], ACT.Copy)\
                   .then_inc(S("wp_turned"), 1)

            def self_turned():
                eng.wait_ge(S("self_turn"), 1)
                eng.activation(a_self_t[:].rearrange("p g n -> p (g n)"), psum[0:TS, 7, 0:2 * P], ACT.Copy)\
                   .then_inc(S("self_turned"), 1)

            def output(g):
                eng.wait_ge(S("o_s_done"), g + 1)
                eng.activation(xh[:, HP:2 * HP, SEQ + 16 * g:SEQ + 16 * g + 16],
                               psum[:, 7, 0:64].rearrange("p (h n) -> p h n", h=HP), ACT.Copy).then_inc(S("o_s_hi"), 1)

            def h_high(q):
                if q == 0:
                    eng.wait_ge(S("h_back"), 16)
                two = slice(2 * q, 2 * q + 2)
                eng.activation(hh[:, two], y[:, two], ACT.Copy).then_inc(S("hh_made"), 1)

            if h == -1:
                eng.wait_ge(S("exponents_p"), 1)
                eng.activation(zp[:], zp[:], ACT.Exp).then_inc(S("wp_made"), 1)
            elif (h, place) == (0, "start"):
                turned(0, 0)
            elif (h, place) == (0, "mid"):
                turned(0, 1)
                eng.wait_ge(S("states_stored"), 32)
                eng.wait_ge(S("o_a_made"), HP)
                eng.dma_start(y[:], io["h"]).then_inc(S("h_back"), 16)
            elif (h, place) == (1, "start"):
                turned(1, 0)
            elif (h, place) == (1, "mid"):
                turned(1, 1)
            elif (h, place) == (2, "start"):
                self_turned()
            elif (h, place) == (4, "mid"):
                output(0)
            elif (h, place) == (7, "end"):
                output(1)
            if place == "mid" and 2 <= h < 6:
                h_high(h - 2)

        def dve_samples(eng, h, place=None):
            def zsums(g):
                for half in range(2):
                    eng.wait_ge(S(f"pages_used{2 + half}"), 1 + 2 * g + 2)
                eng.tensor_tensor(zsum[:].rearrange("p (h n) -> p h n", h=NH),
                                  psum[:, 7, :].rearrange("p (h n) -> p h n", h=NH), each(cc("own_head", NH), HD),
                                  ALU.mult).then_inc(S("zsum_made"), 1)

            def output(g):
                eng.wait_ge(S("o_s_hi"), g + 1)
                cols = slice(SEQ + 16 * g, SEQ + 16 * g + 16)
                eng.tensor_tensor(xl[:, HP:2 * HP, cols], psum[:, 7, 0:64].rearrange("p (h n) -> p h n", h=HP),
                                  xh[:, HP:2 * HP, cols].bitcast(F32), ALU.subtract).then_inc(S("o_s_lo"), 1)

            if h == -1:
                eng.wait_ge(S("soft_p_made"), 3)
                eng.tensor_tensor(zp[:, :, 0:DS], zp[:, :, 0:DS], bcast(cc("cap", DS), 2), ALU.min)\
                   .then_inc(S("exponents_p"), 1)
            elif (h, place) == (0, "start"):
                eng.wait_ge(S("wp_made"), 1)
                for g in range(2):
                    own = cc("own_rows", NB, g * NB)
                    for t in range(DS):
                        eng.tensor_scalar(own_self[:, g, :, t], own, zp[:, g, DS - 1 - t:DS - t], None, ALU.mult)\
                           .then_inc(S("self_spread"), 1)
            elif (h, place) == (4, "mid"):
                zsums(0)
            elif (h, place) == (5, "start"):
                output(0)
            elif (h, place) == (7, "end"):
                zsums(1)
                output(1)

        b_r = Region(big_at, 20 * TX * 4)
        mh = b_r.tensor("mh", [P, KT, T], F32R)
        ml = b_r.tensor("ml", [P, KT, T], F32R)

        def pe_merge(eng, st):
            eng.wait_ge(S("o_s_lo"), 2)
            eng.wait_ge(S("hl_made"), 4)
            with eng.Fori(0, KT) as i:
                for s in range(2):
                    unit_ready(eng, s, i + st.m0)
                    if s:
                        eng.wait_ge(S("o_b_lo"), HP)
                    eng.wait_ge(S("gates_made"), i * 2 + (s + 1))
                    eng.wait_ge(S("gated"), i * 2 + (s + 1))
                    for k in range(KT + HP):
                        w = slice(k * P, (k + 1) * P)
                        if k < KT:
                            bank, a_hi, a_lo = 4 * s, hh[:, k], hl[:, k]
                        else:
                            f = s * HP + k - KT
                            bank, a_hi, a_lo = 4 * s + 2, xh[:, f, 0:T], xl[:, f, 0:T]
                        mm = split_product(eng, bank, whi[s][:, w], wlo[s][:, w], a_hi, a_lo, HALF,
                                           k in (0, KT), k in (KT - 1, KT + HP - 1))
                    mm.then_inc(used[s], 1)

        def act_merge(eng, st, next_cols):
            def work(i, s):
                eng.wait_ge(used[s], i + (st.m0 + 2))
                eng.wait_ge(S("gated"), i * 2 + (s + 1))
                eng.activation(halves(sg[s][:]), two_halves(4 * s), ACT.Sigmoid).then_inc(S("gates_made"), 1)
            eng.preload_act_table(ACT.Sigmoid)
            pipelined(eng, st, work, next_cols)

        def dve_merge(eng, st):
            with eng.Fori(0, KT) as i:
                one = lambda a: a[:, bass.ds(i, 1)].rearrange("p a n -> p (a n)")
                eng.wait_ge(S("merged"), i * 3 + 1)
                for s in range(2):
                    eng.wait_ge(used[s], i + (st.m0 + 2))
                    eng.wait_ge(S("gates_made"), i * 2 + (s + 3))
                    eng.tensor_tensor(halves(u[s][:]), two_halves(4 * s + 2), halves(sg[s][:]), ALU.mult)\
                       .then_inc(S("gated"), 1)
                eng.wait_ge(S("gated"), i * 2 + 4)
                eng.tensor_tensor(u[0][:], u[0][:], u[1][:], ALU.add).then_inc(S("merged"), 1)
                eng.wait_ge(S("merged"), i * 3 + 2)
                eng.tensor_copy(one(mh), u[0][:]).then_inc(S("merged"), 1)
                eng.wait_ge(S("merged"), i * 3 + 3)
                eng.tensor_tensor(one(ml), u[0][:], one(mh).bitcast(F32), ALU.subtract).then_inc(S("merged"), 1)

        def pe_out(eng, st):
            eng.wait_ge(S("merged"), 3 * KT + 1)
            with eng.Fori(0, st.n // 2) as i:
                for s in range(2):
                    unit_ready(eng, s, i + st.m0)
                    eng.wait_ge(S(f"mixed_in{s}"), i * 2 + 1)
                    for t in range(2):
                        for k in range(KT):
                            w = slice((t * KT + k) * P, (t * KT + k + 1) * P)
                            mm = split_product(eng, 4 * s + 2 * t, whi[s][:, w], wlo[s][:, w], mh[:, k], ml[:, k],
                                               HALF, k == 0, k == KT - 1)
                    mm.then_inc(used[s], 1)

        def dve_out(eng, st):
            eng.wait_ge(S("merged"), 3 * KT + 1)
            eng.memset(total[:], 0.0).then_inc(S("totalled"), 1)
            eng.wait_ge(S("h_back"), 16)
            with eng.Fori(0, st.n // 2) as i:
                for s in range(2):
                    eng.wait_ge(used[s], i + (st.m0 + 2))
                    for t in range(2):
                        row = y[:, bass.ds(i * 4 + (2 * s + t), 1)].rearrange("p a (h n) -> p (a h) n", h=2)
                        eng.scalar_tensor_tensor(row, two_halves(4 * s + 2 * t), 1.0 / ALPHA, row, ALU.mult, ALU.add)\
                           .then_inc(S(f"mixed_in{s}"), 1)
                        eng.wait_ge(S(f"mixed_in{s}"), i * 2 + (t + 2))
                        eng.wait_ge(S("totalled"), i * 4 + (KT + 1 + 2 * s + t + 1))
                        eng.tensor_tensor(halves(total[:]), halves(total[:]), row, ALU.add).then_inc(S("totalled"), 1)

        block = ctx.enter_context(nc.Block())

        @block.sync
        def _(sp):
            sp_stage(sp, stages["ffn1_in"], io["ffn1_w_in"])
            sp_stage(sp, stages["ffn1_out"], io["ffn1_w_out"])
            sp_stage(sp, stages["rkv"], io["w_rkv"])
            for q in range(6):
                s, m = mid_unit(q)
                src, cols = ((io["lora_wa"], KT * P), (io["lora_g"][0], KT * GL), (io["lora_g"][1], KT * GL),
                             (io["w_v"][:, 0:1536], 1536), (io["w_v"][:, 1536:3072], 1536),
                             (io["w_v"][:, 3072:4096], 1024))[q]
                load_unit(sp, s, m, src, cols)
                if q == 0:
                    sp.wait_ge(S("normed"), KT)
                    sp.dma_start(io["h"], y[:]).then_inc(S("h_stored"), 16)
                if q == 1:
                    sp.dma_start(inner2[0:HD], io["w_w2"]).then_inc(S("inner2_loaded"), 16)
                    sp.dma_start(inner2[HD:P], io["a_w2"]).then_inc(S("inner2_loaded"), 16)
                    sp.dma_start(inner2g[:], io["g_w2"]).then_inc(S("inner2_loaded"), 16)
            sp.wait_ge(S("k_scaled"), HP)
            sp.dma_start(cst[:], io["constants"][:, 0:NCST - N_MASKS]).then_inc(S("cst_loaded"), 16)
            sp_stage(sp, stages["qk"], io["w_qk"])
            wait_w_in(sp)
            sp.dma_start(masks[:], io["constants"][:, NCST - N_MASKS:NCST]).then_inc(S("masks_loaded"), 16)
            for s in range(2):
                sp.wait_ge(S(f"qk_made{s}"), 3)
            sp.dma_start(io["k_rows"], proj[:, 16:20, 0:T]).then_inc(S("out_stored"), 16)
            sp.dma_start(io["v_rows"][0:SEQ].rearrange("(t p) n -> p t n", p=P), vt[:, 0:NT]).then_inc(S("out_stored"), 16)
            sp.dma_start(io["v_rows"][SEQ:T], vt[0:TS, NT]).then_inc(S("out_stored"), 16)
            sp_k_pages(sp, io)
            sp.wait_ge(S("y_made"), NT + 1)
            sp.dma_start(state_s[:], io["state_s"]).then_inc(S("state_loaded"), 16)
            sp.wait_ge(S("state_made"), last)
            sp.dma_start(io["wkv_p"], state[:]).then_inc(S("states_stored"), 16)
            sp.wait_ge(*step("s_state_final", HP))
            sp.dma_start(io["wkv_s"], state_s[:]).then_inc(S("states_stored"), 16)
            sp.wait_ge(S("states_stored"), 32)
            sp_v_pages(sp, io)
            for j in range(2):
                sp.wait_ge(S(f"pages_used{j}"), NB // 2 + 1)
            sp.wait_ge(S("out_stored"), 16 * 3)
            sp_stage(sp, stages["merge"], io["w_merge"])
            sp_stage(sp, stages["out"], io["w_out"])
            sp_stage(sp, stages["ffn2_in"], io["ffn2_w_in"])
            sp_stage(sp, stages["ffn2_out"], io["ffn2_w_out"])
            for k in range(KT):
                sp.wait_ge(S("normed"), 2 * KT + k + 1)
                sp.dma_start(io["y"][:, k], y[:, k]).then_inc(S("y_stored"), 16)
            sp.wait_ge(S("y_stored"), 16 * KT)
            sp.wait_ge(S("states_stored"), 32)

        @block.gpsimd
        def _(pool):
            for s in range(2):
                pool.sem_inc(lo_made[s], 1)
            for name in ("ffn1_in", "ffn1_out", "rkv"):
                pool_stage(pool, stages[name])
            for q in range(6):
                make_lo(pool, *mid_unit(q), MID_COLS[q])
            pool_stage(pool, stages["qk"])
            pool_wkv(pool)
            pool_wkv_s(pool)
            pool_heads(pool)
            pool_stick(pool)
            pool.wait_ge(S("o_s_done"), 2)
            for name in ("merge", "out", "ffn2_in", "ffn2_out"):
                pool_stage(pool, stages[name])

        @block.scalar
        def _(act):
            for s in range(2):
                act.sem_inc(hi_made[s], 1)
                act.sem_inc(S(f"rkv_made{s}"), 1)
                act.sem_inc(S(f"qk_made{s}"), 1)
            act.sem_inc(S("y_made"), 1)
            for q in range(4):
                act.dma_start(y[:, 2 * q:2 * q + 2], io["x"][:, 2 * q:2 * q + 2]).then_inc(S(f"x_loaded{q}"), 16)
            act.dma_start(vecs[:], io["vecs"]).then_inc(S("vecs_loaded"), 16)
            act.dma_start(before[:], io["before"]).then_inc(S("vecs_loaded"), 16)
            act.dma_start(page_of[:], io["page_table"]).then_inc(S("page_table_loaded"), 16)
            make_hi(act, 0, 0, 2048)
            act_ffn_in(act, stages["ffn1_in"], 0, stages["ffn1_out"].cols)
            act_ffn_out(act, stages["ffn1_out"], stages["rkv"].cols)
            act.wait_ge(S("set_up"), 3)
            act.wait_ge(S("vecs_loaded"), 32)
            act_norm(act, 0, "ln1_g", "ln1_b", True)
            act_pairs(act, stages["rkv"], "rkv_made", 0, ACT.Copy, MID_COLS[0], (S("lora_weights"), 1))
            act_mid(act)
            act_prep(act)
            act_pairs(act, stages["qk"], "qk_made", 12, ACT.Copy, 0)
            act_wkv(act)
            act_wkv_s(act)
            act_heads(act)
            act_stick(act)
            act.sem_inc(S("gates_made"), 2)
            act_merge(act, stages["merge"], stages["out"].cols)
            pipelined(act, stages["out"], lambda i, s: None, stages["ffn2_in"].cols)
            act_norm(act, 1, "ln2_g", "ln2_b", True)
            act_ffn_in(act, stages["ffn2_in"], 1, stages["ffn2_out"].cols)
            act_ffn_out(act, stages["ffn2_out"], 0)
            act_norm(act, 2, "ln3_g", "ln3_b", False)

        @block.tensor
        def _(pe):
            for s in range(2):
                pe.sem_inc(used[s], 1)
                pe.sem_inc(S(f"k_pages_used{s}"), 1)
            pe.sem_inc(S("y_done"), 1)
            for s in range(2):
                for j in (s, 2 + s):
                    pe.sem_inc(S(f"pages_used{j}"), 1)
            pe_ffn_in(pe, stages["ffn1_in"], 0, lambda k: (S("x_split"), 2 * (k + 1)))
            pe_ffn_out(pe, stages["ffn1_out"], 0)
            pe.wait_ge(S("set_up"), 3)
            pe_norm(pe, 0)
            pe.wait_ge(S("x_split"), 2 * (KT + 1))
            pe_pairs(pe, stages["rkv"], "rkv_made", lambda k: (S("norm_lo"), k + 1))
            pe_mid(pe)
            pe_prep(pe)
            pe_pairs(pe, stages["qk"], "qk_made")
            pe_wkv(pe)
            pe_wkv_s(pe)
            pe_heads(pe)
            pe_stick(pe)
            pe_merge(pe, stages["merge"])
            pe_out(pe, stages["out"])
            pe_norm(pe, 1)
            pe_ffn_in(pe, stages["ffn2_in"], 1, lambda k: (S("norm_lo"), KT + k + 1))
            pe_ffn_out(pe, stages["ffn2_out"], 1)
            pe_norm(pe, 2)

        @block.vector
        def _(dve):
            for s in range(2):
                for name in ("ffn_read", "inner_split", "mixed_in"):
                    dve.sem_inc(S(f"{name}{s}"), 1)
            dve.sem_inc(S("gated"), 2)
            dve.sem_inc(S("merged"), 1)
            dve.sem_inc(S("y_added"), 2)
            dve.sem_inc(S("state_made"), 1)
            for a, value in ((mean_w[:], 1.0 / D_MODEL), (eps[:, 0:1], LN_EPS / ALPHA ** 2), (eps[:, 1:2], LNX_EPS)):
                dve.memset(a, value).then_inc(S("set_up"), 1)
            for k in range(KT + 1):
                if k < KT:
                    dve.wait_ge(S(f"x_loaded{k // 2}"), 16)
                    src, hi, lo = y[:, k], xh[:, k, 0:T], xl[:, k, 0:T]
                else:
                    dve.wait_ge(S("vecs_loaded"), 32)
                    src, hi, lo = before[:], xh[:, :, T:TX], xl[:, :, T:TX]
                dve.tensor_copy(hi, src).then_inc(S("x_split"), 1)
                dve.wait_ge(S("x_split"), 2 * k + 1)
                dve.tensor_tensor(lo, src, hi.bitcast(F32), ALU.subtract).then_inc(S("x_split"), 1)
            dve_ffn_in(dve, stages["ffn1_in"], 0)
            dve_ffn_out(dve, stages["ffn1_out"], 0)
            dve_norm(dve, 0, "ln1_g", True)
            dve_lora_weights(dve)
            dve_shift(dve).wait(dve)
            dve_keys(dve)
            dve_lora_sum(dve)
            dve_prep(dve)
            dve_qb(dve)
            dve_wkv(dve)
            dve_wkv_s(dve)
            dve_heads(dve)
            dve_stick(dve)
            dve_merge(dve, stages["merge"])
            dve_out(dve, stages["out"])
            dve_norm(dve, 1, "ln2_g", True)
            dve_ffn_in(dve, stages["ffn2_in"], 1)
            dve_ffn_out(dve, stages["ffn2_out"], 1)
            dve_norm(dve, 2, "ln3_g", False)


def tiles_of(w, k, n):
    return w.reshape(k, P, -1, n).transpose(2, 1, 0, 3)


def kernel(x_prompt, x_sample, cache_k, cache_v, state_wkv, state_shift, page_table,
           ln1_g, ln1_b, ffn1_w_in, ffn1_w_out, w_in, mu_rkv, mu_wag, w0, w_w1, w_w2,
           a0, a_w1, a_w2, g_w1, g_w2, k_k, k_a, r_k, lnx_g, lnx_b, sb_bias, w_branch, w_out,
           ln2_g, ln2_b, ffn2_w_in, ffn2_w_out, ln3_g, ln3_b):
    import concourse.bacc as bacc
    from concourse.bass_utils import run_bass_kernel_spmd

    a = {k: np.asarray(v) for k, v in locals().items() if k not in ("bacc", "run_bass_kernel_spmd")}
    cols = lambda v: v.reshape(-1, P).T
    by_feature = lambda t: t.reshape(-1, KT, P).transpose(2, 1, 0)
    tokens = np.concatenate([a["x_prompt"].reshape(SEQ, D_MODEL), a["x_sample"].reshape(TS, D_MODEL)])
    vecs = {"mu_w": a["mu_wag"][0, 0], "mu_a": a["mu_wag"][0, 1], "mu_g": a["mu_wag"][0, 2]}
    packed = [cols(vecs[n] if n in vecs else a[n].reshape(-1)) for n in VEC if not n.startswith("sb_bias")]
    bias = a["sb_bias"].reshape(NH)
    packed += [np.tile(bias[None], (P, 1)), np.tile(np.repeat(bias, DS), 4)[:, None]]

    def ffn_in(w):
        t = tiles_of(w[0], KT, P)
        return np.stack([t[:FT], t[FT:]], 2).reshape(FT, P, UNIT)

    def ffn_out(w):
        t = tiles_of(w[0], FT, P)
        return t.reshape(KT, P, 2, FH * P).transpose(0, 2, 1, 3).reshape(2 * KT, P, FH * P)

    def pairs(w):
        t = tiles_of(w, KT, P)
        return t.reshape(-1, 2, P, KT * P).transpose(0, 2, 1, 3).reshape(-1, P, UNIT)

    wi = a["w_in"][0]
    n3 = 3 * 512
    rows = lambda c: c[0].reshape(N_PHYS, PAGE, NH * HD)[:, ::-1]
    ins = {
        "vecs": np.concatenate(packed, 1), "before": by_feature(a["state_shift"][0]), "x": by_feature(tokens),
        "constants": constants(),
        "ffn1_w_in": ffn_in(a["ffn1_w_in"]), "ffn1_w_out": ffn_out(a["ffn1_w_out"]),
        "ffn2_w_in": ffn_in(a["ffn2_w_in"]), "ffn2_w_out": ffn_out(a["ffn2_w_out"]),
        "w_rkv": pairs(wi[:, :n3]),
        "lora_wa": tiles_of(np.concatenate([a["w_w1"][0], a["a_w1"][0]], 1), KT, P).reshape(P, KT * P),
        "lora_g": tiles_of(a["g_w1"][0], KT, GL).reshape(2, P, KT * GL),
        "w_v": wi[:, n3 + 1024:n3 + n3].reshape(KT, P, 512).transpose(1, 0, 2).reshape(P, KT * 512),
        "w_qk": pairs(wi[:, n3:n3 + 1024]),
        "w_merge": np.concatenate([
            tiles_of(wi[:, 2 * n3:], KT, P).reshape(2, KT, P, KT * P),
            tiles_of(a["w_branch"][0], KT, P).reshape(KT, P, 2, HP * P).transpose(2, 0, 1, 3)], 3)
            .transpose(1, 0, 2, 3).reshape(2 * KT, P, (KT + HP) * P),
        "w_w2": a["w_w2"][0], "a_w2": a["a_w2"][0],
        "g_w2": a["g_w2"][0].reshape(2, GL, 512).transpose(1, 0, 2),
        "w_out": pairs(a["w_out"][0]),
        "state_s": a["state_wkv"][0].reshape(NB, HP, 2, HD, HD).transpose(2, 4, 1, 0, 3).reshape(P, HP, NB, HD),
        "cache_k": rows(a["cache_k"]).reshape(N_PHYS, PAGE, HP, P).transpose(0, 3, 2, 1),
        "cache_v": rows(a["cache_v"]), "page_table": a["page_table"].reshape(1, -1),
    }
    outs = {"y": [P, KT, T], "h": [P, KT, T], "k_rows": [P, HP, T], "v_rows": [T, 512],
            "wkv_p": [P, HP, P], "wkv_s": [P, HP, NB, HD]}

    nc = bacc.Bacc("TRN2", target_bir_lowering=False, num_devices=1)
    io, arrays = {}, {}
    for n, v in ins.items():
        v = np.ascontiguousarray(v)
        arrays["in_" + n] = v
        io[n] = nc.dram_tensor("in_" + n, list(v.shape), mybir.dt.from_np(v.dtype), kind="ExternalInput").ap()
    for n, shape in outs.items():
        io[n] = nc.dram_tensor("out_" + n, shape, F32, kind="ExternalOutput").ap()
    build(nc, io)
    got = run_bass_kernel_spmd(nc, [arrays], core_ids=[0]).results[0]

    y = got["out_y"].transpose(2, 1, 0).reshape(T, D_MODEL)
    k = got["out_k_rows"].transpose(2, 1, 0).reshape(T, NH, HD)
    v = got["out_v_rows"].reshape(T, NH, HD)
    shift = got["out_h"][:, :, SEQ - 1:][:, :, ::DS].transpose(2, 1, 0).reshape(1 + NB, D_MODEL)
    wp = got["out_wkv_p"].reshape(2, HD, HP, 2, HD)
    wp = np.stack([wp[0, :, :, 0], wp[1, :, :, 1]]).transpose(2, 0, 3, 1).reshape(1, 1, NH, HD, HD)
    ws = got["out_wkv_s"].reshape(2, HD, HP, NB, HD).transpose(3, 2, 0, 4, 1).reshape(1, NB, NH, HD, HD)
    return (y[:SEQ].reshape(1, SEQ, D_MODEL), y[SEQ:].reshape(NB, DS, D_MODEL),
            k[:SEQ].reshape(1, 1, SEQ, NH, HD), v[:SEQ].reshape(1, 1, SEQ, NH, HD), wp,
            shift[:1].reshape(1, 1, D_MODEL),
            k[SEQ:].reshape(1, NB, DS, NH, HD), v[SEQ:].reshape(1, NB, DS, NH, HD), ws,
            shift[1:].reshape(1, NB, D_MODEL))
```
